# Optimizing a Trainium2 kernel written in Bass

```python
import jax, jax.numpy as jnp
from jax import lax
import numpy as np
import math

D_MODEL = 1024
BATCH = 1
SEQ = 512
DEPTH = 1

GRID_W = 64
CTX_LEN = 256
D_MIX = D_MODEL
GLA_WIDTH = D_MIX // 2
POOL_WIDTH = D_MIX - GLA_WIDTH
GLA_HEADS = 4
GLA_DV = GLA_WIDTH // GLA_HEADS
GLA_DK = GLA_DV // 2
GLA_QK = GLA_HEADS * GLA_DK
GATE_RANK = 16
GATE_NORMALIZER = 16.0
GLA_CHUNK = 64
POOL_GROUPS = 4
POOL_GC = POOL_WIDTH // POOL_GROUPS
POOL_WINDOWS = (2, 4, 8, 16)
N_EXPERTS = 32
TOP_K = 4
D_FF = D_MODEL
SWIGLU_LIMIT = 7.0
SWIGLU_ALPHA = 1.702
EXPERT_BLOCK = 128
N_MOD = 6
EPS = 1e-6
D_IN = 2 * GLA_QK + 2 * GLA_WIDTH + 2 * GATE_RANK + POOL_WIDTH
SPLIT_POINTS = (GLA_QK, 2 * GLA_QK, 2 * GLA_QK + GLA_WIDTH, 2 * GLA_QK + 2 * GLA_WIDTH,
                2 * GLA_QK + 2 * GLA_WIDTH + GATE_RANK, 2 * GLA_QK + 2 * GLA_WIDTH + 2 * GATE_RANK)


def rmsnorm(x, w):
    xf = x.astype(jnp.float32)
    var = jnp.mean(xf * xf, axis=-1, keepdims=True)
    return (xf * lax.rsqrt(var + EPS) * w.astype(jnp.float32)).astype(x.dtype)

def modulate(h, shift, scale):
    return h * (1.0 + scale) + shift

def to_heads(t, d):
    b_, n, _ = t.shape
    return t.reshape(b_, n, GLA_HEADS, d).transpose(0, 2, 1, 3).astype(jnp.float32)

def mixer_inputs(p, w_gk_f, b_gk_f, w_gk_b, b_gk_b):
    q, k, v, g, r_f, r_b, pool_in = jnp.split(p, SPLIT_POINTS, axis=-1)
    gk_f = jax.nn.log_sigmoid((r_f @ w_gk_f + b_gk_f).astype(jnp.float32)) / GATE_NORMALIZER
    gk_b = jax.nn.log_sigmoid((r_b @ w_gk_b + b_gk_b).astype(jnp.float32)) / GATE_NORMALIZER
    return (to_heads(q, GLA_DK), to_heads(k, GLA_DK), to_heads(v, GLA_DV),
            to_heads(gk_f, GLA_DK), to_heads(gk_b, GLA_DK), g, pool_in)

def gla_chunked(q, k, v, gk, s0, with_output=True):
    b_, h_, t_, dk = q.shape
    dv = v.shape[-1]
    n_ch = t_ // GLA_CHUNK
    qc = q.reshape(b_, h_, n_ch, GLA_CHUNK, dk) * (dk ** -0.5)
    kc = k.reshape(b_, h_, n_ch, GLA_CHUNK, dk)
    vc = v.reshape(b_, h_, n_ch, GLA_CHUNK, dv)
    bcum = jnp.cumsum(gk.reshape(b_, h_, n_ch, GLA_CHUNK, dk), axis=3)
    b_last = bcum[:, :, :, -1:, :]
    u = jnp.einsum('bhnsk,bhnsv->bhnkv', kc * jnp.exp(b_last - bcum), vc)
    decay = jnp.exp(b_last[:, :, :, 0, :])

    def step(s, inp):
        d, un = inp
        return d[..., None] * s + un, s

    s_final, s_prev = lax.scan(step, s0, (jnp.moveaxis(decay, 2, 0), jnp.moveaxis(u, 2, 0)))
    if not with_output:
        return None, s_final
    s_prev = jnp.moveaxis(s_prev, 0, 2)
    b_mid = bcum[:, :, :, GLA_CHUNK // 2 - 1:GLA_CHUNK // 2, :]
    a = jnp.einsum('bhntk,bhnsk->bhnts', qc * jnp.exp(bcum - b_mid), kc * jnp.exp(b_mid - bcum))
    mask = jnp.tril(jnp.ones((GLA_CHUNK, GLA_CHUNK), dtype=bool))
    a = jnp.where(mask, a, 0.0)
    o = (jnp.einsum('bhnts,bhnsv->bhntv', a, vc)
         + jnp.einsum('bhntk,bhnkv->bhntv', qc * jnp.exp(bcum), s_prev))
    return o.reshape(b_, h_, t_, dv), s_final

def gla_bidir(q, k, v, gk_f, gk_b, s0_f, s0_b, with_output=True):
    flip = lambda t: jnp.flip(t, axis=2)
    o_f, s_f = gla_chunked(q, k, v, gk_f, s0_f, with_output)
    o_b, s_b = gla_chunked(flip(q), flip(k), flip(v), flip(gk_b), s0_b, with_output)
    o = o_f + flip(o_b) if with_output else None
    return o, s_f, s_b

def gla_output(o, g, w_norm):
    b_, _, n, _ = o.shape
    o = o.transpose(0, 2, 1, 3)
    o = o * lax.rsqrt(jnp.mean(o * o, axis=-1, keepdims=True) + EPS) * w_norm.astype(jnp.float32)
    gate = jax.nn.silu(g.astype(jnp.float32)).reshape(o.shape)
    return (o * gate).reshape(b_, n, GLA_WIDTH)

def window_bounds(pos, w, length):
    lo = w // 2
    hi = w - 1 - lo
    return jnp.clip(pos - lo, 0, length), jnp.clip(pos + hi + 1, 0, length)

def pool_grid(xp, rows):
    b_, n, _ = xp.shape
    xf = xp.astype(jnp.float32).reshape(b_, rows, GRID_W, POOL_GROUPS, POOL_GC)
    sat = jnp.pad(jnp.cumsum(jnp.cumsum(xf, axis=1), axis=2), ((0, 0), (1, 0), (1, 0), (0, 0), (0, 0)))
    r = jnp.arange(rows)
    col = jnp.arange(GRID_W)
    outs = []
    for gi, w in enumerate(POOL_WINDOWS):
        r0, r1 = window_bounds(r, w, rows)
        c0, c1 = window_bounds(col, w, GRID_W)
        s = sat[:, :, :, gi]
        s_r1, s_r0 = s[:, r1], s[:, r0]
        tot = s_r1[:, :, c1] - s_r0[:, :, c1] - s_r1[:, :, c0] + s_r0[:, :, c0]
        cnt = ((r1 - r0)[:, None] * (c1 - c0)[None, :]).astype(jnp.float32)
        outs.append(tot / cnt[None, :, :, None])
    mean = jnp.stack(outs, axis=3)
    return (mean - xf).reshape(b_, n, POOL_GROUPS, POOL_GC)

def pool_seq(xp):
    b_, n, _ = xp.shape
    xf = xp.astype(jnp.float32).reshape(b_, n, POOL_GROUPS, POOL_GC)
    cs = jnp.pad(jnp.cumsum(xf, axis=1), ((0, 0), (1, 0), (0, 0), (0, 0)))
    pos = jnp.arange(n)
    outs = []
    for gi, w in enumerate(POOL_WINDOWS):
        i0, i1 = window_bounds(pos, w, n)
        outs.append((cs[:, i1, gi] - cs[:, i0, gi]) / (i1 - i0).astype(jnp.float32)[None, :, None])
    return jnp.stack(outs, axis=2) - xf

def pool_project(pooled, w_pool, pool_scale):
    b_, n = pooled.shape[:2]
    y = jnp.einsum('bngc,gcd->bngd', pooled, w_pool.astype(jnp.float32)).reshape(b_, n, POOL_WIDTH)
    return y * pool_scale.astype(jnp.float32)

def moe(h, w_router, b_router, w_gu, b_gu, w_down, b_down):
    shp = h.shape
    xt = h.reshape(-1, D_MODEL)
    n_tok = xt.shape[0]
    n_assign = n_tok * TOP_K
    logits = (xt @ w_router + b_router).astype(jnp.float32)
    top_vals, top_idx = lax.top_k(logits, TOP_K)
    weights = jax.nn.softmax(top_vals, axis=-1)
    flat_e = top_idx.reshape(-1)
    flat_tok = jnp.repeat(jnp.arange(n_tok, dtype=jnp.int32), TOP_K)
    flat_w = weights.reshape(-1)
    order = jnp.argsort(flat_e)
    sorted_e = flat_e[order]
    counts = jnp.bincount(flat_e, length=N_EXPERTS)
    padded = (counts + EXPERT_BLOCK - 1) // EXPERT_BLOCK * EXPERT_BLOCK
    start_unpad = jnp.cumsum(counts) - counts
    pad_end = jnp.cumsum(padded)
    start_pad = pad_end - padded
    dest = start_pad[sorted_e] + (jnp.arange(n_assign) - start_unpad[sorted_e])
    n_pad = n_assign + N_EXPERTS * EXPERT_BLOCK
    n_blocks = n_pad // EXPERT_BLOCK
    buf_tok = jnp.full((n_pad,), n_tok, dtype=jnp.int32).at[dest].set(flat_tok[order])
    buf_w = jnp.zeros((n_pad,), jnp.float32).at[dest].set(flat_w[order])
    block_e = jnp.minimum(jnp.searchsorted(pad_end, jnp.arange(n_blocks) * EXPERT_BLOCK, side='right'),
                          N_EXPERTS - 1)
    x_pad = jnp.concatenate([xt, jnp.zeros((1, D_MODEL), xt.dtype)], axis=0)
    xb = x_pad[buf_tok].reshape(n_blocks, EXPERT_BLOCK, D_MODEL)

    def expert_block(args):
        xblk, e = args
        gu = xblk @ w_gu[e] + b_gu[e]
        gate, up = jnp.split(gu, 2, axis=-1)
        gate = jnp.minimum(gate, SWIGLU_LIMIT)
        up = jnp.clip(up, -SWIGLU_LIMIT, SWIGLU_LIMIT)
        act = (up + 1.0) * gate * jax.nn.sigmoid(SWIGLU_ALPHA * gate)
        return act @ w_down[e] + b_down[e]

    yb = lax.map(expert_block, (xb, block_e)).reshape(n_pad, D_MODEL)
    y = jnp.zeros((n_tok + 1, D_MODEL), yb.dtype).at[buf_tok].add(yb * buf_w[:, None].astype(yb.dtype))
    return y[:n_tok].reshape(shp)

def first_inputs(seed: int = 0) -> dict:
    key = jax.random.key(seed)
    ks = jax.random.split(key, 32)
    nrm = lambda k, shp, s: jax.random.normal(k, shp, jnp.float32) * s
    L, D, E = DEPTH, D_MODEL, N_EXPERTS
    return {
        "x": nrm(ks[0], (BATCH, SEQ, D), 1.0),
        "c": nrm(ks[1], (BATCH, D), 1.0),
        "ctx": nrm(ks[2], (BATCH, CTX_LEN, D), 1.0),
        "c_ctx": nrm(ks[3], (D,), 1.0),
        "w_ada": nrm(ks[4], (L, D, N_MOD * D), 0.5 * D ** -0.5),
        "b_ada": nrm(ks[5], (L, N_MOD * D), 0.02),
        "norm_mix_w": 1.0 + nrm(ks[6], (L, D), 0.02),
        "norm_mlp_w": 1.0 + nrm(ks[7], (L, D), 0.02),
        "w_in": nrm(ks[8], (L, D, D_IN), D ** -0.5),
        "w_gk_f": nrm(ks[9], (L, GATE_RANK, GLA_QK), GATE_RANK ** -0.5),
        "b_gk_f": jax.random.uniform(ks[10], (L, GLA_QK), jnp.float32, -2.0, 4.0),
        "w_gk_b": nrm(ks[11], (L, GATE_RANK, GLA_QK), GATE_RANK ** -0.5),
        "b_gk_b": jax.random.uniform(ks[12], (L, GLA_QK), jnp.float32, -2.0, 4.0),
        "gla_norm_w": 1.0 + nrm(ks[13], (L, GLA_DV), 0.02),
        "w_pool": nrm(ks[14], (L, POOL_GROUPS, POOL_GC, POOL_GC), POOL_GC ** -0.5),
        "pool_scale": 1.0 + nrm(ks[15], (L, POOL_WIDTH), 0.1),
        "w_out": nrm(ks[16], (L, D_MIX, D), D_MIX ** -0.5),
        "w_router": nrm(ks[17], (L, D, E), D ** -0.5),
        "b_router": nrm(ks[18], (L, E), 0.01),
        "w_gu": nrm(ks[19], (L, E, D, 2 * D_FF), D ** -0.5),
        "b_gu": nrm(ks[20], (L, E, 2 * D_FF), 0.02),
        "w_down": nrm(ks[21], (L, E, D_FF, D), D_FF ** -0.5),
        "b_down": nrm(ks[22], (L, E, D), 0.02),
        "final_norm_w": 1.0 + nrm(ks[23], (D,), 0.02),
    }

def first_block(x, c, ctx, c_ctx, w_ada, b_ada, norm_mix_w, norm_mlp_w, w_in, w_gk_f, b_gk_f, w_gk_b,
              b_gk_b, gla_norm_w, w_pool, pool_scale, w_out, w_router, b_router, w_gu, b_gu, w_down,
              b_down, final_norm_w):
    h, hc = x, ctx
    b_, n_lat, _ = x.shape
    rows = n_lat // GRID_W
    for l in range(DEPTH):
        last = l == DEPTH - 1
        mod_x = (jax.nn.silu(c) @ w_ada[l] + b_ada[l])[:, None, :]
        mod_c = jax.nn.silu(c_ctx) @ w_ada[l] + b_ada[l]
        sh1, sc1, g1, sh2, sc2, g2 = jnp.split(mod_x, N_MOD, axis=-1)
        csh1, csc1, cg1, csh2, csc2, cg2 = jnp.split(mod_c, N_MOD, axis=-1)

        p_x = modulate(rmsnorm(h, norm_mix_w[l]), sh1, sc1) @ w_in[l]
        p_c = modulate(rmsnorm(hc, norm_mix_w[l]), csh1, csc1) @ w_in[l]
        qx, kx, vx, gkfx, gkbx, gx, poolx = mixer_inputs(p_x, w_gk_f[l], b_gk_f[l], w_gk_b[l], b_gk_b[l])
        qc, kc, vc, gkfc, gkbc, gc, poolc = mixer_inputs(p_c, w_gk_f[l], b_gk_f[l], w_gk_b[l], b_gk_b[l])

        s0 = jnp.zeros((b_, GLA_HEADS, GLA_DK, GLA_DV), jnp.float32)
        o_c, s_f, s_b = gla_bidir(qc, kc, vc, gkfc, gkbc, s0, s0, with_output=not last)
        o_x, _, _ = gla_bidir(qx, kx, vx, gkfx, gkbx, s_f, s_b)

        mix_x = jnp.concatenate([gla_output(o_x, gx, gla_norm_w[l]),
                                 pool_project(pool_grid(poolx, rows), w_pool[l], pool_scale[l])], axis=-1)
        h = h + g1 * (mix_x.astype(h.dtype) @ w_out[l])

        if not last:
            mix_c = jnp.concatenate([gla_output(o_c, gc, gla_norm_w[l]),
                                     pool_project(pool_seq(poolc), w_pool[l], pool_scale[l])], axis=-1)
            hc = hc + cg1 * (mix_c.astype(hc.dtype) @ w_out[l])
            hc = hc + cg2 * moe(modulate(rmsnorm(hc, norm_mlp_w[l]), csh2, csc2),
                                w_router[l], b_router[l], w_gu[l], b_gu[l], w_down[l], b_down[l])

        h = h + g2 * moe(modulate(rmsnorm(h, norm_mlp_w[l]), sh2, sc2),
                         w_router[l], b_router[l], w_gu[l], b_gu[l], w_down[l], b_down[l])
    return rmsnorm(h, final_norm_w)


DEPTH_2 = 2

PLE_DIM = 256
ROPE_THETA = 10000.0
NORM_EPS = 1e-6
Q_BLOCK = 128

RET_WIDTH = D_MODEL // 2
RET_HEADS = 8
RET_HEAD_DIM = RET_WIDTH // RET_HEADS
RET_CHUNK = 128
S5_WIDTH = D_MODEL - RET_WIDTH
S5_GROUP = 16
S5_GROUPS = S5_WIDTH // S5_GROUP
S5_STATE = 64
EVEN_IN_WIDTH = 4 * RET_WIDTH + S5_WIDTH
MIX_WIDTH = RET_WIDTH + S5_WIDTH

DIFF_HEADS = 8
DIFF_QK_DIM = 64
DIFF_V_DIM = 2 * DIFF_QK_DIM
DIFF_QK_WIDTH = DIFF_HEADS * 2 * DIFF_QK_DIM
DIFF_WIDTH = DIFF_HEADS * DIFF_V_DIM
DIFF_IN_WIDTH = 2 * DIFF_QK_WIDTH + DIFF_WIDTH

FFN_HIDDEN = -(-8 * D_MODEL // (3 * 256)) * 256

N_EVEN = (DEPTH_2 + 1) // 2
N_ODD = DEPTH_2 // 2


def rms_norm(x, gain):
    xf = x.astype(jnp.float32)
    y = xf * lax.rsqrt(jnp.mean(xf * xf, axis=-1, keepdims=True) + NORM_EPS)
    return (y * gain.astype(jnp.float32)).astype(x.dtype)

def head_layer_norm(x):
    mu = jnp.mean(x, axis=-1, keepdims=True)
    xc = x - mu
    return xc * lax.rsqrt(jnp.mean(xc * xc, axis=-1, keepdims=True) + NORM_EPS)

def rotary(x, pos):
    d = x.shape[-1]
    inv = ROPE_THETA ** (-jnp.arange(0, d, 2, dtype=jnp.float32) / d)
    ang = pos.astype(jnp.float32)[:, None] * inv[None, :]
    cos = jnp.concatenate([jnp.cos(ang), jnp.cos(ang)], axis=-1)
    sin = jnp.concatenate([jnp.sin(ang), jnp.sin(ang)], axis=-1)
    xf = x.astype(jnp.float32)
    x1, x2 = xf[..., : d // 2], xf[..., d // 2:]
    rot = jnp.concatenate([-x2, x1], axis=-1)
    return (xf * cos + rot * sin).astype(x.dtype)

def retention(q, k, v):
    bsz, n_h, s_len, d = q.shape
    c = RET_CHUNK
    n_chunks = s_len // c
    gamma = 1.0 - 2.0 ** (-5.0 - jnp.arange(n_h, dtype=jnp.float32))
    log_g = jnp.log(gamma)
    idx = jnp.arange(c, dtype=jnp.float32)
    rel = idx[:, None] - idx[None, :]
    intra_decay = jnp.where(rel >= 0, jnp.exp(log_g[:, None, None] * jnp.maximum(rel, 0.0)), 0.0)
    k_decay = jnp.exp(log_g[:, None] * (c - 1 - idx))
    q_decay = jnp.exp(log_g[:, None] * (idx + 1.0))
    chunk_decay = jnp.exp(log_g * c)
    qf = q.astype(jnp.float32).reshape(bsz, n_h, n_chunks, c, d)
    kf = k.astype(jnp.float32).reshape(bsz, n_h, n_chunks, c, d) * (d ** -0.5)
    vf = v.astype(jnp.float32).reshape(bsz, n_h, n_chunks, c, d)
    scores = jnp.einsum('bhncd,bhnsd->bhncs', qf, kf) * intra_decay[:, None]
    intra = jnp.einsum('bhncs,bhnse->bhnce', scores, vf)
    kv = jnp.einsum('bhnsd,bhnse->nbhde', kf * k_decay[:, None, :, None], vf)

    def step(r_state, kv_n):
        return chunk_decay[:, None, None] * r_state + kv_n, r_state

    _, r_prev = lax.scan(step, jnp.zeros_like(kv[0]), kv)
    inter = jnp.einsum('bhncd,nbhde->bhnce', qf * q_decay[:, None, :, None], r_prev)
    return (intra + inter).reshape(bsz, n_h, s_len, d)

def s5_mixer(u, lam_re, lam_im, b_re, b_im, c_re, c_im, d_skip, log_step, w_glu):
    bsz, s_len, _ = u.shape
    f32 = jnp.float32
    uf = u.astype(f32).reshape(bsz, s_len, S5_GROUPS, S5_GROUP)
    lam = lax.complex(lam_re.astype(f32), lam_im.astype(f32))
    delta = jnp.exp(log_step.astype(f32))[:, None]
    lam_bar = jnp.exp(lam * delta)
    b_mat = lax.complex(b_re.astype(f32), b_im.astype(f32))
    b_bar = ((lam_bar - 1.0) / lam)[:, :, None] * b_mat
    bu = jnp.einsum('gpc,bsgc->bsgp', b_bar, uf.astype(jnp.complex64))
    a = jnp.broadcast_to(lam_bar, bu.shape)

    def combine(e1, e2):
        a1, x1 = e1
        a2, x2 = e2
        return a2 * a1, a2 * x1 + x2

    _, states = lax.associative_scan(combine, (a, bu), axis=1)
    c_mat = lax.complex(c_re.astype(f32), c_im.astype(f32))
    y = jnp.einsum('gcp,bsgp->bsgc', c_mat, states).real + d_skip.astype(f32) * uf
    y = jax.nn.gelu(y.reshape(bsz, s_len, S5_WIDTH))
    y = y * jax.nn.sigmoid(y @ w_glu.astype(f32))
    return y.astype(u.dtype)

def even_mixer(h, pos, w_in, w_out, lam_re, lam_im, b_re, b_im, c_re, c_im, d_skip, log_step, w_glu):
    bsz, s_len, _ = h.shape
    proj = h @ w_in
    q, k, v, g, u = jnp.split(proj, [RET_WIDTH, 2 * RET_WIDTH, 3 * RET_WIDTH, 4 * RET_WIDTH], axis=-1)

    def heads(t):
        return t.reshape(bsz, s_len, RET_HEADS, RET_HEAD_DIM).transpose(0, 2, 1, 3)

    ret = retention(rotary(heads(q), pos), rotary(heads(k), pos), heads(v))
    ret = head_layer_norm(ret).transpose(0, 2, 1, 3).reshape(bsz, s_len, RET_WIDTH)
    ret = (jax.nn.silu(g.astype(jnp.float32)) * ret).astype(h.dtype)
    ssm = s5_mixer(u, lam_re, lam_im, b_re, b_im, c_re, c_im, d_skip, log_step, w_glu)
    return jnp.concatenate([ret, ssm], axis=-1) @ w_out

def diff_attention(h, pos, w_qkv, w_o, lq1, lk1, lq2, lk2, subln, lambda_init):
    bsz, s_len, _ = h.shape
    f32 = jnp.float32
    proj = h @ w_qkv
    q, k, v = jnp.split(proj, [DIFF_QK_WIDTH, 2 * DIFF_QK_WIDTH], axis=-1)
    q = rotary(q.reshape(bsz, s_len, 2 * DIFF_HEADS, DIFF_QK_DIM).transpose(0, 2, 1, 3), pos)
    k = rotary(k.reshape(bsz, s_len, 2 * DIFF_HEADS, DIFF_QK_DIM).transpose(0, 2, 1, 3), pos)
    vf = v.reshape(bsz, s_len, DIFF_HEADS, DIFF_V_DIM).transpose(0, 2, 1, 3).astype(f32)
    kf = k.astype(f32)
    lam = (jnp.exp(jnp.sum(lq1.astype(f32) * lk1.astype(f32)))
           - jnp.exp(jnp.sum(lq2.astype(f32) * lk2.astype(f32))) + lambda_init)
    scale = DIFF_QK_DIM ** -0.5
    n_blocks = s_len // Q_BLOCK
    q_blocks = q.reshape(bsz, 2 * DIFF_HEADS, n_blocks, Q_BLOCK, DIFF_QK_DIM).transpose(2, 0, 1, 3, 4)
    qpos_blocks = pos.reshape(n_blocks, Q_BLOCK)

    def block(args):
        qblk, qpos = args
        s = jnp.einsum('bhqd,bhkd->bhqk', qblk.astype(f32), kf) * scale
        s = jnp.where(pos[None, :] <= qpos[:, None], s, -jnp.inf)
        att = jax.nn.softmax(s, axis=-1).reshape(bsz, DIFF_HEADS, 2, Q_BLOCK, s_len)
        w = att[:, :, 0] - lam * att[:, :, 1]
        return jnp.einsum('bhqk,bhkd->bhqd', w, vf)

    out = lax.map(block, (q_blocks, qpos_blocks))
    out = out.transpose(1, 2, 0, 3, 4).reshape(bsz, DIFF_HEADS, s_len, DIFF_V_DIM)
    out = rms_norm(out, subln) * (1.0 - lambda_init)
    out = out.transpose(0, 2, 1, 3).reshape(bsz, s_len, DIFF_WIDTH).astype(h.dtype)
    return out @ w_o

def swiglu(h, w_gate, w_up, w_down):
    return (jax.nn.silu(h @ w_gate) * (h @ w_up)) @ w_down

def second_inputs(seed: int = 0) -> dict:
    key = jax.random.key(seed)
    ks = jax.random.split(key, 32)
    nrm = jax.random.normal
    f32 = jnp.float32
    inp = {}
    inp['x'] = nrm(ks[0], (BATCH, SEQ, D_MODEL), f32)
    inp['p'] = nrm(ks[1], (DEPTH_2, BATCH, SEQ, PLE_DIM), f32)
    inp['norm_mix'] = 1.0 + 0.02 * nrm(ks[2], (DEPTH_2, D_MODEL), f32)
    inp['norm_ffn'] = 1.0 + 0.02 * nrm(ks[3], (DEPTH_2, D_MODEL), f32)
    inp['norm_ple'] = 1.0 + 0.02 * nrm(ks[4], (DEPTH_2, D_MODEL), f32)
    inp['ret_s5_w_in'] = nrm(ks[5], (N_EVEN, D_MODEL, EVEN_IN_WIDTH), f32) * D_MODEL ** -0.5
    inp['ret_s5_w_out'] = nrm(ks[6], (N_EVEN, MIX_WIDTH, D_MODEL), f32) * MIX_WIDTH ** -0.5
    inp['s5_lambda_re'] = -0.5 + 0.01 * nrm(ks[7], (N_EVEN, S5_GROUPS, S5_STATE), f32)
    inp['s5_lambda_im'] = (math.pi * jnp.arange(S5_STATE, dtype=f32)
                           + 0.01 * nrm(ks[8], (N_EVEN, S5_GROUPS, S5_STATE), f32))
    inp['s5_b_re'] = nrm(ks[9], (N_EVEN, S5_GROUPS, S5_STATE, S5_GROUP), f32) * (2 * S5_GROUP) ** -0.5
    inp['s5_b_im'] = nrm(ks[10], (N_EVEN, S5_GROUPS, S5_STATE, S5_GROUP), f32) * (2 * S5_GROUP) ** -0.5
    inp['s5_c_re'] = nrm(ks[11], (N_EVEN, S5_GROUPS, S5_GROUP, S5_STATE), f32) * S5_STATE ** -0.5
    inp['s5_c_im'] = nrm(ks[12], (N_EVEN, S5_GROUPS, S5_GROUP, S5_STATE), f32) * S5_STATE ** -0.5
    inp['s5_d'] = nrm(ks[13], (N_EVEN, S5_GROUPS, S5_GROUP), f32)
    inp['s5_log_step'] = jax.random.uniform(ks[14], (N_EVEN, S5_GROUPS), f32,
                                            minval=math.log(1e-3), maxval=math.log(1e-1))
    inp['s5_w_glu'] = nrm(ks[15], (N_EVEN, S5_WIDTH, S5_WIDTH), f32) * S5_WIDTH ** -0.5
    inp['diff_w_qkv'] = nrm(ks[16], (N_ODD, D_MODEL, DIFF_IN_WIDTH), f32) * D_MODEL ** -0.5
    inp['diff_w_o'] = nrm(ks[17], (N_ODD, DIFF_WIDTH, D_MODEL), f32) * DIFF_WIDTH ** -0.5
    inp['diff_lambda_q1'] = 0.1 * nrm(ks[18], (N_ODD, DIFF_QK_DIM), f32)
    inp['diff_lambda_k1'] = 0.1 * nrm(ks[19], (N_ODD, DIFF_QK_DIM), f32)
    inp['diff_lambda_q2'] = 0.1 * nrm(ks[20], (N_ODD, DIFF_QK_DIM), f32)
    inp['diff_lambda_k2'] = 0.1 * nrm(ks[21], (N_ODD, DIFF_QK_DIM), f32)
    inp['diff_subln'] = 1.0 + 0.02 * nrm(ks[22], (N_ODD, DIFF_V_DIM), f32)
    inp['ffn_w_gate'] = nrm(ks[23], (DEPTH_2, D_MODEL, FFN_HIDDEN), f32) * D_MODEL ** -0.5
    inp['ffn_w_up'] = nrm(ks[24], (DEPTH_2, D_MODEL, FFN_HIDDEN), f32) * D_MODEL ** -0.5
    inp['ffn_w_down'] = nrm(ks[25], (DEPTH_2, FFN_HIDDEN, D_MODEL), f32) * FFN_HIDDEN ** -0.5
    inp['ple_w_proj'] = nrm(ks[26], (DEPTH_2, PLE_DIM, D_MODEL), f32) * PLE_DIM ** -0.5
    inp['ple_w_gate'] = nrm(ks[27], (DEPTH_2, D_MODEL, D_MODEL), f32) * D_MODEL ** -0.5
    inp['final_norm'] = 1.0 + 0.02 * nrm(ks[28], (D_MODEL,), f32)
    return inp

def second_block(x, p, norm_mix, norm_ffn, norm_ple, ret_s5_w_in, ret_s5_w_out,
              s5_lambda_re, s5_lambda_im, s5_b_re, s5_b_im, s5_c_re, s5_c_im, s5_d,
              s5_log_step, s5_w_glu, diff_w_qkv, diff_w_o, diff_lambda_q1, diff_lambda_k1,
              diff_lambda_q2, diff_lambda_k2, diff_subln, ffn_w_gate, ffn_w_up, ffn_w_down,
              ple_w_proj, ple_w_gate, final_norm):
    pos = jnp.arange(x.shape[1], dtype=jnp.int32)
    h = x
    for i in range(DEPTH_2):
        hn = rms_norm(h, norm_mix[i])
        j = i // 2
        if i % 2 == 0:
            mix = even_mixer(hn, pos, ret_s5_w_in[j], ret_s5_w_out[j],
                             s5_lambda_re[j], s5_lambda_im[j], s5_b_re[j], s5_b_im[j],
                             s5_c_re[j], s5_c_im[j], s5_d[j], s5_log_step[j], s5_w_glu[j])
        else:
            lambda_init = 0.8 - 0.6 * math.exp(-0.3 * i)
            mix = diff_attention(hn, pos, diff_w_qkv[j], diff_w_o[j],
                                 diff_lambda_q1[j], diff_lambda_k1[j],
                                 diff_lambda_q2[j], diff_lambda_k2[j], diff_subln[j], lambda_init)
        h = h + mix
        h = h + swiglu(rms_norm(h, norm_ffn[i]), ffn_w_gate[i], ffn_w_up[i], ffn_w_down[i])
        gate = jax.nn.sigmoid(rms_norm(h, norm_ple[i]) @ ple_w_gate[i])
        h = h + (p[i] @ ple_w_proj[i]) * gate
    return rms_norm(h, final_norm)


_first_inputs = second_inputs


def second_inputs(seed=0):
    import zlib

    import numpy as np

    out = dict(_first_inputs(seed))
    spreads = {}
    factors = {'norm_ffn': 3.299,
     'norm_ple': 8.0,
     's5_lambda_re': 8.0,
     's5_b_re': 3.524,
     's5_b_im': 3.497,
     's5_c_re': 3.5,
     's5_c_im': 3.572,
     'diff_lambda_q2': 2.891,
     'diff_subln': 7.56,
     'final_norm': 2.75}
    for name, (base, spread) in spreads.items():
        noise = np.random.default_rng([zlib.crc32(name.encode()), seed]).standard_normal(out[name].shape)
        drawn = base * np.exp(spread * noise) if base else spread * noise
        out[name] = __import__('jax').numpy.asarray(drawn.astype(out[name].dtype))
    for name, factor in factors.items():
        out[name] = (out[name] * factor).astype(out[name].dtype)
    return out


_narrow_inputs = second_inputs


def second_inputs(seed=0):

    out = dict(_narrow_inputs(seed))
    wider = {'norm_ple': 12.0, 's5_lambda_re': 12.0, 'diff_subln': 5.76, 'final_norm': 3.09}
    for name, times in wider.items():
        mean = out[name].mean()
        out[name] = (mean + times * (out[name] - mean)).astype(out[name].dtype)
    return out


def setup_inputs(seed=0):
    out = dict(first_inputs(seed))
    for name, value in second_inputs(seed + 1).items():
        if name != "x":
            out[name + "_2"] = value
    return out


def reference(
    x, c, ctx, c_ctx, w_ada, b_ada, norm_mix_w, norm_mlp_w, w_in, w_gk_f, b_gk_f, w_gk_b,
    b_gk_b, gla_norm_w, w_pool, pool_scale, w_out, w_router, b_router, w_gu, b_gu, w_down,
    b_down, final_norm_w, p_2, norm_mix_2, norm_ffn_2, norm_ple_2, ret_s5_w_in_2,
    ret_s5_w_out_2, s5_lambda_re_2, s5_lambda_im_2, s5_b_re_2, s5_b_im_2, s5_c_re_2, s5_c_im_2,
    s5_d_2, s5_log_step_2, s5_w_glu_2, diff_w_qkv_2, diff_w_o_2, diff_lambda_q1_2,
    diff_lambda_k1_2, diff_lambda_q2_2, diff_lambda_k2_2, diff_subln_2, ffn_w_gate_2,
    ffn_w_up_2, ffn_w_down_2, ple_w_proj_2, ple_w_gate_2, final_norm_2,
):
    x = first_block(
        x, c, ctx, c_ctx, w_ada, b_ada, norm_mix_w, norm_mlp_w, w_in, w_gk_f, b_gk_f, w_gk_b,
        b_gk_b, gla_norm_w, w_pool, pool_scale, w_out, w_router, b_router, w_gu, b_gu, w_down,
        b_down, final_norm_w,
    )
    return second_block(
        x, p_2, norm_mix_2, norm_ffn_2, norm_ple_2, ret_s5_w_in_2, ret_s5_w_out_2,
        s5_lambda_re_2, s5_lambda_im_2, s5_b_re_2, s5_b_im_2, s5_c_re_2, s5_c_im_2, s5_d_2,
        s5_log_step_2, s5_w_glu_2, diff_w_qkv_2, diff_w_o_2, diff_lambda_q1_2, diff_lambda_k1_2,
        diff_lambda_q2_2, diff_lambda_k2_2, diff_subln_2, ffn_w_gate_2, ffn_w_up_2,
        ffn_w_down_2, ple_w_proj_2, ple_w_gate_2, final_norm_2,
    )


_drawn_inputs = setup_inputs


def setup_inputs(seed=0):
    import zlib

    import numpy as np

    out = dict(_drawn_inputs(seed))
    spreads = {}
    factors = {'gla_norm_w': 4.098, 'b_gu': 5.493, 'b_down': 6.488, 'diff_lambda_q1_2': 6.033}
    for name, (base, spread) in spreads.items():
        noise = np.random.default_rng([zlib.crc32(name.encode()), seed]).standard_normal(out[name].shape)
        drawn = base * np.exp(spread * noise) if base else spread * noise
        out[name] = __import__('jax').numpy.asarray(drawn.astype(out[name].dtype))
    for name, factor in factors.items():
        out[name] = (out[name] * factor).astype(out[name].dtype)
    return out
```

```python
import numpy as np
import concourse.bass as bass
from concourse import mybir

F32 = mybir.dt.float32
BF16 = mybir.dt.bfloat16
I32 = mybir.dt.int32
U32 = mybir.dt.uint32
ALU = mybir.AluOpType
ACT = mybir.ActivationFunctionType
AX = mybir.AxisListType

EPS = 1e-6
NRING = 6
SLOT = 4096
NBLK = 47
LAMBDA_INIT = 0.8 - 0.6 * float(np.exp(-0.3))
TWO_PI = 2.0 * float(np.pi)


def const_tables():
    f = np.float32
    p = np.arange(128)
    out = {}
    out["ident"] = np.eye(128, dtype=f)
    out["ones"] = np.ones((128, 128), f)
    out["tri"] = (p[:, None] < p[None, :]).astype(f)
    same = (p[:, None] // 64) == (p[None, :] // 64)
    out["maskf"] = np.tile(((p[:, None] <= p[None, :]) & same).astype(f), (1, 4))
    out["maskb"] = np.tile(((p[:, None] >= p[None, :]) & same).astype(f), (1, 4))
    out["scan"] = np.tile((np.arange(768) % 64 != 0).astype(f), (128, 1))
    out["iota"] = np.tile(np.arange(128, dtype=f), (128, 1))
    out["tok"] = (p[:, None] + 128 * np.arange(4)[None, :]).astype(f)
    out["pmod"] = np.tile((p % 32).astype(f)[:, None], (1, 4))
    out["sel"] = (p[:, None] % 32 == np.arange(32)[None, :]).astype(f)
    inv = (10000.0 ** (-np.arange(0, 64, 2, dtype=f) / f(64))).astype(f)
    ang = (np.arange(512, dtype=f)[None, :] * inv[p % 32][:, None]).astype(f)
    out["cos"] = np.cos(ang.astype(np.float64)).astype(f)
    out["sin"] = np.sin(ang.astype(np.float64)).astype(f)
    rot = np.zeros((128, 128), f)
    for m in range(128):
        b, r = m // 64 * 64, m % 64
        rot[b + (r + 32) % 64, m] = -1.0 if r < 32 else 1.0
    out["rot"] = rot
    gamma = (1.0 - 2.0 ** (-5.0 - np.arange(8, dtype=f))).astype(f)
    lg = np.log(gamma).astype(f).astype(np.float64)
    rel = p[None, :] - p[:, None]
    dt = np.where(rel[None] >= 0, np.exp(lg[:, None, None] * np.maximum(rel, 0)[None]), 0.0) * 0.125
    out["dt"] = np.concatenate(list(dt), axis=1).astype(f)
    out["kdec"] = np.repeat(np.exp(lg[None, :] * (127 - p[:, None])) * 0.125, 64, axis=1).astype(f)
    qd = np.exp(lg[:, None] * (p[None, :] + 1.0))
    out["qdec"] = np.concatenate([np.repeat(qd[2 * i:2 * i + 2], 64, axis=0) for i in range(4)], axis=1).astype(f)
    cd = np.exp(lg * 128.0)
    out["cdec"] = np.stack([np.repeat(cd[2 * i:2 * i + 2], 64) for i in range(4)], axis=1).astype(f)
    out["b64"] = same.astype(f)
    out["caus"] = np.where(p[None, :] <= p[:, None], 0.0, -1e30).astype(f)
    jm = np.zeros((128, 128), f)
    for m in range(64):
        jm[m + 64, m] = -1.0
        jm[m, m + 64] = 1.0
    out["jm"] = jm
    out["b16"] = ((p[:, None] // 16) == (p[None, :] // 16)).astype(f)
    return out


def pool_tables():
    f = np.float64
    out = []
    for w in (2, 4, 8, 16):
        lo = w // 2
        hi = w - 1 - lo

        def band(n):
            i = np.arange(n)
            a = np.clip(i - lo, 0, n)
            b = np.clip(i + hi + 1, 0, n)
            m = ((i[:, None] >= a[None, :]) & (i[:, None] < b[None, :])).astype(f)
            return m, (b - a).astype(f)

        mr, cr = band(8)
        mc, cc = band(64)
        m = np.kron(mr, mc) / np.kron(cr, cc)[None, :]
        out.append((m - np.eye(512)).astype(np.float32))
    return np.stack(out)


TABLE_ORDER = ["ident", "ones", "tri", "maskf", "maskb", "scan", "iota", "tok", "pmod", "sel", "cos", "sin",
               "rot", "dt", "kdec", "qdec", "cdec", "b64", "caus", "jm", "b16"]


def table_offsets():
    t = const_tables()
    at, out = 0, {}
    for n in TABLE_ORDER:
        out[n] = (at, t[n].shape[1])
        at += t[n].shape[1]
    return out, at


class Queue:

    def __init__(self, sem, chained):
        self.sem, self.chained = sem, chained
        self.ops, self.n, self.seen = [], 0, {}

    @property
    def now(self):
        return (self.sem, self.n)

    def wait(self, *toks):
        for sem, val in toks:
            if val > self.seen.get(sem, 0):
                self.seen[sem] = val
                self.ops.append((0, sem, val))

    def do(self, fn, *toks, inc=True):
        self.wait(*toks)
        if self.chained:
            self.wait(self.now)
        if inc:
            self.n += 1
        self.ops.append((1, fn, inc))
        return self.now

    def dma(self, sem, counts, fn, *toks):
        self.wait(*toks)
        counts[sem] = counts.get(sem, 0) + 16
        self.ops.append((2, fn, sem))
        return (sem, counts[sem])

    def emit(self, eng, shift=None, after=None):
        for kind, a, b in self.ops:
            if kind == 3:
                a(eng)
                continue
            if kind == 0:
                eng.wait_ge(a, shift(a, b) if shift else b)
                if shift:
                    eng.sem_inc(after, 1)
            elif kind == 1:
                ins = a(eng)
                if b:
                    ins.then_inc(self.sem, 1)
            else:
                a(eng).then_inc(b, 16)


def build(nc, ins, out):
    TOFF, _ = table_offsets()

    def sb(name, shape, dt=F32):
        return nc.alloc_sbuf_tensor(name, shape, dt)

    ring = sb("ring", [128, NRING * SLOT])
    H = sb("H", [128, 8 * 512])
    KC = sb("KC", [128, 256])
    COLS = sb("COLS", [128, 160])
    MOD = sb("MOD", [128, 96])
    SM = sb("SM", [128, 256])
    ar = sb("arena", [128, 22528])
    PB = [nc.alloc_psum_tensor(f"pb{i}", [128, 512], F32) for i in range(8)]
    hm_d = nc.dram_tensor("hm_scratch", (512, 1024), F32).ap()
    y_d = nc.dram_tensor("y_scratch", (NBLK * 128, 1024), F32).ap()
    ZB = sb("ZB", [128, 1024])
    ident = KC[:, 0:128]
    ones = KC[:, 128:256]

    def sem(name):
        return nc.alloc_semaphore(name)

    V = Queue(sem("s_dve"), True)
    A = Queue(sem("s_act"), True)
    G = Queue(sem("s_pool"), True)
    P = Queue(sem("s_pe"), False)
    S = Queue(sem("s_sp"), False)
    QS = (V, A, G, P)
    counts = {}
    s_ring = [sem(f"s_ring{i}") for i in range(NRING)]
    s_small = {}

    def load(q, name, dst, src, *toks):
        if name not in s_small:
            s_small[name] = sem("s_" + name)
        return q.dma(s_small[name], counts, lambda e: e.dma_start(dst, src), *toks)

    def a(lo, n, shape=None):
        v = ar[:, lo:lo + n]
        if shape is not None:
            v = v.rearrange("p (a b) -> p a b", b=shape)
        return v

    def barrier():
        toks = [q.now for q in QS]
        for q in QS:
            q.wait(*[t for t in toks if t[1]])

    pieces = []

    class Piece:
        pass

    def piece(parts, dt=F32):
        w = Piece()
        w.i = len(pieces)
        slot = w.i % NRING
        base = slot * SLOT
        prev = pieces[w.i - NRING] if w.i >= NRING else None
        if prev is not None:
            assert prev.free is not None, "a slot that nobody gave back"
            S.wait(*prev.free)
        for off, src in parts:
            n = src.shape[1] * src.shape[2]
            dst = ring[:, base + off:base + off + n].rearrange("p (a b) -> p a b", b=src.shape[2])
            w.tok = S.dma(s_ring[slot], counts, lambda e, d=dst, s=src: e.dma_start(d, s))
        w.base = base
        w.free = None
        pieces.append(w)
        return w

    queue = []

    def plan(parts):
        queue.append(parts)

    opened = []

    def refill():
        while queue and (len(pieces) < NRING or pieces[len(pieces) - NRING].free is not None):
            opened.append(piece(queue.pop(0)))

    def take():
        refill()
        return opened.pop(0)

    def give(w, *toks):
        w.free = toks
        refill()

    def rv(w, off, na, nb):
        return ring[:, w.base + off:w.base + off + na * nb].rearrange("p (a b) -> p a b", b=nb)

    bfree = [[] for _ in range(8)]
    turn = [0]

    def bank(held=()):
        while True:
            b = turn[0] % 8
            turn[0] += 1
            if b not in held:
                return b

    def wsrc(w, rows, lo, n):
        return w[:, lo:lo + n].rearrange("(j p) n -> p j n", p=128)

    def mm(outp, lhsT, rhs, start, stop, *toks, inc=False):
        return P.do(lambda e: e.matmul(outp, lhsT, rhs, start=start, stop=stop, skip_group_check=True),
                    *toks, inc=inc)

    def tp(outp, in_, *toks, inc=False):
        k = in_.shape[0]
        return P.do(lambda e: e.transpose(outp, in_, ident[0:k, 0:k]), *toks, inc=inc)

    def vtt(o, x, y, op, *toks, q=None):
        return (q or V).do(lambda e: e.tensor_tensor(o, x, y, op), *toks)

    def vts(o, x, s1, s2, op0, op1, *toks, q=None):
        if op1 is None:
            return (q or V).do(lambda e: e.tensor_scalar(o, x, s1, None, op0), *toks)
        return (q or V).do(lambda e: e.tensor_scalar(o, x, s1, s2, op0, op1), *toks)

    def stt(o, x, s, y, op0, op1, *toks):
        return V.do(lambda e: e.scalar_tensor_tensor(out=o, in0=x, scalar=s, in1=y, op0=op0, op1=op1), *toks)

    def act(o, x, f, *toks, bias=None, scale=None, accum=None):
        kw = {}
        if bias is not None:
            kw["bias"] = bias
        if scale is not None:
            kw["scale"] = scale
        if accum is not None:
            kw["accum_out"] = accum
        return A.do(lambda e: e.activation(o, x, f, **kw), *toks)

    def copy(q, o, x, *toks):
        if q is A:
            return act(o, x, ACT.Copy, *toks)
        return q.do(lambda e: e.tensor_copy(o, x), *toks)

    def dense(ncols_list, rhs_fn, ktg, evac, *toks, mode="fm", ntile=4, held=()):
        for c, width in enumerate(ncols_list):
            nt = (width // 128) if mode == "fm" else ntile
            banks = [bank(held) for _ in range(nt)]
            k0 = 0
            for gi, g in enumerate(ktg):
                w = take()
                wv = rv(w, 0, g, width)
                last = gi == len(ktg) - 1
                for m in range(nt):
                    b = banks[m]
                    for k in range(g):
                        kk = k0 + k
                        st, sp = kk == 0, last and k == g - 1
                        tk = ([w.tok] if m == 0 and k == 0 else []) + (bfree[b] if st else []) + list(toks)
                        if mode == "fm":
                            t = mm(PB[b][:, :], wv[:, k, m * 128:(m + 1) * 128], rhs_fn(kk), st, sp, *tk,
                                   inc=(k == g - 1))
                        else:
                            t = mm(PB[b][:, 0:width], rhs_fn(kk, m), wv[:, k, :], st, sp, *tk, inc=(k == g - 1))
                    if last:
                        evac(c, m, b, t)
                k0 += g
                give(w, P.now)

    def norm_stat(src, nk, T, sq, r, scale, *toks, mat=None, b=None):
        b = bank() if b is None else b
        m_ = ones if mat is None else mat
        pt = [None, None]
        for k in range(nk):
            w = [pt[k % 2]] if pt[k % 2] else []
            t = act(sq[k % 2][:, 0:T], src(k), ACT.Square, *w, *toks)
            pt[k % 2] = mm(PB[b][:, 0:T], m_, sq[k % 2][:, 0:T], k == 0, k == nk - 1, t,
                           *(bfree[b] if k == 0 else []), inc=True)
        t = vts(r, PB[b][:, 0:T], scale, EPS, ALU.mult, ALU.add, pt[(nk - 1) % 2], *toks)
        bfree[b] = [t]
        t = act(r, r, ACT.Sqrt, t)
        t = V.do(lambda e: e.reciprocal(r, r), t)
        return t

    def norm_apply(src, dst, nk, r, gain, shift, *toks):
        for k in range(nk):
            t = stt(dst(k), src(k), gain(k), r, ALU.mult, ALU.mult, *toks)
            if shift is not None:
                act(dst(k), dst(k), ACT.Identity, t, bias=shift(k))

    def hk(k):
        return H[:, k * 512:(k + 1) * 512]

    I = ins
    w_ada, w_in = I["w_ada"][0], I["w_in"][0]

    def plan_cols(w, kt, lo, n):
        plan([(0, wsrc(w, kt, lo, n))])

    for c in range(4):
        plan_cols(w_ada, 8, c * 512, 512)
    for lo, n in ((0, 512), (512, 512), (1024, 512), (1536, 32), (1568, 512)):
        plan_cols(w_in, 8, lo, n)
    for g in range(0, 4, 2):
        plan([(0, I["ptab"][g].rearrange("(j p) n -> p j n", p=128)),
              (2048, I["ptab"][g + 1].rearrange("(j p) n -> p j n", p=128))])
    for c in range(4, 12):
        plan_cols(w_ada, 8, c * 512, 512)
    for c in range(2):
        plan_cols(I["w_out"][0], 8, c * 512, 512)
    for e_ in range(32):
        for h in range(2):
            plan_cols(I["w_gu"][0, e_], 8, h * 512, 512)
            plan_cols(I["w_gu"][0, e_], 8, 1024 + h * 512, 512)
        for h in range(2):
            plan([(0, I["w_down"][0, e_, h * 512:(h + 1) * 512, :].rearrange("(j p) n -> p j n", p=128))])

    tk0 = load(A, "kc", KC[:, :], I["tabs"][:, 0:256])
    rows = a(0, 256)
    R1 = []
    at = 0

    def vec(name, src, n, half):
        nonlocal at
        R1.append((name, at, n, half))
        load(A, "rows", rows[at:at + n, half * 128:half * 128 + 128], src)
        at += n

    def r2(x, n):
        return x.rearrange("(j p) -> j p", p=128)

    vec("nmix", r2(I["norm_mix_w"][0], 8), 8, 0)
    vec("nmlp", r2(I["norm_mlp_w"][0], 8), 8, 0)
    vec("nfin", r2(I["final_norm_w"], 8), 8, 0)
    vec("glan", r2(I["gla_norm_w"][0], 1), 1, 0)
    vec("pscale", r2(I["pool_scale"][0], 4), 4, 0)
    vec("bgk", r2(I["b_gk_f"][0], 2), 2, 0)
    vec("bgk2", r2(I["b_gk_b"][0], 2), 2, 0)
    for l in range(2):
        vec(f"mix{l}", r2(I["norm_mix_2"][l], 8), 8, 0)
        vec(f"ffn{l}", r2(I["norm_ffn_2"][l], 8), 8, 0)
        vec(f"ple{l}", r2(I["norm_ple_2"][l], 8), 8, 0)
    vec("fin2", r2(I["final_norm_2"], 8), 8, 0)
    vec("subln", r2(I["diff_subln_2"][0], 1), 1, 0)
    vec("s5d", I["s5_d_2"][0].rearrange("(j g) c -> j (g c)", g=8), 4, 0)
    vec("c", r2(I["c"][0], 8), 8, 0)
    vec("cctx", r2(I["c_ctx"], 8), 8, 0)
    n0 = at
    at = 0
    vec("bada", r2(I["b_ada"][0], 48), 48, 1)
    tk_rows = (s_small["rows"], counts[s_small["rows"]])
    b = bank()
    tp(PB[b][:, 0:n0], rows[0:n0, 0:128], tk0, tk_rows)
    t = tp(PB[b][:, n0:n0 + 48], rows[0:48, 128:256], inc=True)
    t_cols = copy(V, COLS[:, 0:n0 + 48], PB[b][:, 0:n0 + 48], t)
    bfree[b] = [t_cols]
    col = {}
    for name, at_, n, half in R1:
        col[name] = (n0 if half else 0) + at_

    def C(name, k=0, n=1):
        return COLS[:, col[name] + k:col[name] + k + n]

    xt = a(256, 4096, 1024)
    ct = a(4352, 2048, 1024)
    HC = a(16640, 2048, 256)
    tx = load(A, "x", xt, I["x"][0].rearrange("(t p) d -> p t d", p=128))
    tc = load(A, "ctx", ct, I["ctx"][0].rearrange("(t p) d -> p t d", p=128))
    for k in range(8):
        b = bank()
        for t_ in range(4):
            t = tp(PB[b][:, t_ * 128:(t_ + 1) * 128], xt[:, t_, k * 128:(k + 1) * 128], tx, *bfree[b], inc=t_ == 3)
        q = A if k % 2 else V
        bfree[b] = [copy(q, hk(k), PB[b][:, :], t)]
    for k in range(8):
        b = bank()
        for t_ in range(2):
            t = tp(PB[b][:, t_ * 128:(t_ + 1) * 128], ct[:, t_, k * 128:(k + 1) * 128], tc, *bfree[b], inc=t_ == 1)
        q = A if k % 2 else V
        bfree[b] = [copy(q, HC[:, k, :], PB[b][:, 0:256], t)]
    barrier()

    cc = SM[:, 0:16].rearrange("p (k s) -> p k s", s=2)
    t = act(cc[:, :, 0], C("c", 0, 8), ACT.Silu, t_cols)
    t_cc = act(cc[:, :, 1], C("cctx", 0, 8), ACT.Silu)

    HN = a(10496, 6144, 768)
    sq = [a(18688, 512), a(19200, 512)]
    rx = a(19712, 512)
    rc = a(20224, 256)
    t_rx = norm_stat(hk, 8, 512, sq, rx, 1.0 / 1024)
    t_rc = norm_stat(lambda k: HC[:, k, :], 8, 256, sq, rc, 1.0 / 1024)

    modrow = a(0, 1024)
    mcol = MOD[:, :].rearrange("p (j s) -> p j s", s=2)
    tmod = [None, None]

    def ada(c, w):
        b = bank()
        wv = rv(w, 0, 8, 512)
        for k in range(8):
            t = mm(PB[b][0:2, :], cc[:, k, :], wv[:, k, :], k == 0, k == 7, w.tok, t_cc, *bfree[b], inc=k == 7)
        give(w, t)
        mr = modrow[0:2, (c % 2) * 512:(c % 2) * 512 + 512]
        t = copy(A, mr, PB[b][0:2, :], t, *([tmod[c % 2]] if tmod[c % 2] else []))
        bfree[b] = [t]
        b = bank()
        for j in range(4):
            t = tp(PB[b][:, 2 * j:2 * j + 2], mr[:, j * 128:(j + 1) * 128], t, *bfree[b], inc=j == 3)
        tmod[c % 2] = t
        t = V.do(lambda e: e.tensor_tensor(
            mcol[:, 4 * c:4 * c + 4, :], PB[b][:, 0:8].rearrange("p (j s) -> p j s", s=2),
            C("bada", 4 * c, 4).unsqueeze(2).to_broadcast([128, 4, 2]), ALU.add), t)
        bfree[b] = [t]

    for c in range(4):
        ada(c, take())

    def M(i, k, s=0):
        return mcol[:, i * 8 + k, s:s + 1]

    gm = SM[:, 32:64].rearrange("p (a k) -> p a k", k=8)
    for s in range(2):
        vts(gm[:, s, :], mcol[:, 8:16, s], 1.0, None, ALU.add, None)
        t_gm = vtt(gm[:, s, :], gm[:, s, :], C("nmix", 0, 8), ALU.mult)
    for k in range(8):
        t = stt(HN[:, k, 0:512], hk(k), gm[:, 0, k:k + 1], rx, ALU.mult, ALU.mult)
        act(HN[:, k, 0:512], HN[:, k, 0:512], ACT.Identity, t, bias=M(0, k, 0))
        t = stt(HN[:, k, 512:768], HC[:, k, :], gm[:, 1, k:k + 1], rc, ALU.mult, ALU.mult)
        act(HN[:, k, 512:768], HN[:, k, 512:768], ACT.Identity, t, bias=M(0, k, 1))
    t_hn = A.now

    tz = G.do(lambda e: e.memset(ZB[:, :], 0.0))
    t_zero = load(G, "zero", y_d[4096:NBLK * 128, :].rearrange("(b p) d -> p b d", p=128),
                  ZB[:, :].unsqueeze(1).to_broadcast([128, NBLK - 32, 1024]), tz)

    barrier()
    QX = a(0, 1024, 512)
    KX = a(1024, 1536, 768)
    GX = a(2560, 2048, 512)
    MX = a(2560, 4096, 512)
    PT = a(16640, 2048, 512)
    VT = a(6656, 3072, 512)
    RX = ar[0:32, 9728:10496]
    w = take()
    wv = rv(w, 0, 8, 512)
    for m in range(4):
        b = bank()
        for k in range(8):
            t = mm(PB[b][:, :], wv[:, k, m * 128:(m + 1) * 128], HN[:, k, 0:512], k == 0, k == 7, w.tok, *bfree[b],
                   inc=k == 7)
        dst = QX[:, m, :] if m < 2 else KX[:, m - 2, 0:512]
        bfree[b] = [copy(V if m % 2 else A, dst, PB[b][:, :], t)]
        if m >= 2:
            b = bank()
            for k in range(8):
                t = mm(PB[b][:, 0:256], wv[:, k, m * 128:(m + 1) * 128], HN[:, k, 512:768], k == 0, k == 7,
                       *bfree[b], inc=k == 7)
            bfree[b] = [copy(V, KX[:, m - 2, 512:768], PB[b][:, 0:256], t)]
    give(w, t)
    dense([512], lambda k, m: HN[:, k, m * 128:(m + 1) * 128], [8],
          lambda c, m, b, t: bfree.__setitem__(b, [copy(V if m % 2 else A, VT[:, m, :], PB[b][:, :], t)]),
          mode="tm", ntile=6)
    dense([512], lambda k: HN[:, k, 0:512], [8],
          lambda c, m, b, t: bfree.__setitem__(b, [act(GX[:, m, :], PB[b][:, :], ACT.Silu, t)]))
    w = take()
    wv = rv(w, 0, 8, 32)
    for lo, n in ((0, 512), (512, 256)):
        b = bank()
        for k in range(8):
            t = mm(PB[b][0:32, 0:n], wv[:, k, :], HN[:, k, lo:lo + n], k == 0, k == 7, w.tok, *bfree[b], inc=k == 7)
        bfree[b] = [copy(V, RX[:, lo:lo + n], PB[b][0:32, 0:n], t)]
    give(w, t)
    dense([512], lambda k, m: HN[:, k, m * 128:(m + 1) * 128], [8],
          lambda c, m, b, t: bfree.__setitem__(b, [copy(V if m % 2 else A, PT[:, m, :], PB[b][:, :], t)]),
          mode="tm", ntile=4)
    barrier()

    wp = a(18688, 512, 128)
    tw = load(A, "wpool", wp, I["w_pool"][0].rearrange("g c d -> c g d"))
    pl = [a(19200, 512), a(19712, 512)]
    for g in range(4):
        if g % 2 == 0:
            w = take()
        pv = rv(w, (g % 2) * 2048, 4, 512)
        b = bank()
        for j in range(4):
            t = mm(PB[b][:, :], PT[:, j, g * 128:(g + 1) * 128], pv[:, j, :], j == 0, j == 3, w.tok, *bfree[b],
                   inc=j == 3)
        if g % 2 == 1:
            give(w, t)
        t = copy(A, pl[g % 2], PB[b][:, :], t)
        bfree[b] = [t]
        b = bank()
        t = mm(PB[b][:, :], wp[:, g, :], pl[g % 2], True, True, t, tw, *bfree[b], inc=True)
        bfree[b] = [vts(MX[:, 4 + g, :], PB[b][:, :], C("pscale", g), None, ALU.mult, None, t)]
    barrier()

    BC = a(10496, 3072, 768)
    E1 = a(13568, 3072, 768)
    wg = ar[0:32, 16640:17152]
    tz = V.do(lambda e: e.memset(wg, 0.0))
    load(A, "wgk", wg[0:16, 0:256], I["w_gk_f"][0], tz)
    tg = load(A, "wgk", wg[16:32, 256:512], I["w_gk_b"][0])
    smask = a(17152, 768)
    tsm = load(A, "scan", smask, I["tabs"][:, TOFF["scan"][0]:TOFF["scan"][0] + 768])
    for c4 in range(4):
        for lo, n in ((0, 512), (512, 256)):
            b = bank()
            t = mm(PB[b][:, 0:n], wg[:, c4 * 128:(c4 + 1) * 128], RX[:, lo:lo + n], True, True, tg, *bfree[b], inc=True)
            t = vts(BC[:, c4, lo:lo + n], PB[b][:, 0:n], C("bgk", c4), None, ALU.add, None, t)
            bfree[b] = [t]
            act(E1[:, c4, lo:lo + n], BC[:, c4, lo:lo + n], ACT.Abs, t)
    f1, fb = a(13568, 3072), a(10496, 3072)
    act(f1, f1, ACT.Exp, scale=-1.0)
    t = act(f1, f1, ACT.Ln, bias=1.0)
    t = stt(fb, fb, 0.0, f1, ALU.min, ALU.subtract, t)
    for c4 in range(4):
        src = BC[:, c4, :]
        dst = E1[:, c4, :]
        if c4 >= 2:
            src, dst = src[:, ::-1], dst[:, ::-1]
        V.do(lambda e, s=src, d=dst: e.tensor_tensor_scan(d, smask, s, 0.0, ALU.mult, ALU.add), tsm)
    BC = E1
    barrier()

    AB = [a(10496, 512), a(11008, 512)]
    mk = a(11520, 1024, 512)
    tm1 = load(A, "mask", mk[:, 0, :], I["tabs"][:, TOFF["maskf"][0]:TOFF["maskf"][0] + 512])
    tm1 = load(A, "mask", mk[:, 1, :], I["tabs"][:, TOFF["maskb"][0]:TOFF["maskb"][0] + 512])
    dec = a(12544, 12)
    X0 = 16640
    KU = a(X0, 768)
    KUT = a(X0 + 768, 768, 128)
    ST = a(X0 + 1536, 2048, 256)
    QM, KM, QB = a(X0 + 3584, 512), a(X0 + 4096, 512), a(X0 + 4608, 512)
    ro = a(X0 + 5120, 512)
    sqo = [a(12576, 512), a(12576, 512)]
    kt3 = KU.rearrange("p (n c) -> p n c", c=64)
    for ht in range(2):
        OB = [bank(), bank()]
        held = tuple(OB)
        for d in range(2):
            barrier()
            cb = d * 2 + ht
            B3 = BC[:, cb, :].rearrange("p (n c) -> p n c", c=64)
            il, im = (63, 31) if d == 0 else (0, 32)
            t = V.do(lambda e, B3=B3, il=il: e.tensor_tensor(
                kt3, B3[:, :, il:il + 1].to_broadcast([128, 12, 64]), B3, ALU.subtract))
            t1 = act(KU, KU, ACT.Exp, t, scale=1.0 / 16)
            act(dec, B3[:, :, il], ACT.Exp, scale=1.0 / 16)
            t = V.do(lambda e, B3=B3, im=im: e.tensor_tensor(
                QM.rearrange("p (n c) -> p n c", c=64), B3[:, 0:8, :],
                B3[:, 0:8, im:im + 1].to_broadcast([128, 8, 64]), ALU.subtract))
            t2 = act(KM, QM, ACT.Exp, t, scale=-1.0 / 16)
            t3 = act(QM, QM, ACT.Exp, scale=1.0 / 16)
            t4 = act(QB, BC[:, cb, 0:512], ACT.Exp, scale=1.0 / 16)
            tku = vtt(KU, KU, KX[:, ht, :], ALU.mult, t1)
            tkm = vtt(KM, KM, KX[:, ht, 0:512], ALU.mult, t2)
            tqm = stt(QM, QM, 0.125, QX[:, ht, :], ALU.mult, ALU.mult, t3)
            tqb = stt(QB, QB, 0.125, QX[:, ht, :], ALU.mult, ALU.mult, t4)
            for j0, nj in ((0, 4), (4, 2)):
                b = bank(held)
                for j in range(nj):
                    t = tp(PB[b][:, j * 128:(j + 1) * 128], KU[:, (j0 + j) * 128:(j0 + j + 1) * 128], tku, *bfree[b],
                           inc=j == nj - 1)
                t = copy(A, KUT[:, j0:j0 + nj, :], PB[b][:, 0:nj * 128].rearrange("p (j c) -> p j c", c=128), t)
                bfree[b] = [t]
            tkt = A.now
            for hl in range(2):
                b = bank(held)
                ps = slice(hl * 64, hl * 64 + 64)
                for j in range(4):
                    js = slice(j * 128, (j + 1) * 128)
                    t = mm(PB[b][:, js], KM[ps, js], QM[ps, js], j == 0, j == 3, tqm, tkm, *bfree[b], inc=j == 3)
                tz = G.do(lambda e, x=AB[hl]: e.memset(x, 0.0))
                t = V.do(lambda e, x=AB[hl], m_=mk[:, d, :], y=PB[b][:, :]: e.copy_predicated(
                    x, m_.bitcast(U32), y), t, tz, tm1)
                bfree[b] = [t]
                for j in range(4):
                    js = slice(j * 128, (j + 1) * 128)
                    h4 = 2 * ht + hl
                    mm(PB[OB[hl]][:, js], VT[:, j, h4 * 128:(h4 + 1) * 128], AB[hl][:, js],
                       d == 0 and j == 0, False, t, *bfree[OB[hl]])
            order = [8, 9, 10, 11] + list(range(0, 7)) if d == 0 else [11, 10, 9, 8] + list(range(7, 0, -1))
            cur = None
            lastslot = 7 if d == 0 else 0
            for i, n in enumerate(order):
                if i % 4 == 0:
                    ub = [bank(held), bank(held)]
                    for i2 in range(i, min(i + 4, len(order))):
                        n2 = order[i2]
                        hh = slice((n2 % 2) * 64, (n2 % 2) * 64 + 64)
                        b = ub[i2 % 2]
                        q2 = (i2 % 4) // 2
                        mm(PB[b][:, q2 * 256:q2 * 256 + 256], KUT[hh, n2 // 2, :],
                           VT[hh, n2 // 2, ht * 256:(ht + 1) * 256], q2 == 0, True, tkt, *bfree[b], inc=True)
                    tu = P.now
                b = ub[i % 2]
                pu = PB[b][:, ((i % 4) // 2) * 256:((i % 4) // 2) * 256 + 256]
                nxt = lastslot if i < 3 else ((i - 3) if d == 0 else 7 - (i - 3))
                if i == 0:
                    t = copy(V, ST[:, nxt, :], pu, tu)
                else:
                    t = stt(ST[:, nxt, :], ST[:, cur, :], dec[:, n:n + 1], pu, ALU.mult, ALU.add, tu)
                bfree[b] = [t]
                cur = nxt
            ts = V.now
            for hl in range(2):
                ps = slice(hl * 64, hl * 64 + 64)
                for n in range(8):
                    ns = slice(n * 64, (n + 1) * 64)
                    t = mm(PB[OB[hl]][:, ns], ST[ps, n, hl * 128:(hl + 1) * 128], QB[ps, ns], False,
                           d == 1 and n == 7, ts, tqb, inc=n == 7)
        barrier()
        for hl in range(2):
            h4 = 2 * ht + hl
            ob = PB[OB[hl]][:, :]
            t = norm_stat(lambda k: ob, 1, 512, sqo, ro, 1.0 / 128, b=bank(held))
            t = vtt(ro, ob, ro, ALU.mult, t)
            bfree[OB[hl]] = [t]
            stt(GX[:, h4, :], ro, C("glan"), GX[:, h4, :], ALU.mult, ALU.mult)
    barrier()
    for c in range(4, 12):
        ada(c, take())

    def resid(gcol, n0_=0):
        def f(c, m, b, t):
            kk = c * 4 + m
            if gcol is None:
                t = vtt(hk(kk), PB[b][:, :], hk(kk), ALU.add, t)
            else:
                t = stt(hk(kk), PB[b][:, :], gcol(kk), hk(kk), ALU.mult, ALU.add, t)
            bfree[b] = [t]
        return f

    barrier()
    dense([512, 512], lambda k: MX[:, k, :], [8], resid(lambda k: M(2, k)))
    barrier()

    def store_out(src):
        toks = []
        for t_ in range(4):
            ob_ = a(16384 + (t_ % 2) * 1024, 1024)
            for h in range(2):
                b = bank()
                for k in range(4):
                    t = tp(PB[b][:, k * 128:(k + 1) * 128], src(4 * h + k)[:, t_ * 128:(t_ + 1) * 128], V.now, A.now,
                           *bfree[b], inc=k == 3)
                prev = [toks[t_ - 2]] if t_ >= 2 else []
                bfree[b] = [copy(A if h else V, ob_[:, h * 512:(h + 1) * 512], PB[b][:, :], t, *prev)]
            toks.append(S.dma(s_out[t_ % 2], counts, lambda e, o=ob_, t_=t_: e.dma_start(
                out[0, t_ * 128:(t_ + 1) * 128, :], o), V.now, A.now))
        S.wait(*toks)

    s_out = [sem("s_out0"), sem("s_out1")]

    def emit_all():
        with nc.Block() as block:
            @block.sync
            def _(eng):
                S.emit(eng)

            @block.tensor
            def _(eng):
                P.emit(eng)

            @block.vector
            def _(eng):
                V.emit(eng)

            @block.scalar
            def _(eng):
                A.emit(eng)

            @block.gpsimd
            def _(eng):
                G.emit(eng)

    def tab2(name, at):
        o, n = TOFF[name]
        v = a(at, n)
        return v, load(A, "u_" + name, v, I["tabs"][:, o:o + n])

    def tab(name, at, *toks, q=None):
        o, n = TOFF[name]
        v = a(at, n)
        return v, load(q or A, "t_" + name, v, I["tabs"][:, o:o + n], *toks)


    HM = a(0, 4096, 512)
    gm2 = SM[:, 64:72]
    vts(gm2, mcol[:, 32:40, 0], 1.0, None, ALU.add, None)
    vtt(gm2, gm2, C("nmlp", 0, 8), ALU.mult)
    rr = a(4608, 512)
    t = norm_stat(hk, 8, 512, [a(5120, 512), a(5632, 512)], rr, 1.0 / 1024)
    norm_apply(hk, lambda k: HM[:, k, :], 8, rr, lambda k: gm2[:, k:k + 1], lambda k: M(3, k), t)
    xs = [a(6144, 1024), a(7168, 1024)]
    s_hm = sem("s_hm")
    s_hm2 = sem("s_hm2")
    th = []
    for t_ in range(4):
        for h in range(2):
            b = bank()
            for k in range(4):
                t = tp(PB[b][:, k * 128:(k + 1) * 128], HM[:, 4 * h + k, t_ * 128:(t_ + 1) * 128], V.now, A.now,
                       *bfree[b], inc=k == 3)
            prev = [th[t_ - 2]] if t_ >= 2 else []
            bfree[b] = [copy(A if h else V, xs[t_ % 2][:, h * 512:(h + 1) * 512], PB[b][:, :], t, *prev)]
        th.append(A.dma([s_hm, s_hm2][t_ % 2], counts, lambda e, t_=t_: e.dma_start(
            hm_d[t_ * 128:(t_ + 1) * 128, :], xs[t_ % 2]), V.now, A.now))

    wr = a(4096, 256, 32)
    br = ar[0:1, 4352:4384]
    load(A, "router", wr, I["w_router"][0].rearrange("(j p) n -> p j n", p=128), P.now)
    twr = load(A, "router", br, I["b_router"])
    tri, t1 = tab("tri", 8192)
    iota, t2 = tab("iota", 8320)
    tokc, t3 = tab("tok", 8448)
    pmod, t4 = tab("pmod", 8452)
    selc, t5 = tab("sel", 8460)
    ttab = [t1, t2, t3, t4, t5]
    bl = bank()
    LGp = PB[bl][:, 0:128].rearrange("p (t e) -> p t e", e=32)
    for t_ in range(4):
        mm(LGp[:, t_, :], ones[0:1, :], br, t_ == 0, False, twr, *bfree[bl])
        for k in range(8):
            t = mm(LGp[:, t_, :], HM[:, k, t_ * 128:(t_ + 1) * 128], wr[:, k, :], False, k == 7, A.now, inc=k == 7)
    o = 8500
    LG = a(o, 128, 32)
    MXV = a(o + 128, 32, 8)
    MXI = a(o + 160, 32, 8).bitcast(U32)
    IDF = a(o + 192, 32, 8)
    ID4 = a(o + 224, 16, 4)
    SEL = a(o + 240, 128, 32)
    RK = a(o + 368, 128, 32)
    RBK = a(o + 496, 128, 32)
    OFF = a(o + 624, 128, 32)
    BLK = a(o + 752, 128, 32)
    CNT = a(o + 880, 32)
    NX = a(o + 912, 32)
    XI = a(o + 944, 32)
    T1 = a(o + 976, 128, 32)
    OH = a(o + 1104, 512)
    T2 = a(o + 1616, 512)
    T3 = a(o + 2128, 512)
    BK4 = a(o + 2640, 16)
    OF4 = a(o + 2656, 16)
    XE = a(o + 2672, 16)
    SS = a(o + 2688, 4)
    LH = [a(o + 2700, 128), a(o + 2828, 128)]
    RH = [a(o + 2956, NBLK), a(o + 3004, NBLK)]
    DF = a(o + 3056, 16)
    K0 = 20000
    IDXI = a(K0, NBLK).bitcast(I32)
    DEST = a(K0 + 48, 16).bitcast(I32)
    WTS = a(K0 + 64, 16)
    SI = a(K0 + 80, 32).bitcast(I32)
    IDC = a(K0 + 112, 1).bitcast(I32)
    SELB = a(K0 + 120, 16).bitcast(BF16)
    SELX = a(K0 + 136, 8).bitcast(BF16)
    SELJ = a(K0 + 144, 64).bitcast(BF16)
    BP = a(K0 + 240, 1536).bitcast(BF16)
    t = copy(V, LG, LGp, t)
    bfree[bl] = [t]
    for t_ in range(4):
        V.do(lambda e, t_=t_: e.max(MXV[:, t_, :], LG[:, t_, :]))
        V.do(lambda e, t_=t_: e.max_index(MXI[:, t_, :], MXV[:, t_, :], LG[:, t_, :]))
    copy(V, IDF, MXI)
    copy(V, ID4, IDF[:, :, 0:4])
    W4 = WTS.rearrange("p (t k) -> p t k", k=4)
    t = vtt(W4, MXV[:, :, 0:4], MXV[:, :, 0:1].to_broadcast([128, 4, 4]), ALU.subtract)
    t = act(WTS, WTS, ACT.Exp, t)
    V.do(lambda e: e.tensor_reduce(SS, W4, AX.X, ALU.add), t)
    V.do(lambda e: e.reciprocal(SS, SS))
    vtt(W4, W4, SS.unsqueeze(2).to_broadcast([128, 4, 4]), ALU.mult)
    OH3 = OH.rearrange("p (i e) -> p i e", e=32)
    vtt(OH3, iota[:, 0:32].unsqueeze(1).to_broadcast([128, 16, 32]),
        a(o + 224, 16).unsqueeze(2).to_broadcast([128, 16, 32]), ALU.is_equal, *ttab)
    t = V.do(lambda e: e.tensor_reduce(SEL, OH.rearrange("p (t k e) -> p t e k", k=4, e=32), AX.X, ALU.add))
    b = bank()
    for t_ in range(4):
        mm(PB[b][:, t_ * 32:(t_ + 1) * 32], tri, SEL[:, t_, :], t_ == 0, t_ == 0, t, *bfree[b])
        for u_ in range(t_):
            mm(PB[b][:, t_ * 32:(t_ + 1) * 32], ones, SEL[:, u_, :], False, u_ == t_ - 1)
    for u_ in range(4):
        t = mm(PB[b][:, 128:160], ones, SEL[:, u_, :], False, u_ == 3, inc=u_ == 3)
    RKf, RBf, OFf, BKf, T1f = (a(o + 368, 128), a(o + 496, 128), a(o + 624, 128), a(o + 752, 128), a(o + 976, 128))
    copy(V, RKf, PB[b][:, 0:128], t)
    bfree[b] = [copy(V, CNT, PB[b][:, 128:160])]
    vts(NX, CNT, 128.5, None, ALU.is_gt, None)
    for lim in (256.5, 384.5):
        stt(NX, CNT, lim, NX, ALU.is_gt, ALU.add)
    V.do(lambda e: e.tensor_tensor_scan(XI, ones[:, 0:32], NX, 0.0, ALU.mult, ALU.add))
    vts(RBf, RKf, 127.5, None, ALU.is_gt, None)
    for lim in (255.5, 383.5):
        stt(RBf, RKf, lim, RBf, ALU.is_gt, ALU.add)
    stt(OFf, RBf, -128.0, RKf, ALU.mult, ALU.add)
    vtt(NX, XI, NX, ALU.subtract)
    vtt(NX, NX, iota[:, 0:32], ALU.subtract)
    vts(NX, NX, 31.0, None, ALU.add, None)
    vts(T1f, RBf, 0.5, None, ALU.is_gt, None)
    vtt(T1, T1, NX.unsqueeze(1).to_broadcast([128, 4, 32]), ALU.mult)
    vtt(T1f, T1f, RBf, ALU.add)
    vtt(BLK, T1, iota[:, 0:32].unsqueeze(1).to_broadcast([128, 4, 32]), ALU.add)
    OH4 = OH.rearrange("p (t k e) -> p t k e", k=4, e=32)
    for src, tmp, res in ((BLK, T2, BK4), (OFF, T3, OF4)):
        vtt(tmp.rearrange("p (t k e) -> p t k e", k=4, e=32), OH4,
            src.unsqueeze(2).to_broadcast([128, 4, 4, 32]), ALU.mult)
        V.do(lambda e, tmp=tmp, res=res: e.tensor_reduce(res, tmp.rearrange("p (i e) -> p i e", e=32), AX.X, ALU.add))
    stt(DF, BK4, 128.0, OF4, ALU.mult, ALU.add)
    copy(V, DEST, DF)
    t = vtt(T2.rearrange("p (j e) -> p j e", e=32), iota[:, 0:16].unsqueeze(2).to_broadcast([128, 16, 32]),
            XI.unsqueeze(1).to_broadcast([128, 16, 32]), ALU.is_ge)
    V.do(lambda e: e.tensor_reduce(XE, T2.rearrange("p (j e) -> p j e", e=32), AX.X, ALU.add))
    vts(XE, XE, 31.0, None, ALU.min, None)
    copy(V, SI[:, 0:16], XE)
    t_si = copy(V, SI[:, 16:17], XI[:, 31:32])
    copy(V, SELB, selc)
    vts(SELX, XE, pmod[:, 0:1], None, ALU.is_equal, None)
    b = bank()
    tp_ = [None, None]
    for i in range(16):
        w_ = [tp_[i % 2]] if tp_[i % 2] else []
        vts(LH[i % 2], iota, OF4[:, i:i + 1], None, ALU.is_equal, None, *w_)
        t = vts(RH[i % 2], iota[:, 0:NBLK], BK4[:, i:i + 1], tokc[:, i // 4:i // 4 + 1], ALU.is_equal, ALU.mult)
        tp_[i % 2] = mm(PB[b][:, 0:NBLK], LH[i % 2], RH[i % 2], i == 0, i == 15, t, *bfree[b], inc=True)
    t_idx = copy(V, IDXI, PB[b][:, 0:NBLK], tp_[1])
    bfree[b] = [t_idx]
    raw = ar[0:96, 12000:15072]
    part = ar[0:96, 15072:16608].bitcast(BF16)
    for j in range(3):
        load(A, "bias", raw[32 * j:32 * j + 32, 0:2048], I["b_gu"][0])
        tb = load(A, "bias", raw[32 * j:32 * j + 32, 2048:3072], I["b_down"][0])
    G.wait(tb)
    for j in range(3):
        copy(G, part, raw)
        copy(G, BP[32 * j:32 * j + 32, :], part[32 * j:32 * j + 32, :])
        if j < 2:
            vtt(raw, raw, part, ALU.subtract, q=G)
    barrier()

    XG = [a(0, 1024), a(1024, 1024)]
    XT = [a(2048, 1024, 128), a(3072, 1024, 128)]
    GT = [a(4096, 512), a(4608, 512)]
    UT = [a(5120, 512), a(5632, 512)]
    ZT = [a(6144, 512), a(6656, 512)]
    AC = [a(7168, 512), a(7680, 512)]
    AT = [a(8192, 512, 128), a(8704, 512, 128)]
    YB = [a(9216, 1024), a(10240, 1024)]
    s_g = [sem("s_g0"), sem("s_g1")]
    s_y = [sem("s_y0"), sem("s_y1")]

    class Block:

        def __init__(self, v, ac, p):
            self.V, self.A, self.P = v, ac, p
            self.bf = [[] for _ in range(8)]

        def xturn(self, i, tg_):
            for h in range(2):
                for k in range(4):
                    kk = 4 * h + k
                    t = self.P.do(lambda e, h=h, k=k, kk=kk: e.transpose(
                        PB[h][:, k * 128:(k + 1) * 128], XG[i][:, kk * 128:(kk + 1) * 128], ident),
                        tg_, *self.bf[h], inc=k == 3)
                q = self.A if h else self.V
                dst = XT[i][:, 4 * h:4 * h + 4, :].rearrange("p k c -> p (k c)")
                if h:
                    t = q.do(lambda e, dst=dst: e.activation(dst, PB[1][:, :], ACT.Copy), t, self.P.now)
                else:
                    t = q.do(lambda e, dst=dst: e.tensor_copy(dst, PB[0][:, :]), t, self.P.now)
                self.bf[h] = [t]
            return [self.bf[0][0], self.bf[1][0]]

        def mmb(self, b, lhsT, rhs, st, sp, *toks, inc=False):
            return self.P.do(lambda e: e.matmul(PB[b][:, :], lhsT, rhs, start=st, stop=sp, skip_group_check=True),
                             *toks, inc=inc)

        def run(self, i, txt, views, toks, gave, bias_lhs, tbias, mid, prev_store):
            V_, A_, P_ = self.V, self.A, self.P
            done = [None, None]
            for h in range(2):
                for g in range(2):
                    n = 2 * h + g
                    b = 2 + n
                    c0 = g * 1024 + h * 512
                    self.mmb(b, bias_lhs, BP[0:96, c0:c0 + 512], True, False, tbias, *self.bf[b])
                    for k in range(8):
                        t = self.mmb(b, XT[i][:, k, :], views[n][:, k, :], False, k == 7, toks[n], *txt, inc=k == 7)
                    gave(n, t)
                    if g == 0:
                        tg = V_.do(lambda e, h=h, b=b: e.tensor_scalar(GT[h], PB[b][:, :], 7.0, None, ALU.min), t)
                        self.bf[b] = [tg]
                        tz = A_.do(lambda e, h=h: e.activation(ZT[h], GT[h], ACT.Sigmoid, scale=1.702), tg)
                    else:
                        tu = V_.do(lambda e, h=h, b=b: e.tensor_scalar(UT[h], PB[b][:, :], 7.0, -7.0, ALU.min, ALU.max), t)
                        self.bf[b] = [tu]
                        V_.do(lambda e, h=h: e.scalar_tensor_tensor(
                            out=UT[h], in0=UT[h], scalar=1.0, in1=GT[h], op0=ALU.add, op1=ALU.mult))
                        done[h] = V_.do(lambda e, h=h: e.tensor_tensor(AC[h], UT[h], ZT[h], ALU.mult), tz, P_.now)
            for h in range(2):
                for k in range(4):
                    t = P_.do(lambda e, h=h, k=k: e.transpose(
                        PB[h][:, k * 128:(k + 1) * 128], AC[h][:, k * 128:(k + 1) * 128], ident),
                        done[h], *self.bf[h], inc=k == 3)
                dst = AT[h].rearrange("p k c -> p (k c)")
                ta = A_.do(lambda e, h=h, dst=dst: e.activation(dst, PB[h][:, :], ACT.Copy), t)
                self.bf[h] = [ta]
                if h == 0:
                    mid()
                for n in range(2):
                    if h == 0:
                        self.mmb(6 + n, bias_lhs, BP[0:96, 2048 + n * 512:2560 + n * 512], True, False,
                                 *self.bf[6 + n])
                    for k in range(4):
                        t = self.mmb(6 + n, AT[h][:, k, :], views[4 + h][:, k, n * 512:(n + 1) * 512], False,
                                     h == 1 and k == 3, ta, toks[4 + h], inc=k == 3)
                    if h == 1:
                        dst = YB[i][:, n * 512:(n + 1) * 512]
                        if n:
                            t2 = A_.do(lambda e, dst=dst: e.activation(dst, PB[7][:, :], ACT.Copy), t, *prev_store)
                        else:
                            t2 = V_.do(lambda e, dst=dst: e.tensor_copy(dst, PB[6][:, :]), t, *prev_store)
                        self.bf[6 + n] = [t2]
                gave(4 + h, t)
            return [self.bf[6][0], self.bf[7][0]]

    def gather(q, cnt, i, idx, *toks):
        return q.dma(s_g[i], cnt, lambda e: e.indirect_dma_start(
            out=XG[i], out_offset=None, in_=hm_d, in_offset=bass.IndirectOffsetOnAxis(ap=idx, axis=0)), *toks)

    stream = Block(V, A, P)
    tgs = [gather(G, counts, 0, IDXI[:, 0:1], *th[2:]), gather(G, counts, 1, IDXI[:, 1:2])]
    txt = stream.xturn(0, tgs[0])
    tstore = [[], []]
    for e_ in range(32):
        i = e_ % 2
        ws = []
        for n in range(6):
            ws.append(None)

        class Views:
            def __init__(self):
                self.w = [None] * 6

            def get(self, n):
                if self.w[n] is None:
                    self.w[n] = take()
                return self.w[n]

        vw = Views()

        class LazyV:
            def __getitem__(self, n, vw=vw):
                w = vw.get(n)
                return rv(w, 0, 8, 512) if n < 4 else rv(w, 0, 4, 1024)

        class LazyT:
            def __getitem__(self, n, vw=vw):
                return vw.get(n).tok

        nxt = [None]

        def mid():
            if e_ + 1 < 32:
                nxt[0] = stream.xturn(1 - i, tgs[1 - i])
                if e_ + 2 < 32:
                    tgs[i] = gather(G, counts, i, IDXI[:, e_ + 2:e_ + 3], P.now)

        ty = stream.run(i, txt, LazyV(), LazyT(), lambda n, t, vw=vw: give(vw.get(n), t),
                        SELB[0:96, e_:e_ + 1].to_broadcast([96, 128]), A.now, mid, tstore[i])
        tstore[i] = [A.dma(s_y[i], counts, lambda e, e_=e_, i=i: e.dma_start(
            y_d[e_ * 128:(e_ + 1) * 128, :], YB[i]), *ty)]
        txt = nxt[0]
    for b in range(8):
        bfree[b] = stream.bf[b]
    A.wait(*tstore[0], *tstore[1])
    for q in (S, V, G, P):
        q.wait(*tstore[0], *tstore[1])
    barrier()
    S.wait(*[q.now for q in QS])

    for q in (S, G):
        q.wait(t_zero)
    L = {n: Queue(sem("s_l" + n), n in "vag") for n in "vagps"}
    lc = {}
    s_lw = [sem(f"s_lw{n}") for n in range(6)]
    s_lg, s_lst = sem("s_lgather"), sem("s_lst")
    regs = {}
    wgu = I["w_gu"][0]
    wdn = I["w_down"][0]
    lv = []
    ltok = []
    for n in range(6):
        if n < 4:
            v_ = ring[:, n * SLOT:(n + 1) * SLOT].rearrange("p (a b) -> p a b", b=512)
            c0 = (n % 2) * 1024 + (n // 2) * 512

            def f(e, v_=v_, c0=c0):
                return e.dma_start(v_, wgu[bass.ds(regs["e"], 1), :, c0:c0 + 512].rearrange(
                    "o (j p) n -> p (o j) n", p=128))
        else:
            v_ = ring[:, n * SLOT:(n + 1) * SLOT].rearrange("p (a b) -> p a b", b=1024)
            r0 = (n - 4) * 512

            def f(e, v_=v_, r0=r0):
                return e.dma_start(v_, wdn[bass.ds(regs["e"], 1), r0:r0 + 512, :].rearrange(
                    "o (j p) n -> p (o j) n", p=128))
        lv.append(v_)
        ltok.append(L["s"].dma(s_lw[n], lc, f))
    tic = L["g"].do(lambda e: e.tensor_copy(IDC, IDXI[:, bass.ds(regs["g"] + 32, 1)]))
    tlg = L["g"].dma(s_lg, lc, lambda e: e.indirect_dma_start(
        out=XG[0], out_offset=None, in_=hm_d, in_offset=bass.IndirectOffsetOnAxis(ap=IDC, axis=0)), tic)
    tsel = L["v"].do(lambda e: e.tensor_copy(SELJ[0:96, :], SELX[0:96, bass.ds(regs["v"], 1)].to_broadcast([96, 128])))
    extra = Block(L["v"], L["a"], L["p"])
    tx_ = extra.xturn(0, tlg)
    ty = extra.run(0, tx_, lv, ltok, lambda n, t: None, SELJ[0:96, :], tsel, lambda: None, [])
    y3 = y_d.rearrange("(b p) d -> b p d", p=128)
    L["s"].dma(s_lst, lc, lambda e: e.dma_start(
        y3[bass.ds(regs["s"] + 32, 1), :, :].rearrange("o p d -> p (o d)"), YB[0]), *ty)
    per = dict(lc)
    for q in L.values():
        if q.n:
            per[q.sem] = q.n
    for q in L.values():
        for s_, n in per.items():
            q.ops.append((0, s_, n))

    s_dum = {key: sem("s_after_" + key) for key in "vagps"}

    def looped(key):
        def f(e):
            n_ = e.value_load(SI[0:1, 16:17], min_val=0, max_val=15)
            with e.If(n_ > 0):
                with e.Fori(0, n_) as j:
                    regs[key] = j
                    if key == "s":
                        regs["e"] = e.value_load(SI[0:1, bass.ds(j, 1)], min_val=0, max_val=31)
                    L[key].emit(e, lambda s_, v_: j * per[s_] + v_, s_dum[key])
        return f

    for q, key in ((S, "s"), (V, "v"), (A, "a"), (G, "g"), (P, "p")):
        q.ops.append((3, looped(key), None))

    RW = [a(0, 1024), a(1024, 1024), a(2048, 1024), a(3072, 1024)]
    YA = [a(4096, 1024), a(5120, 1024)]
    s_rw = [sem(f"s_rw{k}") for k in range(4)]
    rfree = [[], [], [], []]
    yfree = [[], []]
    for t_ in range(4):
        ya = YA[t_ % 2]
        for k in range(4):
            i = t_ * 4 + k
            tg = G.dma(s_rw[k], counts, lambda e, i=i, k=k: e.indirect_dma_start(
                out=RW[k], out_offset=None, in_=y_d,
                in_offset=bass.IndirectOffsetOnAxis(ap=DEST[:, i:i + 1], axis=0)), *rfree[k])
            if k == 0:
                t = vts(ya, RW[k], WTS[:, i:i + 1], None, ALU.mult, None, tg, *yfree[t_ % 2])
            else:
                t = stt(ya, RW[k], WTS[:, i:i + 1], ya, ALU.mult, ALU.add, tg)
            rfree[k] = [t]
        for h in range(2):
            b = bank()
            for k in range(4):
                kk = 4 * h + k
                tt_ = tp(PB[b][:, k * 128:(k + 1) * 128], ya[:, kk * 128:(kk + 1) * 128], t, *bfree[b], inc=k == 3)
            for k in range(4):
                kk = 4 * h + k
                hs = hk(kk)[:, t_ * 128:(t_ + 1) * 128]
                t3 = stt(hs, PB[b][:, k * 128:(k + 1) * 128], M(5, kk), hs, ALU.mult, ALU.add, tt_)
            bfree[b] = [t3]
        yfree[t_ % 2] = [P.now]
    barrier()


    l_in, l_out = I["ret_s5_w_in_2"][0], I["ret_s5_w_out_2"][0]
    for c in range(5):
        plan_cols(l_in, 8, c * 512, 512)
    plan_cols(I["s5_w_glu_2"][0], 4, 0, 512)
    HCH = [512] * 5 + [256]

    def plan_ffn(l):
        for c, n in enumerate(HCH):
            plan_cols(I["ffn_w_gate_2"][l], 8, c * 512, n)
            plan_cols(I["ffn_w_up_2"][l], 8, c * 512, n)
        for c in range(2):
            for r0, g in ((0, 8), (8, 8), (16, 6)):
                plan([(0, wsrc(I["ffn_w_down_2"][l][r0 * 128:(r0 + g) * 128, :], g, c * 512, 512))])

    def plan_ple(l):
        for c in range(2):
            plan_cols(I["ple_w_gate_2"][l], 8, c * 512, 512)
        plan_cols(I["ple_w_proj_2"][l], 2, 0, 1024)

    for c in range(2):
        plan_cols(l_out, 8, c * 512, 512)
    plan_ffn(0)
    plan_ple(0)
    for c in range(6):
        plan_cols(I["diff_w_qkv_2"][0], 8, c * 512, 512)
    for c in range(2):
        plan_cols(I["diff_w_o_2"][0], 8, c * 512, 512)
    plan_ffn(1)
    plan_ple(1)

    def norm(gain, dst, src=None):
        src = src or hk
        t = norm_stat(src, 8, 512, [a(21504, 512), a(22016, 512)], a(20992, 512), 1.0 / 1024, V.now)
        norm_apply(src, dst, 8, a(20992, 512), gain, None, t)

    norm(lambda k: C("nfin", k), hk)
    HN = a(0, 4096, 512)
    hn = lambda k: HN[:, k, :]

    def ev(dst, f=None, dve=None):
        def g(c, m, b, t):
            if f is not None:
                bfree[b] = [act(dst(c, m), PB[b][:, 0:dst(c, m).shape[-1]], f, t)]
            else:
                bfree[b] = [copy(V if m % 2 else A, dst(c, m), PB[b][:, 0:dst(c, m).shape[-1]], t)]
        return g

    norm(lambda k: C("mix0", k), hn)
    barrier()
    Q3 = a(4096, 2048, 512)
    K3 = a(6144, 2048, 512)
    V3 = a(8192, 2048, 512)
    G3 = a(10240, 2048, 512)
    MX = a(10240, 4096, 512)
    U3 = a(14336, 2048, 512)
    dense([512], hn, [8], ev(lambda c, m: Q3[:, m, :]))
    dense([512], hn, [8], ev(lambda c, m: K3[:, m, :]))
    dense([512], lambda k, m: HN[:, k, m * 128:(m + 1) * 128], [8], ev(lambda c, m: V3[:, m, :]), mode="tm")
    dense([512], hn, [8], ev(lambda c, m: G3[:, m, :], ACT.Silu))
    dense([512], hn, [8], ev(lambda c, m: U3[:, m, :]))
    barrier()

    def rotary(tiles, cos, sin, rot, tmp, *toks):
        for x in tiles:
            b = bank()
            t = mm(PB[b][:, :], rot, x, True, True, V.now, A.now, *toks, *bfree[b], inc=True)
            t = vtt(tmp, PB[b][:, :], sin, ALU.mult, t, *toks)
            bfree[b] = [t]
            vtt(x, x, cos, ALU.mult, t)
            vtt(x, x, tmp, ALU.add)

    cosT, t1 = tab("cos", 0)
    sinT, t2 = tab("sin", 512)
    rotT, t3 = tab("rot", 1024)
    rotary([Q3[:, m, :] for m in range(4)] + [K3[:, m, :] for m in range(4)], cosT, sinT, rotT, a(1152, 512),
           t1, t2, t3)
    DT, t4 = tab("dt", 16384)
    KD, t5 = tab("kdec", 17408)
    QD_, t6 = tab("qdec", 17920)
    CD, t7 = tab("cdec", 18432)
    B64, t8 = tab("b64", 18440)
    QD = a(18568, 2048, 512)
    t = vtt(QD.rearrange("p a (c t) -> p a c t", t=128), Q3.rearrange("p a (c t) -> p a c t", t=128),
            QD_.rearrange("p (a t) -> p a t", t=128).unsqueeze(2).to_broadcast([128, 4, 4, 128]), ALU.mult, t6)
    KT = a(1664, 1536, 512)
    barrier()
    for ch in range(3):
        b = bank()
        for pr in range(4):
            t = tp(PB[b][:, pr * 128:(pr + 1) * 128], K3[:, pr, ch * 128:(ch + 1) * 128], *bfree[b], inc=pr == 3)
        bfree[b] = [vtt(KT[:, ch, :], PB[b][:, :], KD, ALU.mult, t, t5)]
    RS = a(0, 1536).rearrange("p (c a e) -> p c a e", a=4, e=128)
    for ch in range(3):
        b = bank()
        for pr in range(4):
            t = mm(PB[b][:, pr * 128:(pr + 1) * 128], KT[:, ch, pr * 128:(pr + 1) * 128],
                   V3[:, ch, pr * 128:(pr + 1) * 128], pr == 0, pr == 3, V.now, *bfree[b], inc=pr == 3)
        for pr in range(4):
            pu = PB[b][:, pr * 128:(pr + 1) * 128]
            if ch == 0:
                t = copy(V, RS[:, 0, pr, :], pu, t)
            else:
                t = stt(RS[:, ch, pr, :], RS[:, ch - 1, pr, :], CD[:, pr:pr + 1], pu, ALU.mult, ALU.add, t, t7)
        bfree[b] = [t]
    t_rs = V.now
    SMs = [a(3200, 512), a(3712, 512)]
    OT = a(20616, 512)
    XC, SQ_ = a(21128, 512), a(21640, 512)
    RV = OT
    pfree = [[], []]
    for pr in range(4):
        ob = bank()
        for hl in range(2):
            h = 2 * pr + hl
            ps = slice(hl * 64, hl * 64 + 64)
            b = bank((ob,))
            for ch in range(4):
                cs = slice(ch * 128, (ch + 1) * 128)
                t = mm(PB[b][:, cs], K3[ps, pr, cs], Q3[ps, pr, cs], ch == 0, ch == 3, *bfree[b], inc=ch == 3)
            t = vtt(SMs[hl].rearrange("p (c t) -> p c t", t=128), PB[b][:, :].rearrange("p (c t) -> p c t", t=128),
                    DT[:, h * 128:(h + 1) * 128].unsqueeze(1).to_broadcast([128, 4, 128]), ALU.mult, t, t4,
                    *pfree[hl])
            bfree[b] = [t]
            for ch in range(4):
                cs = slice(ch * 128, (ch + 1) * 128)
                mm(PB[ob][ps, cs], V3[:, ch, h * 64:(h + 1) * 64], SMs[hl][:, cs], ch == 0, False, t, *bfree[ob])
            for ch in range(1, 4):
                cs = slice(ch * 128, (ch + 1) * 128)
                t = mm(PB[ob][ps, cs], RS[ps, ch - 1, pr, hl * 64:hl * 64 + 64], QD[ps, pr, cs], False, ch == 3,
                       t_rs, inc=ch == 3)
            pfree[hl] = [t]
        t = copy(V, OT, PB[ob][:, :], t)
        bfree[ob] = [t]
        b = bank()
        t = mm(PB[b][:, :], B64, OT, True, True, t, t8, *bfree[b], inc=True)
        t = stt(XC, PB[b][:, :], -1.0 / 64, OT, ALU.mult, ALU.add, t)
        bfree[b] = [t]
        t = act(SQ_, XC, ACT.Square, t)
        b = bank()
        t = mm(PB[b][:, :], B64, SQ_, True, True, t, *bfree[b], inc=True)
        t = vts(RV, PB[b][:, :], 1.0 / 64, EPS, ALU.mult, ALU.add, t)
        bfree[b] = [t]
        t = act(RV, RV, ACT.Sqrt, t)
        V.do(lambda e: e.reciprocal(RV, RV), t)
        vtt(XC, XC, RV, ALU.mult)
        vtt(G3[:, pr, :], XC, G3[:, pr, :], ALU.mult)
    barrier()

    f0 = 16384
    lraw = ar[0:32, f0:f0 + 260]
    load(A, "s5p", lraw[:, 0:64], I["s5_lambda_re_2"][0])
    load(A, "s5p", lraw[:, 64:128], I["s5_lambda_re_2"][0])
    load(A, "s5p", lraw[:, 128:192], I["s5_lambda_im_2"][0])
    load(A, "s5p", lraw[:, 192:256], I["s5_lambda_im_2"][0])
    dl = a(f0 + 260, 32)
    t_sp = load(A, "s5p", dl, I["s5_log_step_2"][0:1, :].to_broadcast([128, 32]))
    B0 = a(0, 512, 16)
    BI = a(512, 512, 16)
    for lo, dst, nm in ((0, B0, "s5_b_re_2"), (64, B0, "s5_b_im_2"), (64, BI, "s5_b_re_2"), (0, BI, "s5_b_im_2")):
        t_b = load(A, "s5b", dst[lo:lo + 64, :, :], I[nm][0].rearrange("g p c -> p g c"))
    cr = a(1024, 512, 128)
    for lo, nm in ((0, "s5_c_re_2"), (64, "s5_c_im_2")):
        t_c = load(A, "s5c", cr[:, :, lo:lo + 64], I[nm][0].rearrange("(j g) c p -> (g c) j p", g=8))
    jmT, t_jm = tab("jm", f0 + 300)
    b16, t_b16 = tab("b16", f0 + 428)
    b = bank()
    tp(PB[b][:, 0:32], lraw[:, 0:128], t_sp, *bfree[b])
    t = tp(PB[b][:, 32:64], lraw[:, 128:256], inc=True)
    o = f0 + 556

    def sm(n=1):
        nonlocal o
        r = a(o, 32 * n)
        o += 32 * n
        return r

    LR, LI, DL, RE, TH, XX, KI, S_, Cc, RHO, R8, DD, FR, FI, TA, TB = (sm() for _ in range(16))
    AR, AI = sm(9), sm(9)
    TH8, WC, WS = sm(), sm(), sm()
    copy(V, LR, PB[b][:, 0:32], t)
    bfree[b] = [copy(V, LI, PB[b][:, 32:64])]
    t = act(DL, dl, ACT.Exp, t_sp)
    vtt(RE, LR, DL, ALU.mult, t)
    t = vtt(TH, LI, DL, ALU.mult)
    act(RHO, RE, ACT.Exp, t)
    t_r = act(R8, RE, ACT.Exp, scale=8.0)
    vts(TH8, TH, 8.0, None, ALU.mult, None)
    C1 = float(np.float32(6.28125))
    C2 = float(np.float32(TWO_PI - C1))
    C3 = float(TWO_PI - C1 - C2)

    def sincos(x, s, c):
        ki = KI.bitcast(I32)
        vts(XX, x, 1.0 / TWO_PI, None, ALU.mult, None)
        copy(V, ki, XX)
        copy(V, XX, ki)
        vts(TA, x, 1.0, None, ALU.mult, None)
        for cst in (C1, C2, C3):
            stt(TA, XX, -cst, TA, ALU.mult, ALU.add)
        t = vts(TA, TA, 3.1415925, -3.1415925, ALU.min, ALU.max)
        act(s, TA, ACT.Sin, t)
        t = act(TB, TA, ACT.Sin, scale=0.5)
        vtt(TB, TB, TB, ALU.mult, t)
        vts(c, TB, -2.0, 1.0, ALU.mult, ALU.add)

    sincos(TH, S_, Cc)
    sincos(TH8, WS, WC)

    def sl(x, i):
        return x[:, i * 32:(i + 1) * 32]

    V.do(lambda e: e.memset(sl(AR, 0), 1.0))
    V.do(lambda e: e.memset(sl(AI, 0), 0.0))
    vtt(sl(AR, 1), RHO, Cc, ALU.mult, t_r)
    vtt(sl(AI, 1), RHO, S_, ALU.mult)
    for i in range(2, 9):
        h1, h2 = i // 2, i - i // 2
        vtt(TA, sl(AR, h1), sl(AR, h2), ALU.mult)
        vtt(TB, sl(AI, h1), sl(AI, h2), ALU.mult)
        vtt(sl(AR, i), TA, TB, ALU.subtract)
        vtt(TA, sl(AR, h1), sl(AI, h2), ALU.mult)
        vtt(TB, sl(AI, h1), sl(AR, h2), ALU.mult)
        vtt(sl(AI, i), TA, TB, ALU.add)
    vtt(TA, LR, LR, ALU.mult)
    vtt(TB, LI, LI, ALU.mult)
    vtt(DD, TA, TB, ALU.add)
    V.do(lambda e: e.reciprocal(DD, DD))
    vts(XX, sl(AR, 1), -1.0, None, ALU.add, None)
    vtt(TA, XX, LR, ALU.mult)
    vtt(TB, sl(AI, 1), LI, ALU.mult)
    vtt(FR, TA, TB, ALU.add)
    vtt(TA, sl(AI, 1), LR, ALU.mult)
    vtt(TB, XX, LI, ALU.mult)
    vtt(FI, TA, TB, ALU.subtract)
    vtt(FR, FR, DD, ALU.mult)
    vtt(FI, FI, DD, ALU.mult)
    vts(BI[0:64, :, :], BI[0:64, :, :], -1.0, None, ALU.mult, None, t_b)
    tmp = a(1536, 512, 16)
    PA, PI_ = a(2048, 512, 16), a(2560, 512, 16)

    def bc(x):
        return x.unsqueeze(2).to_broadcast([128, 32, 16])

    vtt(tmp, BI, bc(FI), ALU.mult)
    vtt(PA, B0, bc(FR), ALU.mult)
    vtt(PA, PA, tmp, ALU.add)
    vtt(tmp, B0, bc(FI), ALU.mult)
    vtt(PI_, BI, bc(FR), ALU.mult)
    vtt(PI_, PI_, tmp, ALU.subtract)
    QA, QI = B0, BI
    b = bank()
    for j in range(4):
        t = tp(PB[b][:, j * 128:(j + 1) * 128], cr[:, j, :], t_c, *bfree[b], inc=j == 3)
    t = copy(V, QA.rearrange("p g c -> p (g c)"), PB[b][:, :], t)
    bfree[b] = [t]
    V.do(lambda e: e.tensor_scalar(QA[64:128, :, :], QA[64:128, :, :], -1.0, None, ALU.mult))
    b = bank()
    t = mm(PB[b][:, :], jmT, QA.rearrange("p g c -> p (g c)"), True, True, V.now, t_jm, *bfree[b], inc=True)
    bfree[b] = [copy(V, QI.rearrange("p g c -> p (g c)"), PB[b][:, :], t)]

    def power(dst, X, XI_, i, sign):
        vtt(tmp, XI_, bc(sl(AI, i)), ALU.mult)
        vtt(dst, X, bc(sl(AR, i)), ALU.mult)
        vtt(dst, dst, tmp, ALU.add if sign > 0 else ALU.subtract)

    PAf = PA.rearrange("p g c -> p (g c)")
    QT = [a(3072, 512, 16), a(3584, 512, 16)]
    KK = a(6144, 4096, 128)
    tq = [[], []]
    barrier()
    for tau in range(8):
        q_ = QT[tau % 2]
        V.wait(*tq[tau % 2])
        power(q_, QA, QI, tau, -1)
        b = bank()
        for j in range(4):
            t = mm(PB[b][:, j * 128:(j + 1) * 128], PAf[:, j * 128:(j + 1) * 128],
                   q_.rearrange("p g c -> p (g c)")[:, j * 128:(j + 1) * 128], j == 0, j == 3, V.now, *bfree[b],
                   inc=j == 3)
        tq[tau % 2] = [t]
        bfree[b] = [vtt(KK[:, tau * 4:tau * 4 + 4, :], PB[b][:, :].rearrange("p (j c) -> p j c", c=128),
                        b16.unsqueeze(1).to_broadcast([128, 4, 128]), ALU.mult, t, t_b16)]
        if tau == 0:
            for j in range(4):
                stt(KK[:, j, :], ident, C("s5d", j), KK[:, j, :], ALU.mult, ALU.add)
    barrier()
    for j in range(4):
        bank()
    turn[0] = 4
    for b_ in range(4):
        P.wait(*bfree[b_])
    for j in range(4):
        yv = PB[j][:, :].rearrange("p (n t) -> p n t", t=8)
        uv = U3[:, j, :].rearrange("p (n t) -> p n t", t=8)
        for tau in range(8):
            mm(yv[:, :, tau:8], KK[:, tau * 4 + j, :], uv[:, :, 0:8 - tau], tau == 0, False, inc=tau == 7)
    barrier()
    hb = (0, 1, 2, 3)
    PM = a(6144, 4096)
    PM4 = PM.rearrange("p (g s c) -> p g s c", s=8, c=16)
    for s_ in range(8):
        power(PM4[:, :, s_, :], PA, PI_, 7 - s_, 1)
    MG = a(18304, 4096)
    t_pm = V.now
    for g0 in range(0, 32, 4):
        b = bank(hb)
        for g in range(4):
            t = tp(PB[b][:, g * 128:(g + 1) * 128], PM[:, (g0 + g) * 128:(g0 + g + 1) * 128], t_pm, *bfree[b],
                   inc=g == 3)
        bfree[b] = [copy(A, MG[:, g0 * 128:(g0 + 4) * 128], PB[b][:, :], t)]
    barrier()
    UN = ar[0:64, 6144:10240].rearrange("p (g s c) -> p g s c", s=8, c=16)
    for s_ in range(8):
        b = bank(hb)
        for j in range(4):
            t = tp(PB[b][0:64, j * 128:(j + 1) * 128], U3[:, j, s_::8], *bfree[b], inc=j == 3)
        bfree[b] = [copy(V if s_ % 2 else A, UN[:, :, s_, :], PB[b][0:64, :].rearrange("p (g c) -> p g c", c=16), t)]
    barrier()
    UG = a(14336, 2048, 64)
    for g0 in range(0, 32, 8):
        b = bank(hb)
        for g in range(8):
            t = tp(PB[b][:, g * 64:(g + 1) * 64], ar[0:64, 6144 + (g0 + g) * 128:6144 + (g0 + g + 1) * 128], *bfree[b], inc=g == 7)
        bfree[b] = [copy(V if g0 % 16 else A, UG[:, g0:g0 + 8, :], PB[b][:, :].rearrange("p (g n) -> p g n", n=64), t)]
    barrier()
    VV = a(6144, 2048)
    VI = a(8192, 2048)
    for g0 in range(0, 32, 8):
        b = bank(hb)
        for g in range(8):
            t = mm(PB[b][:, g * 64:(g + 1) * 64], MG[:, (g0 + g) * 128:(g0 + g + 1) * 128], UG[:, g0 + g, :],
                   g == 0, g == 7, *bfree[b], inc=g == 7)
        t = copy(V, VV[:, g0 * 64:(g0 + 8) * 64], PB[b][:, :], t)
        bfree[b] = [t]
        b = bank(hb)
        t = mm(PB[b][:, :], jmT, VV[:, g0 * 64:(g0 + 8) * 64], True, True, t, *bfree[b], inc=True)
        bfree[b] = [copy(A, VI[:, g0 * 64:(g0 + 8) * 64], PB[b][:, :], t)]
    barrier()
    WR_, WI_ = a(18304, 2048, 64), a(20352, 2048, 64)
    TT1, TT2 = a(14336, 1024), a(15360, 1024)
    copy(V, WR_[:, :, 0:1], WC.unsqueeze(2))
    copy(V, WI_[:, :, 0:1], WS.unsqueeze(2))
    m_ = 1
    while m_ < 64:
        br_ = WR_[:, :, m_ - 1:m_].to_broadcast([128, 32, m_])
        bi_ = WI_[:, :, m_ - 1:m_].to_broadcast([128, 32, m_])
        x1 = TT1[:, 0:32 * m_].rearrange("p (g n) -> p g n", n=m_)
        x2 = TT2[:, 0:32 * m_].rearrange("p (g n) -> p g n", n=m_)
        vtt(x1, WR_[:, :, 0:m_], br_, ALU.mult)
        vtt(x2, WI_[:, :, 0:m_], bi_, ALU.mult)
        vtt(WR_[:, :, m_:2 * m_], x1, x2, ALU.subtract)
        vtt(x1, WR_[:, :, 0:m_], bi_, ALU.mult)
        vtt(x2, WI_[:, :, 0:m_], br_, ALU.mult)
        vtt(WI_[:, :, m_:2 * m_], x1, x2, ALU.add)
        m_ *= 2
    WRf, WIf = a(18304, 2048), a(20352, 2048)
    vtt(VV, VV, WRf, ALU.mult)
    vtt(VI, VI, WIf, ALU.mult)
    vtt(VV, VV, VI, ALU.subtract)
    D0 = a(14336, 2048, 64)
    copy(V, D0, R8.unsqueeze(2).to_broadcast([128, 32, 64]), t_r)
    V.do(lambda e: e.memset(D0[:, :, 0:1], 0.0))
    ZZ = VI
    V.do(lambda e: e.tensor_tensor_scan(ZZ, a(14336, 2048), VV, 0.0, ALU.mult, ALU.add))
    ZI = a(14336, 2048)
    for g0 in range(0, 4):
        b = bank(hb)
        t = mm(PB[b][:, :], jmT, ZZ[:, g0 * 512:(g0 + 1) * 512], True, True, V.now, *bfree[b], inc=True)
        bfree[b] = [copy(A, ZI[:, g0 * 512:(g0 + 1) * 512], PB[b][:, :], t)]
    XS = a(6144, 2048, 64)
    V.do(lambda e: e.memset(XS[:, :, 0:1], 0.0), A.now)
    Z3, I3 = ZZ.rearrange("p (g n) -> p g n", n=64), ZI.rearrange("p (g n) -> p g n", n=64)
    vtt(ZZ, ZZ, WRf, ALU.mult)
    vtt(ZI, ZI, WIf, ALU.mult)
    vtt(XS[:, :, 1:64], Z3[:, :, 0:63], I3[:, :, 0:63], ALU.add)
    barrier()
    GS = a(18304, 4096)
    GS4 = GS.rearrange("p (g s c) -> p g s c", s=8, c=16)
    for s_ in range(8):
        power(GS4[:, :, s_, :], QA, QI, s_ + 1, -1)
    YN = ar[0:64, 2048:6144].rearrange("p (t c) -> p t c", c=512)
    barrier()
    for g0 in range(0, 32, 4):
        b = bank(hb)
        for g in range(4):
            t = mm(PB[b][0:64, g * 128:(g + 1) * 128], XS[:, g0 + g, :], GS[:, (g0 + g) * 128:(g0 + g + 1) * 128],
                   g == 0, g == 3, *bfree[b], inc=g == 3)
        src = PB[b][0:64, :].rearrange("p (g t c) -> p t g c", t=8, c=16)
        dst = YN[:, :, g0 * 16:(g0 + 4) * 16].rearrange("p t (g c) -> p t g c", c=16)
        bfree[b] = [copy(V, dst, src, t)]
    t_yn = V.now
    SS3 = a(8192, 2048, 512)
    for j in range(4):
        yv = PB[j][:, :].rearrange("p (n t) -> p t n", t=8)
        for s_ in range(8):
            t = mm(yv[:, s_, :], YN[:, s_, j * 128:(j + 1) * 128], ident[0:64, 0:64], False, s_ == 7, t_yn,
                   inc=s_ == 7)
        t = act(SS3[:, j, :], PB[j][:, :], ACT.Gelu_apprx_tanh, t)
        bfree[j] = [t]
    t_ss = A.now

    def glu_ev(c, m, b, t):
        z = a(14336 + m * 512, 512)
        t = act(z, PB[b][:, :], ACT.Sigmoid, t)
        bfree[b] = [t]
        vtt(MX[:, 4 + m, :], SS3[:, m, :], z, ALU.mult, t)

    dense([512], lambda k: SS3[:, k, :], [4], glu_ev, t_ss)
    barrier()
    dense([512, 512], lambda k: MX[:, k, :], [8], resid(None))

    def ffn(l):
        barrier()
        norm(lambda k: C(f"ffn{l}", k), hn)
        barrier()
        ACC = a(4096, 11264, 512)
        sg = [a(15360 + i * 512, 512) for i in range(4)]
        sgf = [[], [], [], []]
        kk = 0
        for n in HCH:
            def ev_g(c, m, b, t):
                bfree[b] = [act(sg[m], PB[b][:, :], ACT.Silu, t, *sgf[m])]

            def ev_u(c, m, b, t):
                t = vtt(ACC[:, kk + m, :], sg[m], PB[b][:, :], ALU.mult, t, A.now)
                bfree[b] = [t]
                sgf[m] = [t]

            dense([n], hn, [8], ev_g)
            dense([n], hn, [8], ev_u)
            kk += n // 128
        barrier()
        dense([512, 512], lambda k: ACC[:, k, :], [8, 8, 6], resid(None))

    def ple(l):
        barrier()
        norm(lambda k: C(f"ple{l}", k), hn)
        pt = a(4096, 1024, 256)
        t0 = load(A, f"p{l}", pt, I["p_2"][l, 0].rearrange("(t p) d -> p t d", p=128))
        PTT = a(5120, 1024, 512)
        for k in range(2):
            b = bank()
            for t_ in range(4):
                t = tp(PB[b][:, t_ * 128:(t_ + 1) * 128], pt[:, t_, k * 128:(k + 1) * 128], t0, *bfree[b], inc=t_ == 3)
            bfree[b] = [copy(V, PTT[:, k, :], PB[b][:, :], t)]
        barrier()
        SG = a(6144, 4096, 512)
        dense([512, 512], hn, [8], lambda c, m, b, t: bfree.__setitem__(
            b, [act(SG[:, c * 4 + m, :], PB[b][:, :], ACT.Sigmoid, t)]))
        w = take()
        wv = rv(w, 0, 2, 1024)
        tp1 = [a(10240, 512), a(10752, 512)]
        for m in range(8):
            b = bank()
            for k in range(2):
                t = mm(PB[b][:, :], wv[:, k, m * 128:(m + 1) * 128], PTT[:, k, :], k == 0, k == 1, w.tok, *bfree[b],
                       inc=k == 1)
            t = vtt(tp1[m % 2], PB[b][:, :], SG[:, m, :], ALU.mult, t, A.now)
            bfree[b] = [t]
            vtt(hk(m), hk(m), tp1[m % 2], ALU.add)
        give(w, P.now)

    ffn(0)
    ple(0)

    barrier()
    norm(lambda k: C("mix1", k), hn)
    barrier()
    Q8 = a(4096, 4096, 512)
    K8 = a(8192, 4096, 512)
    V8 = a(12288, 4096, 1024)
    dense([512, 512], hn, [8], ev(lambda c, m: Q8[:, c * 4 + m, :]))
    dense([512, 512], hn, [8], ev(lambda c, m: K8[:, c * 4 + m, :]))
    dense([512, 512], lambda k, m: HN[:, k, m * 128:(m + 1) * 128], [8],
          ev(lambda c, m: V8[:, m, c * 512:(c + 1) * 512]), mode="tm")
    barrier()
    OO = a(0, 4096, 512)
    cosT, t1 = tab2("cos", 16384)
    sinT, t2 = tab2("sin", 16896)
    rotT, t3 = tab2("rot", 17408)
    rotary([Q8[:, m, :] for m in range(8)] + [K8[:, m, :] for m in range(8)], cosT, sinT, rotT, a(17536, 512),
           t1, t2, t3)
    lv_ = ar[0:1, 18048:18304].rearrange("p (i d) -> p i d", d=64)
    for i, nm in enumerate(("diff_lambda_q1_2", "diff_lambda_k1_2", "diff_lambda_q2_2", "diff_lambda_k2_2")):
        t = load(A, "lam", lv_[:, i, :], I[nm])
    ls = ar[0:1, 18304:18306]
    for i in range(2):
        vtt(lv_[:, 2 * i, :], lv_[:, 2 * i, :], lv_[:, 2 * i + 1, :], ALU.mult, t)
        V.do(lambda e, i=i: e.tensor_reduce(ls[:, i:i + 1], lv_[:, 2 * i, :], AX.X, ALU.add))
    t = act(ls, ls, ACT.Exp, V.now)
    b = bank()
    t = mm(PB[b][:, 0:2], ones[0:1, :], ls, True, True, t, *bfree[b], inc=True)
    le = a(18306, 2)
    copy(V, le, PB[b][:, 0:2], t)
    nlam = a(18308, 1)
    vtt(nlam, le[:, 1:2], le[:, 0:1], ALU.subtract)
    t = vts(nlam, nlam, -LAMBDA_INIT, None, ALU.add, None)
    bfree[b] = [t]
    caus, t_ca = tab("caus", 18320)
    SC = [a(18448, 512), a(18960, 512)]
    EE = [a(19472, 512), a(19984, 512)]
    WT = a(20496, 512)
    mxc = a(21008, 2)
    dnc = a(21010, 2)
    rro = a(21024, 512)
    sq1 = a(21536, 512)
    barrier()
    for h in range(8):
        ob = bank()
        for i in range(4):
            nk = (i + 1) * 128
            qs = slice(i * 128, nk)
            for s_ in range(2):
                ps = slice(s_ * 64, s_ * 64 + 64)
                b = bank((ob,))
                t = mm(PB[b][:, 0:nk], Q8[ps, h, qs], K8[ps, h, 0:nk], True, True, *bfree[b], inc=True)
                if i:
                    copy(V, SC[s_][:, 0:i * 128], PB[b][:, 0:i * 128], t)
                bfree[b] = [vtt(SC[s_][:, qs], PB[b][:, qs], caus, ALU.add, t, t_ca)]
                V.do(lambda e, s_=s_, nk=nk: e.tensor_reduce(mxc[:, s_:s_ + 1], SC[s_][:, 0:nk], AX.X, ALU.max))
                t = vts(mxc[:, s_:s_ + 1], mxc[:, s_:s_ + 1], -0.125, None, ALU.mult, None)
                t = act(EE[s_][:, 0:nk], SC[s_][:, 0:nk], ACT.Exp, t, bias=mxc[:, s_:s_ + 1], scale=0.125,
                        accum=dnc[:, s_:s_ + 1])
            V.do(lambda e: e.reciprocal(dnc, dnc), t)
            vtt(dnc[:, 1:2], dnc[:, 1:2], nlam, ALU.mult)
            vts(EE[0][:, 0:nk], EE[0][:, 0:nk], dnc[:, 0:1], None, ALU.mult, None)
            t = stt(EE[0][:, 0:nk], EE[1][:, 0:nk], dnc[:, 1:2], EE[0][:, 0:nk], ALU.mult, ALU.add)
            b = bank((ob,))
            for j in range(i + 1):
                tt_ = tp(PB[b][:, j * 128:(j + 1) * 128], EE[0][:, j * 128:(j + 1) * 128], t, *bfree[b], inc=j == i)
            t = copy(A, WT[:, 0:nk], PB[b][:, 0:nk], tt_)
            bfree[b] = [t]
            for j in range(i + 1):
                t2 = mm(PB[ob][:, qs], V8[:, j, h * 128:(h + 1) * 128], WT[:, j * 128:(j + 1) * 128],
                        i == 0 and j == 0, j == i, t, *bfree[ob], inc=j == i)
            A.wait(t2)
        obv = PB[ob][:, :]
        V.wait(t2)
        t = norm_stat(lambda k: obv, 1, 512, [sq1, sq1], rro, 1.0 / 128, b=bank((ob,)))
        t = vtt(OO[:, h, :], obv, rro, ALU.mult, t)
        bfree[ob] = [t]
        vts(OO[:, h, :], OO[:, h, :], C("subln"), 1.0 - LAMBDA_INIT, ALU.mult, ALU.mult)
    barrier()
    dense([512, 512], lambda k: OO[:, k, :], [8], resid(None))
    ffn(1)
    ple(1)
    barrier()
    norm(lambda k: C("fin2", k), hk)
    barrier()
    store_out(hk)
    emit_all()


_INS = ["x", "c", "ctx", "c_ctx", "w_ada", "b_ada", "norm_mix_w", "norm_mlp_w", "w_in", "w_gk_f", "b_gk_f", "w_gk_b",
        "b_gk_b", "gla_norm_w", "w_pool", "pool_scale", "w_out", "w_router", "b_router", "w_gu", "b_gu", "w_down",
        "b_down", "final_norm_w", "p_2", "norm_mix_2", "norm_ffn_2", "norm_ple_2", "ret_s5_w_in_2", "ret_s5_w_out_2",
        "s5_lambda_re_2", "s5_lambda_im_2", "s5_b_re_2", "s5_b_im_2", "s5_c_re_2", "s5_c_im_2", "s5_d_2",
        "s5_log_step_2", "s5_w_glu_2", "diff_w_qkv_2", "diff_w_o_2", "diff_lambda_q1_2", "diff_lambda_k1_2",
        "diff_lambda_q2_2", "diff_lambda_k2_2", "diff_subln_2", "ffn_w_gate_2", "ffn_w_up_2", "ffn_w_down_2",
        "ple_w_proj_2", "ple_w_gate_2", "final_norm_2"]


def kernel(**inputs):
    import concourse.bacc as bacc
    from concourse.bass_utils import run_bass_kernel_spmd

    nc = bacc.Bacc("TRN2", target_bir_lowering=False, num_devices=1)
    arrays, ins = {}, {}
    consts = const_tables()
    held = {name: np.ascontiguousarray(inputs[name]) for name in _INS}
    held["tabs"] = np.concatenate([consts[n] for n in TABLE_ORDER], axis=1)
    held["ptab"] = pool_tables()
    for name, v in held.items():
        arrays[f"in_{name}"] = v
        ins[name] = nc.dram_tensor(f"in_{name}", v.shape, F32, kind="ExternalInput").ap()
    out = nc.dram_tensor("out_0", (1, 512, 1024), F32, kind="ExternalOutput").ap()
    build(nc, ins, out)
    r = run_bass_kernel_spmd(nc, [arrays], core_ids=[0])
    return r.results[0]["out_0"]
```

```python
import numpy as np
import concourse.bass as bass
from concourse import mybir

F32 = mybir.dt.float32
F32R = mybir.dt.float32r
BF16 = mybir.dt.bfloat16
I32 = mybir.dt.int32
U32 = mybir.dt.uint32
ALU = mybir.AluOpType
ACT = mybir.ActivationFunctionType
AX = mybir.AxisListType

EPS = 1e-6
NRING = 18
SLOT = 1024
NUNIT = 4
UNIT = 1024
ARENA = 24064
NBLK = 47
LAMBDA_INIT = 0.8 - 0.6 * float(np.exp(-0.3))
TWO_PI = 2.0 * float(np.pi)


def const_tables():
    f = np.float32
    p = np.arange(128)
    out = {}
    out["ident"] = np.eye(128, dtype=f)
    out["ones"] = np.ones((128, 128), f)
    out["tri"] = (p[:, None] < p[None, :]).astype(f)
    same = (p[:, None] // 64) == (p[None, :] // 64)
    out["maskf"] = np.tile(((p[:, None] <= p[None, :]) & same).astype(f), (1, 4))
    out["maskb"] = np.tile(((p[:, None] >= p[None, :]) & same).astype(f), (1, 4))
    out["scan"] = np.tile((np.arange(768) % 64 != 0).astype(f), (128, 1))
    out["iota"] = np.tile(np.arange(128, dtype=f), (128, 1))
    out["tok"] = (p[:, None] + 128 * np.arange(4)[None, :]).astype(f)
    out["pmod"] = np.tile((p % 32).astype(f)[:, None], (1, 4))
    out["sel"] = (p[:, None] % 32 == np.arange(32)[None, :]).astype(f)
    inv = (10000.0 ** (-np.arange(0, 64, 2, dtype=f) / f(64))).astype(f)
    ang = (np.arange(512, dtype=f)[None, :] * inv[p % 32][:, None]).astype(f)
    out["cos"] = np.cos(ang.astype(np.float64)).astype(f)
    out["sin"] = np.sin(ang.astype(np.float64)).astype(f)
    rot = np.zeros((128, 128), f)
    for m in range(128):
        b, r = m // 64 * 64, m % 64
        rot[b + (r + 32) % 64, m] = -1.0 if r < 32 else 1.0
    out["rot"] = rot
    gamma = (1.0 - 2.0 ** (-5.0 - np.arange(8, dtype=f))).astype(f)
    lg = np.log(gamma).astype(f).astype(np.float64)
    rel = p[None, :] - p[:, None]
    dt = np.where(rel[None] >= 0, np.exp(lg[:, None, None] * np.maximum(rel, 0)[None]), 0.0) * 0.125
    out["dt"] = np.concatenate(list(dt), axis=1).astype(f)
    out["kdec"] = np.repeat(np.exp(lg[None, :] * (127 - p[:, None])) * 0.125, 64, axis=1).astype(f)
    qd = np.exp(lg[:, None] * (p[None, :] + 1.0))
    out["qdec"] = np.concatenate([np.repeat(qd[2 * i:2 * i + 2], 64, axis=0) for i in range(4)], axis=1).astype(f)
    cd = np.exp(lg * 128.0)
    out["cdec"] = np.stack([np.repeat(cd[2 * i:2 * i + 2], 64) for i in range(4)], axis=1).astype(f)
    out["b64"] = same.astype(f)
    out["caus"] = np.where(p[None, :] <= p[:, None], 0.0, -1e30).astype(f)
    jm = np.zeros((128, 128), f)
    for m in range(64):
        jm[m + 64, m] = -1.0
        jm[m, m + 64] = 1.0
    out["jm"] = jm
    out["b16"] = ((p[:, None] // 16) == (p[None, :] // 16)).astype(f)
    return out


def pool_tables():
    f = np.float64
    out = []
    for w in (2, 4, 8, 16):
        lo = w // 2
        hi = w - 1 - lo

        def band(n):
            i = np.arange(n)
            a = np.clip(i - lo, 0, n)
            b = np.clip(i + hi + 1, 0, n)
            m = ((i[:, None] >= a[None, :]) & (i[:, None] < b[None, :])).astype(f)
            return m, (b - a).astype(f)

        mr, cr = band(8)
        mc, cc = band(64)
        m = np.kron(mr, mc) / np.kron(cr, cc)[None, :]
        out.append((m - np.eye(512)).astype(np.float32))
    return np.stack(out)


TABLE_ORDER = ["ident", "ones", "tri", "maskf", "maskb", "scan", "iota", "tok", "pmod", "sel", "cos", "sin",
               "rot", "dt", "kdec", "qdec", "cdec", "b64", "caus", "jm", "b16"]


def table_offsets():
    t = const_tables()
    at, out = 0, {}
    for n in TABLE_ORDER:
        out[n] = (at, t[n].shape[1])
        at += t[n].shape[1]
    return out, at


class Queue:

    def __init__(self, sem, chained):
        self.sem, self.chained = sem, chained
        self.ops, self.n, self.seen = [], 0, {}

    @property
    def now(self):
        return (self.sem, self.n)

    def wait(self, *toks):
        for sem, val in toks:
            if val > self.seen.get(sem, 0):
                self.seen[sem] = val
                self.ops.append((0, sem, val))

    def do(self, fn, *toks, inc=True, chain=True):
        self.wait(*toks)
        if self.chained and chain:
            self.wait(self.now)
        if inc:
            self.n += 1
        self.ops.append((1, fn, inc))
        return self.now

    def dma(self, sem, counts, fn, *toks):
        self.wait(*toks)
        counts[sem] = counts.get(sem, 0) + 16
        self.ops.append((2, fn, sem))
        return (sem, counts[sem])

    def emit(self, eng, shift=None, after=None):
        for kind, a, b in self.ops:
            if kind == 3:
                a(eng)
                continue
            if kind == 0:
                eng.wait_ge(a, shift(a, b) if shift else b)
                if shift:
                    eng.sem_inc(after, 1)
            elif kind == 1:
                ins = a(eng)
                if b:
                    ins.then_inc(self.sem, 1)
            else:
                a(eng).then_inc(b, 16)


def build(nc, ins, out):
    TOFF, _ = table_offsets()

    def sb(name, shape, dt=F32):
        return nc.alloc_sbuf_tensor(name, shape, dt)

    H = sb("H", [128, 8 * 512])
    KC = sb("KC", [128, 256])
    COLS = sb("COLS", [128, 160])
    MOD = sb("MOD", [128, 96])
    SM = sb("SM", [128, 256])
    BPT = sb("BPT", [128, 1536])
    base = (nc.sbuf_base + 31) // 32 * 32
    ar = nc.alloc_sbuf_tensor_at("arena", [128, ARENA], F32, offset=base)
    arr = nc.alloc_sbuf_tensor_at("arena_r", [128, ARENA], F32R, offset=base)
    ring = nc.alloc_sbuf_tensor_at("ring", [128, NRING * SLOT], F32, offset=base + 4 * ARENA)
    ring_r = nc.alloc_sbuf_tensor_at("ring_r", [128, NRING * SLOT], F32R, offset=base + 4 * ARENA)
    WU = nc.alloc_sbuf_tensor_at("wunits", [128, NUNIT * UNIT], F32R, offset=base + 4 * (ARENA + NRING * SLOT))
    PB = [nc.alloc_psum_tensor(f"pb{i}", [128, 512], F32) for i in range(8)]
    hm_d = nc.dram_tensor("hm_scratch", (512, 1024), F32).ap()
    y_d = nc.dram_tensor("y_scratch", (NBLK * 128, 1024), F32).ap()
    ident = KC[:, 0:128]
    ones = KC[:, 128:256]

    def sem(name):
        return nc.alloc_semaphore(name)

    V = Queue(sem("s_dve"), True)
    A = Queue(sem("s_act"), True)
    G = Queue(sem("s_pool"), True)
    P = Queue(sem("s_pe"), False)
    S = Queue(sem("s_sp"), False)
    QS = (V, A, G, P)
    counts = {}
    s_ring = [sem(f"s_ring{i}") for i in range(NRING)]
    s_more = [sem(f"s_more{i}") for i in range(8)]
    s_small = {}

    def load(q, name, dst, src, *toks):
        if name not in s_small:
            s_small[name] = sem("s_" + name)
        return q.dma(s_small[name], counts, lambda e: e.dma_start(dst, src), *toks)

    def a(lo, n, shape=None):
        v = ar[:, lo:lo + n]
        if shape is not None:
            v = v.rearrange("p (a b) -> p a b", b=shape)
        return v

    def barrier():
        toks = [q.now for q in QS]
        for q in QS:
            q.wait(*[t for t in toks if t[1]])

    def r(lo, n, shape=None):
        v = arr[:, lo:lo + n]
        if shape is not None:
            v = v.rearrange("p (a b) -> p a b", b=shape)
        return v

    def place(base_, n, split=False):
        if base_ < ARENA:
            return (arr if split else ar)[:, base_:base_ + n]
        return (ring_r if split else ring)[:, base_ - ARENA:base_ - ARENA + n]

    class Piece:
        pass

    class Stream:

        def __init__(self, sp, sc, ve, cnt, sems):
            self.S, self.A, self.V, self.counts = sp, sc, ve, cnt
            self.slots = [(s_, ARENA + i * SLOT, Piece()) for i, s_ in enumerate(sems)]
            for x in self.slots:
                x[2].free = []
            self.planned, self.pieces, self.units = [], [], []
            self.used = self.raws = 0

        def plan(self, src, kt, n, split=True):
            self.planned.append((src, kt, n))
            w = Piece()
            w.i, w.n, w.kt, w.split, w.free, w.tok = len(self.planned) - 1, n, kt, split, None, None
            self.pieces.append(w)
            if split:
                ku = UNIT // n
                k = 0
                while k < kt:
                    u = Piece()
                    u.i, u.w, u.k0, u.kt, u.n, u.free, u.tok = len(self.units), w, k, min(ku, kt - k), n, None, None
                    self.units.append(u)
                    k += ku
                u.last = True
                for x in self.units:
                    if x.w is w and x is not u:
                        x.last = False

        def add(self, sems, bases, *toks):
            for s_, base in zip(sems, bases):
                old = Piece()
                old.free = list(toks)
                self.slots.insert(0, (s_, base, old))
            self.fetch()

        def drop(self, sems):
            self.slots = [x for x in self.slots if x[0] not in sems]

        def fetch(self):
            for w in self.pieces[self.raws:]:
                sem_, base, old = self.slots[0]
                if old.free is None:
                    return
                self.slots = self.slots[1:] + [(sem_, base, w)]
                src, kt, n = self.planned[w.i]
                w.base = base
                dst = place(base, kt * n).rearrange("p (a b) -> p a b", b=n)
                w.tok = self.S.dma(sem_, self.counts, lambda e, d=dst, s_=src: e.dma_start(d, s_()), *old.free)
                self.raws += 1

        def convert(self):
            self.fetch()
            while self.conv_ok():
                u = self.units[self.conv_n]
                wait = [self.units[u.i - NUNIT].free] if u.i >= NUNIT else []
                o = (u.i % NUNIT) * UNIT
                m_ = u.kt * u.n
                lo = u.w.base + u.k0 * u.n
                raw = place(lo, m_)
                h, l_ = WU[:, o:o + m_], place(lo, m_, True)
                t = self.A.do(lambda e, h=h, raw=raw: e.activation(h, raw, ACT.Copy), u.w.tok, *wait, chain=False)
                u.tok = self.V.do(lambda e, h=h, l_=l_, raw=raw: e.tensor_tensor(
                    l_, raw, h.bitcast(F32), ALU.subtract), t, u.w.tok, chain=False)
                u.h = h.rearrange("p (a b) -> p a b", b=u.n)
                u.l = l_.rearrange("p (a b) -> p a b", b=u.n)
                self.conv_n += 1

        conv_n = 0

        def conv_ok(self):
            if self.conv_n >= len(self.units) or self.conv_n >= self.used + NUNIT:
                return False
            u = self.units[self.conv_n]
            return u.w.tok is not None and (u.i < NUNIT or self.units[u.i - NUNIT].free is not None)

        def unit(self):
            self.convert()
            u = self.units[self.used]
            assert u.tok is not None
            self.used += 1
            return u

        def done(self, u, tok):
            u.free = tok
            if u.last:
                u.w.free = [tok]
            self.convert()

    W = Stream(S, A, V, counts, s_ring)
    raw_at = [0]

    def take():
        W.fetch()
        while W.pieces[raw_at[0]].split:
            raw_at[0] += 1
        w = W.pieces[raw_at[0]]
        raw_at[0] += 1
        assert w.tok is not None
        return w

    def give(w, *toks):
        w.free = list(toks)
        W.convert()

    def rv(w, off, na, nb):
        return place(w.base + off, na * nb).rearrange("p (a b) -> p a b", b=nb)

    bfree = [[] for _ in range(8)]
    turn = [0]

    inuse = []
    jobs, slow = [], []

    def bank(held=()):
        while True:
            b = turn[0] % 8
            turn[0] += 1
            if b not in held and b not in inuse:
                return b

    def step():
        for some in (jobs, slow):
            while some:
                for _ in some[0]:
                    return
                some.pop(0)

    def finish_jobs():
        while jobs:
            step()

    def wsrc(w, rows, lo, n):
        return w[:, lo:lo + n].rearrange("(j p) n -> p j n", p=128)

    def mm(outp, lhsT, rhs, start, stop, *toks, inc=False):
        return P.do(lambda e: e.matmul(outp, lhsT, rhs, start=start, stop=stop, skip_group_check=True),
                    *toks, inc=inc)

    def tp(outp, in_, *toks, inc=False):
        k = in_.shape[0]
        return P.do(lambda e: e.transpose(outp, in_, ident[0:k, 0:k]), *toks, inc=inc)

    def vtt(o, x, y, op, *toks, q=None):
        return (q or V).do(lambda e: e.tensor_tensor(o, x, y, op), *toks)

    def vts(o, x, s1, s2, op0, op1, *toks, q=None):
        if op1 is None:
            return (q or V).do(lambda e: e.tensor_scalar(o, x, s1, None, op0), *toks)
        return (q or V).do(lambda e: e.tensor_scalar(o, x, s1, s2, op0, op1), *toks)

    def stt(o, x, s, y, op0, op1, *toks):
        return V.do(lambda e: e.scalar_tensor_tensor(out=o, in0=x, scalar=s, in1=y, op0=op0, op1=op1), *toks)

    def act(o, x, f, *toks, bias=None, scale=None, accum=None):
        kw = {}
        if bias is not None:
            kw["bias"] = bias
        if scale is not None:
            kw["scale"] = scale
        if accum is not None:
            kw["accum_out"] = accum
        return A.do(lambda e: e.activation(o, x, f, **kw), *toks)

    def copy(q, o, x, *toks):
        if q is A:
            return act(o, x, ACT.Copy, *toks)
        return q.do(lambda e: e.tensor_copy(o, x), *toks)

    def mm3(outp, l_, x, start, stop, *toks, inc=False, q=None):
        q = q or P
        (lh, ll), (rh, rl) = l_, x
        q.do(lambda e: e.matmul(outp, lh, rh, start=start, stop=False, skip_group_check=True), *toks, inc=False)
        q.do(lambda e: e.matmul(outp, lh, rl, start=False, stop=False, skip_group_check=True), inc=False)
        return q.do(lambda e: e.matmul(outp, ll, rh, start=False, stop=stop, skip_group_check=True), inc=inc)

    def split(dh, dl, src, *toks):
        t = act(dh, src, ACT.Copy, *toks)
        return vtt(dl, src, dh.bitcast(F32), ALU.subtract, t, *toks)

    def dense(widths, x_fn, kt, evac, *toks, mode="fm", ntile=4, held=(), n=512):
        for c, width in enumerate(widths):
            nt = (width // 128) if mode == "fm" else ntile
            banks = [bank(held) for _ in range(nt)]
            inuse.extend(banks)
            k0 = 0
            while k0 < kt:
                u = W.unit()
                assert u.n == width, (u.n, width)
                g = u.kt
                last = k0 + g == kt
                for m in range(nt):
                    b = banks[m]
                    for k in range(g):
                        kk = k0 + k
                        st = kk == 0
                        tk = ([u.tok] if m == 0 and k == 0 else []) + (bfree[b] if st else [])
                        xt_ = []
                        if mode == "fm":
                            x = x_fn(kk)
                            t = mm3(PB[b][:, 0:n], (u.h[:, k, m * 128:(m + 1) * 128], u.l[:, k, m * 128:(m + 1) * 128]),
                                    x[0:2], st, last and k == g - 1, *tk, *toks, *x[2:], inc=(k == g - 1))
                        else:
                            x = x_fn(kk, m)
                            t = mm3(PB[b][:, 0:width], x[0:2], (u.h[:, k, :], u.l[:, k, :]), st,
                                    last and k == g - 1, *tk, *toks, *x[2:], inc=(k == g - 1))
                    if last:
                        evac(c, m, b, t)
                k0 += g
                W.done(u, P.now)
                if not last:
                    step()
            for b in banks:
                inuse.remove(b)
            step()

    def norm_stat(src, nk, T, sq, r, scale, *toks, mat=None, b=None):
        b = bank() if b is None else b
        m_ = ones if mat is None else mat
        pt = [None, None]
        for k in range(nk):
            w = [pt[k % 2]] if pt[k % 2] else []
            t = act(sq[k % 2][:, 0:T], src(k), ACT.Square, *w, *toks)
            pt[k % 2] = mm(PB[b][:, 0:T], m_, sq[k % 2][:, 0:T], k == 0, k == nk - 1, t,
                           *(bfree[b] if k == 0 else []), inc=True)
        t = vts(r, PB[b][:, 0:T], scale, EPS, ALU.mult, ALU.add, pt[(nk - 1) % 2], *toks)
        bfree[b] = [t]
        t = act(r, r, ACT.Sqrt, t)
        t = V.do(lambda e: e.reciprocal(r, r), t)
        return t

    def norm_apply(src, dst, nk, r_, gain, shift, *toks):
        for k in range(nk):
            t = stt(dst(k), src(k), gain(k), r_, ALU.mult, ALU.mult, *toks)
            if shift is not None:
                act(dst(k), dst(k), ACT.Identity, t, bias=shift(k))

    def norm_split(src, dh, dl, nk, r_, gain, shift, tmp, *toks):
        out_, free = [], [[], []]
        for k in range(nk):
            x = tmp[k % 2]
            n_ = src(k).shape[-1]
            x = x[:, 0:n_]
            t = stt(x, src(k), gain(k), r_, ALU.mult, ALU.mult, *toks, *free[k % 2])
            if shift is None:
                t = act(dh(k), x, ACT.Copy, t)
                t = vtt(dl(k), x, dh(k).bitcast(F32), ALU.subtract, t)
            else:
                t = act(dh(k), x, ACT.Identity, t, bias=shift(k))
                t = stt(dl(k), x, shift(k), dh(k).bitcast(F32), ALU.add, ALU.subtract, t)
            free[k % 2] = [t]
            out_.append(t)
        return out_

    def hk(k):
        return H[:, k * 512:(k + 1) * 512]

    I = ins
    w_ada, w_in = I["w_ada"][0], I["w_in"][0]

    def plan_cols(w, kt, lo, n, split=True):
        kp = SLOT // n
        for k in range(0, kt, kp):
            g = min(kp, kt - k)
            W.plan(lambda w=w, k=k, g=g, lo=lo, n=n: wsrc(w[k * 128:(k + g) * 128, :], g, lo, n), g, n, split)

    for c in range(4):
        plan_cols(w_ada, 8, c * 512, 512, False)
    for lo, n in ((0, 512), (512, 512), (1024, 512), (1536, 128), (1568, 512)):
        plan_cols(w_in, 8, lo, n)
    for g in range(4):
        for h in range(2):
            W.plan(lambda g=g, h=h: I["ptab"][g, h * 256:(h + 1) * 256, :].rearrange("(j p) n -> p j n", p=128), 2, 512,
                   False)
    for c in range(4, 12):
        plan_cols(w_ada, 8, c * 512, 512, False)
    for c in range(2):
        plan_cols(I["w_out"][0], 8, c * 512, 512)
    for e_ in range(33):
        for n in range(4):
            if e_ < 32:
                plan_cols(I["w_gu"][0, e_], 8, (n % 2) * 1024 + (n // 2) * 512, 512)
            if n == 0 and e_:
                plan_cols(I["w_down"][0, e_ - 1, 512:1024, :], 4, 0, 1024)
        if e_ < 32:
            plan_cols(I["w_down"][0, e_, 0:512, :], 4, 0, 1024)

    tk0 = load(A, "kc", KC[:, :], I["tabs"][:, 0:256])
    rows = a(22784, 256)
    R1 = []
    at = 0

    def vec(name, src, n, half):
        nonlocal at
        R1.append((name, at, n, half))
        load(A, "rows", rows[at:at + n, half * 128:half * 128 + 128], src)
        at += n

    def r2(x, n):
        return x.rearrange("(j p) -> j p", p=128)

    vec("nmix", r2(I["norm_mix_w"][0], 8), 8, 0)
    vec("nmlp", r2(I["norm_mlp_w"][0], 8), 8, 0)
    vec("nfin", r2(I["final_norm_w"], 8), 8, 0)
    vec("glan", r2(I["gla_norm_w"][0], 1), 1, 0)
    vec("pscale", r2(I["pool_scale"][0], 4), 4, 0)
    vec("bgk", r2(I["b_gk_f"][0], 2), 2, 0)
    vec("bgk2", r2(I["b_gk_b"][0], 2), 2, 0)
    for l in range(2):
        vec(f"mix{l}", r2(I["norm_mix_2"][l], 8), 8, 0)
        vec(f"ffn{l}", r2(I["norm_ffn_2"][l], 8), 8, 0)
        vec(f"ple{l}", r2(I["norm_ple_2"][l], 8), 8, 0)
    vec("fin2", r2(I["final_norm_2"], 8), 8, 0)
    vec("subln", r2(I["diff_subln_2"][0], 1), 1, 0)
    vec("s5d", I["s5_d_2"][0].rearrange("(j g) c -> j (g c)", g=8), 4, 0)
    vec("c", r2(I["c"][0], 8), 8, 0)
    vec("cctx", r2(I["c_ctx"], 8), 8, 0)
    n0 = at
    at = 0
    vec("bada", r2(I["b_ada"][0], 48), 48, 1)
    tk_rows = (s_small["rows"], counts[s_small["rows"]])
    b = bank()
    tp(PB[b][:, 0:n0], rows[0:n0, 0:128], tk0, tk_rows)
    t = tp(PB[b][:, n0:n0 + 48], rows[0:48, 128:256], inc=True)
    t_cols = copy(V, COLS[:, 0:n0 + 48], PB[b][:, 0:n0 + 48], t)
    bfree[b] = [t_cols]
    col = {}
    for name, at_, n, half in R1:
        col[name] = (n0 if half else 0) + at_

    def C(name, k=0, n=1):
        return COLS[:, col[name] + k:col[name] + k + n]

    xt = a(256, 4096, 1024)
    ct = a(4352, 2048, 1024)
    HC = a(6400, 2048, 256)
    tx = load(A, "x", xt, I["x"][0].rearrange("(t p) d -> p t d", p=128))
    tc = load(A, "ctx", ct, I["ctx"][0].rearrange("(t p) d -> p t d", p=128))
    for k in range(8):
        b = bank()
        for t_ in range(4):
            t = tp(PB[b][:, t_ * 128:(t_ + 1) * 128], xt[:, t_, k * 128:(k + 1) * 128], tx, *bfree[b], inc=t_ == 3)
        q = A if k % 2 else V
        bfree[b] = [copy(q, hk(k), PB[b][:, :], t)]
    for k in range(8):
        b = bank()
        for t_ in range(2):
            t = tp(PB[b][:, t_ * 128:(t_ + 1) * 128], ct[:, t_, k * 128:(k + 1) * 128], tc, *bfree[b], inc=t_ == 1)
        q = A if k % 2 else V
        bfree[b] = [copy(q, HC[:, k, :], PB[b][:, 0:256], t)]
    barrier()

    cc = SM[:, 0:16].rearrange("p (k s) -> p k s", s=2)
    t = act(cc[:, :, 0], C("c", 0, 8), ACT.Silu, t_cols)
    t_cc = act(cc[:, :, 1], C("cctx", 0, 8), ACT.Silu)

    HNh, HNl = r(10496, 6144, 768), r(16640, 6144, 768)
    sq = [a(8448, 512), a(8960, 512)]
    rx = a(9472, 512)
    rc = a(9984, 256)
    t_rx = norm_stat(hk, 8, 512, sq, rx, 1.0 / 1024)
    t_rc = norm_stat(lambda k: HC[:, k, :], 8, 256, sq, rc, 1.0 / 1024)

    modrow = a(1024, 1024)
    mcol = MOD[:, :].rearrange("p (j s) -> p j s", s=2)
    tmod = [None, None]

    def ada(c):
        b = bank()
        for k in range(8):
            if k % 2 == 0:
                w = take()
                wv = rv(w, 0, 2, 512)
            t = mm(PB[b][0:2, :], cc[:, k, :], wv[:, k % 2, :], k == 0, k == 7, w.tok, t_cc, *bfree[b], inc=k % 2 == 1)
            if k % 2 == 1:
                give(w, t)
        mr = modrow[0:2, (c % 2) * 512:(c % 2) * 512 + 512]
        t = copy(A, mr, PB[b][0:2, :], t, *([tmod[c % 2]] if tmod[c % 2] else []))
        bfree[b] = [t]
        b = bank()
        for j in range(4):
            t = tp(PB[b][:, 2 * j:2 * j + 2], mr[:, j * 128:(j + 1) * 128], t, *bfree[b], inc=j == 3)
        tmod[c % 2] = t
        t = V.do(lambda e: e.tensor_tensor(
            mcol[:, 4 * c:4 * c + 4, :], PB[b][:, 0:8].rearrange("p (j s) -> p j s", s=2),
            C("bada", 4 * c, 4).unsqueeze(2).to_broadcast([128, 4, 2]), ALU.add), t)
        bfree[b] = [t]

    for c in range(4):
        ada(c)

    def M(i, k, s=0):
        return mcol[:, i * 8 + k, s:s + 1]

    gm = SM[:, 32:64].rearrange("p (a k) -> p a k", k=8)
    for s in range(2):
        vts(gm[:, s, :], mcol[:, 8:16, s], 1.0, None, ALU.add, None)
        t_gm = vtt(gm[:, s, :], gm[:, s, :], C("nmix", 0, 8), ALU.mult)
    ntmp = [a(0, 512), a(512, 512)]
    norm_split(hk, lambda k: HNh[:, k, 0:512], lambda k: HNl[:, k, 0:512], 8, rx, lambda k: gm[:, 0, k:k + 1],
               lambda k: M(0, k, 0), ntmp, t_rx)
    norm_split(lambda k: HC[:, k, :], lambda k: HNh[:, k, 512:768], lambda k: HNl[:, k, 512:768], 8, rc,
               lambda k: gm[:, 1, k:k + 1], lambda k: M(0, k, 1), ntmp, t_rc, V.now)

    ZB = a(23040, 1024)
    tz = G.do(lambda e: e.memset(ZB, 0.0))
    t_zero = load(G, "zero", y_d[4096:NBLK * 128, :].rearrange("(b p) d -> p b d", p=128),
                  ZB.unsqueeze(1).to_broadcast([128, NBLK - 32, 1024]), tz)

    barrier()
    QX = a(0, 1024, 512)
    KX = a(1024, 1536, 768)
    GX = a(2560, 2048, 512)
    MX = a(2560, 4096, 512)
    PT = a(4608, 2048, 512)
    VT = a(6656, 3072, 512)
    RX = ar[0:32, 9728:10496]
    def xh(k):
        return HNh[:, k, 0:512], HNl[:, k, 0:512]

    def xtok(k, m):
        return HNh[:, k, m * 128:(m + 1) * 128], HNl[:, k, m * 128:(m + 1) * 128]

    banks = [bank() for _ in range(6)]
    for u_ in range(4):
        u = W.unit()
        for m in range(4):
            for k in range(2):
                kk = 2 * u_ + k
                l_ = (u.h[:, k, m * 128:(m + 1) * 128], u.l[:, k, m * 128:(m + 1) * 128])
                t = mm3(PB[banks[m]][:, :], l_, xh(kk), kk == 0, kk == 7, u.tok, *bfree[banks[m]], inc=k == 1)
            if m >= 2:
                for k in range(2):
                    kk = 2 * u_ + k
                    l_ = (u.h[:, k, m * 128:(m + 1) * 128], u.l[:, k, m * 128:(m + 1) * 128])
                    b = banks[m + 2]
                    t = mm3(PB[b][:, 0:256], l_, (HNh[:, kk, 512:768], HNl[:, kk, 512:768]), kk == 0, kk == 7,
                            *bfree[b], inc=k == 1)
        W.done(u, P.now)
    for m in range(6):
        b = banks[m]
        dst = QX[:, m, :] if m < 2 else KX[:, m - 2, 0:512] if m < 4 else KX[:, m - 4, 512:768]
        bfree[b] = [copy(V if m % 2 else A, dst, PB[b][:, 0:dst.shape[-1]], P.now)]
    dense([512], xtok, 8,
          lambda c, m, b, t: bfree.__setitem__(b, [copy(V if m % 2 else A, VT[:, m, :], PB[b][:, :], t)]),
          mode="tm", ntile=6)
    dense([512], xh, 8,
          lambda c, m, b, t: bfree.__setitem__(b, [act(GX[:, m, :], PB[b][:, :], ACT.Silu, t)]))
    u = W.unit()
    for lo, n in ((0, 512), (512, 256)):
        b = bank()
        for k in range(8):
            t = mm3(PB[b][:, 0:n], (u.h[:, k, :], u.l[:, k, :]), (HNh[:, k, lo:lo + n], HNl[:, k, lo:lo + n]), k == 0,
                    k == 7, u.tok, *bfree[b], inc=k == 7)
        bfree[b] = [copy(V, RX[:, lo:lo + n], PB[b][0:32, 0:n], t)]
    W.done(u, P.now)
    dense([512], xtok, 8,
          lambda c, m, b, t: bfree.__setitem__(b, [copy(V if m % 2 else A, PT[:, m, :], PB[b][:, :], t)]),
          mode="tm", ntile=4)
    barrier()

    wp = a(18688, 512, 128)
    tw = load(A, "wpool", wp, I["w_pool"][0].rearrange("g c d -> c g d"))
    pl = a(10496, 2048, 512)
    for g in range(4):
        b = bank()
        for j in range(4):
            if j % 2 == 0:
                w = take()
                pv = rv(w, 0, 2, 512)
            t = mm(PB[b][:, :], PT[:, j, g * 128:(g + 1) * 128], pv[:, j % 2, :], j == 0, j == 3, w.tok, *bfree[b],
                   inc=j % 2 == 1)
            if j % 2 == 1:
                give(w, t)
        bfree[b] = [copy(A, pl[:, g, :], PB[b][:, :], t)]
    for g in range(4):
        b = bank()
        t = mm(PB[b][:, :], wp[:, g, :], pl[:, g, :], True, True, A.now, tw, *bfree[b], inc=True)
        bfree[b] = [vts(MX[:, 4 + g, :], PB[b][:, :], C("pscale", g), None, ALU.mult, None, t)]
    barrier()

    BC = a(10496, 3072, 768)
    E1 = a(13568, 3072, 768)
    wg = ar[0:32, 16640:17152]
    tz = V.do(lambda e: e.memset(wg, 0.0))
    load(A, "wgk", wg[0:16, 0:256], I["w_gk_f"][0], tz)
    tg = load(A, "wgk", wg[16:32, 256:512], I["w_gk_b"][0])
    smask = a(17152, 768)
    tsm = load(A, "scan", smask, I["tabs"][:, TOFF["scan"][0]:TOFF["scan"][0] + 768])
    for c4 in range(4):
        for lo, n in ((0, 512), (512, 256)):
            b = bank()
            t = mm(PB[b][:, 0:n], wg[:, c4 * 128:(c4 + 1) * 128], RX[:, lo:lo + n], True, True, tg, *bfree[b], inc=True)
            t = vts(BC[:, c4, lo:lo + n], PB[b][:, 0:n], C("bgk", c4), None, ALU.add, None, t)
            bfree[b] = [t]
            act(E1[:, c4, lo:lo + n], BC[:, c4, lo:lo + n], ACT.Abs, t)
    f1, fb = a(13568, 3072), a(10496, 3072)
    act(f1, f1, ACT.Exp, scale=-1.0)
    t = act(f1, f1, ACT.Ln, bias=1.0)
    t = stt(fb, fb, 0.0, f1, ALU.min, ALU.subtract, t)
    for c4 in range(4):
        src = BC[:, c4, :]
        dst = E1[:, c4, :]
        if c4 >= 2:
            src, dst = src[:, ::-1], dst[:, ::-1]
        V.do(lambda e, s=src, d=dst: e.tensor_tensor_scan(d, smask, s, 0.0, ALU.mult, ALU.add), tsm)
    BC = E1
    barrier()

    AB = [a(10496, 512), a(11008, 512)]
    mk = a(11520, 1024, 512)
    tm1 = load(A, "mask", mk[:, 0, :], I["tabs"][:, TOFF["maskf"][0]:TOFF["maskf"][0] + 512])
    tm1 = load(A, "mask", mk[:, 1, :], I["tabs"][:, TOFF["maskb"][0]:TOFF["maskb"][0] + 512])
    dec = a(12544, 12)
    X0 = 16640
    KU = a(X0, 768)
    KUT = a(X0 + 768, 768, 128)
    ST = a(X0 + 1536, 2048, 256)
    QM, KM, QB = a(X0 + 3584, 512), a(X0 + 4096, 512), a(X0 + 4608, 512)
    ro = a(X0 + 5120, 512)
    sqo = [a(12576, 512), a(12576, 512)]
    kt3 = KU.rearrange("p (n c) -> p n c", c=64)
    for ht in range(2):
        OB = [bank(), bank()]
        held = tuple(OB)
        for d in range(2):
            barrier()
            cb = d * 2 + ht
            B3 = BC[:, cb, :].rearrange("p (n c) -> p n c", c=64)
            il, im = (63, 31) if d == 0 else (0, 32)
            t = V.do(lambda e, B3=B3, il=il: e.tensor_tensor(
                kt3, B3[:, :, il:il + 1].to_broadcast([128, 12, 64]), B3, ALU.subtract))
            t1 = act(KU, KU, ACT.Exp, t, scale=1.0 / 16)
            act(dec, B3[:, :, il], ACT.Exp, scale=1.0 / 16)
            t = V.do(lambda e, B3=B3, im=im: e.tensor_tensor(
                QM.rearrange("p (n c) -> p n c", c=64), B3[:, 0:8, :],
                B3[:, 0:8, im:im + 1].to_broadcast([128, 8, 64]), ALU.subtract))
            t2 = act(KM, QM, ACT.Exp, t, scale=-1.0 / 16)
            t3 = act(QM, QM, ACT.Exp, scale=1.0 / 16)
            t4 = act(QB, BC[:, cb, 0:512], ACT.Exp, scale=1.0 / 16)
            tku = vtt(KU, KU, KX[:, ht, :], ALU.mult, t1)
            tkm = vtt(KM, KM, KX[:, ht, 0:512], ALU.mult, t2)
            tqm = stt(QM, QM, 0.125, QX[:, ht, :], ALU.mult, ALU.mult, t3)
            tqb = stt(QB, QB, 0.125, QX[:, ht, :], ALU.mult, ALU.mult, t4)
            for j0, nj in ((0, 4), (4, 2)):
                b = bank(held)
                for j in range(nj):
                    t = tp(PB[b][:, j * 128:(j + 1) * 128], KU[:, (j0 + j) * 128:(j0 + j + 1) * 128], tku, *bfree[b],
                           inc=j == nj - 1)
                t = copy(A, KUT[:, j0:j0 + nj, :], PB[b][:, 0:nj * 128].rearrange("p (j c) -> p j c", c=128), t)
                bfree[b] = [t]
            tkt = A.now
            for hl in range(2):
                b = bank(held)
                ps = slice(hl * 64, hl * 64 + 64)
                for j in range(4):
                    js = slice(j * 128, (j + 1) * 128)
                    t = mm(PB[b][:, js], KM[ps, js], QM[ps, js], j == 0, j == 3, tqm, tkm, *bfree[b], inc=j == 3)
                tz = G.do(lambda e, x=AB[hl]: e.memset(x, 0.0))
                t = V.do(lambda e, x=AB[hl], m_=mk[:, d, :], y=PB[b][:, :]: e.copy_predicated(
                    x, m_.bitcast(U32), y), t, tz, tm1)
                bfree[b] = [t]
                for j in range(4):
                    js = slice(j * 128, (j + 1) * 128)
                    h4 = 2 * ht + hl
                    mm(PB[OB[hl]][:, js], VT[:, j, h4 * 128:(h4 + 1) * 128], AB[hl][:, js],
                       d == 0 and j == 0, False, t, *bfree[OB[hl]])
            order = [8, 9, 10, 11] + list(range(0, 7)) if d == 0 else [11, 10, 9, 8] + list(range(7, 0, -1))
            cur = None
            lastslot = 7 if d == 0 else 0
            for i, n in enumerate(order):
                if i % 4 == 0:
                    ub = [bank(held), bank(held)]
                    for i2 in range(i, min(i + 4, len(order))):
                        n2 = order[i2]
                        hh = slice((n2 % 2) * 64, (n2 % 2) * 64 + 64)
                        b = ub[i2 % 2]
                        q2 = (i2 % 4) // 2
                        mm(PB[b][:, q2 * 256:q2 * 256 + 256], KUT[hh, n2 // 2, :],
                           VT[hh, n2 // 2, ht * 256:(ht + 1) * 256], q2 == 0, True, tkt, *bfree[b], inc=True)
                    tu = P.now
                b = ub[i % 2]
                pu = PB[b][:, ((i % 4) // 2) * 256:((i % 4) // 2) * 256 + 256]
                nxt = lastslot if i < 3 else ((i - 3) if d == 0 else 7 - (i - 3))
                if i == 0:
                    t = copy(V, ST[:, nxt, :], pu, tu)
                else:
                    t = stt(ST[:, nxt, :], ST[:, cur, :], dec[:, n:n + 1], pu, ALU.mult, ALU.add, tu)
                bfree[b] = [t]
                cur = nxt
            ts = V.now
            for hl in range(2):
                ps = slice(hl * 64, hl * 64 + 64)
                for n in range(8):
                    ns = slice(n * 64, (n + 1) * 64)
                    t = mm(PB[OB[hl]][:, ns], ST[ps, n, hl * 128:(hl + 1) * 128], QB[ps, ns], False,
                           d == 1 and n == 7, ts, tqb, inc=n == 7)
        barrier()
        for hl in range(2):
            h4 = 2 * ht + hl
            ob = PB[OB[hl]][:, :]
            t = norm_stat(lambda k: ob, 1, 512, sqo, ro, 1.0 / 128, b=bank(held))
            t = vtt(ro, ob, ro, ALU.mult, t)
            bfree[OB[hl]] = [t]
            stt(GX[:, h4, :], ro, C("glan"), GX[:, h4, :], ALU.mult, ALU.mult)
    barrier()
    for c in range(4, 12):
        ada(c)

    def resid(gcol, n0_=0):
        def f(c, m, b, t):
            kk = c * 4 + m
            if gcol is None:
                t = vtt(hk(kk), PB[b][:, :], hk(kk), ALU.add, t)
            else:
                t = stt(hk(kk), PB[b][:, :], gcol(kk), hk(kk), ALU.mult, ALU.add, t)
            bfree[b] = [t]
        return f

    def split_tiles(src, lo, nk=8):
        h_, l_ = r(lo, nk * 512, 512), r(lo + nk * 512, nk * 512, 512)
        toks = [split(h_[:, k, :], l_[:, k, :], src(k)) for k in range(nk)]
        return lambda k: (h_[:, k, :], l_[:, k, :], toks[k])

    barrier()
    mx = split_tiles(lambda k: MX[:, k, :], 6656)
    dense([512, 512], mx, 8, resid(lambda k: M(2, k)))
    barrier()

    def store_out(src):
        toks = []
        for t_ in range(4):
            ob_ = a(16384 + (t_ % 2) * 1024, 1024)
            for h in range(2):
                b = bank()
                for k in range(4):
                    t = tp(PB[b][:, k * 128:(k + 1) * 128], src(4 * h + k)[:, t_ * 128:(t_ + 1) * 128], V.now, A.now,
                           *bfree[b], inc=k == 3)
                prev = [toks[t_ - 2]] if t_ >= 2 else []
                bfree[b] = [copy(A if h else V, ob_[:, h * 512:(h + 1) * 512], PB[b][:, :], t, *prev)]
            toks.append(S.dma(s_out[t_ % 2], counts, lambda e, o=ob_, t_=t_: e.dma_start(
                out[0, t_ * 128:(t_ + 1) * 128, :], o), V.now, A.now))
        S.wait(*toks)

    s_out = [sem("s_out0"), sem("s_out1")]

    def emit_all():
        with nc.Block() as block:
            @block.sync
            def _(eng):
                S.emit(eng)

            @block.tensor
            def _(eng):
                P.emit(eng)

            @block.vector
            def _(eng):
                V.emit(eng)

            @block.scalar
            def _(eng):
                A.emit(eng)

            @block.gpsimd
            def _(eng):
                G.emit(eng)

    def tab2(name, at):
        o, n = TOFF[name]
        v = a(at, n)
        return v, load(A, "u_" + name, v, I["tabs"][:, o:o + n])

    def tab(name, at, *toks, q=None):
        o, n = TOFF[name]
        v = a(at, n)
        return v, load(q or A, "t_" + name, v, I["tabs"][:, o:o + n], *toks)


    HM = a(0, 4096, 512)
    gm2 = SM[:, 64:72]
    vts(gm2, mcol[:, 32:40, 0], 1.0, None, ALU.add, None)
    vtt(gm2, gm2, C("nmlp", 0, 8), ALU.mult)
    rr = a(4608, 512)
    t = norm_stat(hk, 8, 512, [a(5120, 512), a(5632, 512)], rr, 1.0 / 1024)
    norm_apply(hk, lambda k: HM[:, k, :], 8, rr, lambda k: gm2[:, k:k + 1], lambda k: M(3, k), t)
    xs = [a(6144, 1024), a(7168, 1024)]
    s_hm = sem("s_hm")
    s_hm2 = sem("s_hm2")
    th = []
    for t_ in range(4):
        for h in range(2):
            b = bank()
            for k in range(4):
                t = tp(PB[b][:, k * 128:(k + 1) * 128], HM[:, 4 * h + k, t_ * 128:(t_ + 1) * 128], V.now, A.now,
                       *bfree[b], inc=k == 3)
            prev = [th[t_ - 2]] if t_ >= 2 else []
            bfree[b] = [copy(A if h else V, xs[t_ % 2][:, h * 512:(h + 1) * 512], PB[b][:, :], t, *prev)]
        th.append(A.dma([s_hm, s_hm2][t_ % 2], counts, lambda e, t_=t_: e.dma_start(
            hm_d[t_ * 128:(t_ + 1) * 128, :], xs[t_ % 2]), V.now, A.now))

    wr = a(4096, 256, 32)
    br = ar[0:1, 4352:4384]
    load(A, "router", wr, I["w_router"][0].rearrange("(j p) n -> p j n", p=128), P.now)
    twr = load(A, "router", br, I["b_router"])
    tri, t1 = tab("tri", 8192)
    iota, t2 = tab("iota", 8320)
    tokc, t3 = tab("tok", 8448)
    pmod, t4 = tab("pmod", 8452)
    selc, t5 = tab("sel", 8460)
    ttab = [t1, t2, t3, t4, t5]
    bl = bank()
    LGp = PB[bl][:, 0:128].rearrange("p (t e) -> p t e", e=32)
    for t_ in range(4):
        mm(LGp[:, t_, :], ones[0:1, :], br, t_ == 0, False, twr, *bfree[bl])
        for k in range(8):
            t = mm(LGp[:, t_, :], HM[:, k, t_ * 128:(t_ + 1) * 128], wr[:, k, :], False, k == 7, A.now, inc=k == 7)
    o = 8500
    LG = a(o, 128, 32)
    MXV = a(o + 128, 32, 8)
    MXI = a(o + 160, 32, 8).bitcast(U32)
    IDF = a(o + 192, 32, 8)
    ID4 = a(o + 224, 16, 4)
    SEL = a(o + 240, 128, 32)
    RK = a(o + 368, 128, 32)
    RBK = a(o + 496, 128, 32)
    OFF = a(o + 624, 128, 32)
    BLK = a(o + 752, 128, 32)
    CNT = a(o + 880, 32)
    NX = a(o + 912, 32)
    XI = a(o + 944, 32)
    T1 = a(o + 976, 128, 32)
    OH = a(o + 1104, 512)
    T2 = a(o + 1616, 512)
    T3 = a(o + 2128, 512)
    BK4 = a(o + 2640, 16)
    OF4 = a(o + 2656, 16)
    XE = a(o + 2672, 16)
    SS = a(o + 2688, 4)
    LH = [a(o + 2700, 128), a(o + 2828, 128)]
    RH = [a(o + 2956, NBLK), a(o + 3004, NBLK)]
    DF = a(o + 3056, 16)
    K0 = 20000
    IDXI = a(K0, NBLK).bitcast(I32)
    DEST = a(K0 + 48, 16).bitcast(I32)
    WTS = a(K0 + 64, 16)
    SI = a(K0 + 80, 32).bitcast(I32)
    IDC = a(K0 + 112, 1).bitcast(I32)
    SELB = a(K0 + 120, 16).bitcast(BF16)
    SELX = a(K0 + 136, 8).bitcast(BF16)
    SELJ = a(K0 + 144, 64).bitcast(BF16)
    BP = BPT[:, :].bitcast(BF16)
    t = copy(V, LG, LGp, t)
    bfree[bl] = [t]
    for t_ in range(4):
        V.do(lambda e, t_=t_: e.max(MXV[:, t_, :], LG[:, t_, :]))
        V.do(lambda e, t_=t_: e.max_index(MXI[:, t_, :], MXV[:, t_, :], LG[:, t_, :]))
    copy(V, IDF, MXI)
    copy(V, ID4, IDF[:, :, 0:4])
    W4 = WTS.rearrange("p (t k) -> p t k", k=4)
    t = vtt(W4, MXV[:, :, 0:4], MXV[:, :, 0:1].to_broadcast([128, 4, 4]), ALU.subtract)
    t = act(WTS, WTS, ACT.Exp, t)
    V.do(lambda e: e.tensor_reduce(SS, W4, AX.X, ALU.add), t)
    V.do(lambda e: e.reciprocal(SS, SS))
    vtt(W4, W4, SS.unsqueeze(2).to_broadcast([128, 4, 4]), ALU.mult)
    OH3 = OH.rearrange("p (i e) -> p i e", e=32)
    vtt(OH3, iota[:, 0:32].unsqueeze(1).to_broadcast([128, 16, 32]),
        a(o + 224, 16).unsqueeze(2).to_broadcast([128, 16, 32]), ALU.is_equal, *ttab)
    t = V.do(lambda e: e.tensor_reduce(SEL, OH.rearrange("p (t k e) -> p t e k", k=4, e=32), AX.X, ALU.add))
    b = bank()
    for t_ in range(4):
        mm(PB[b][:, t_ * 32:(t_ + 1) * 32], tri, SEL[:, t_, :], t_ == 0, t_ == 0, t, *bfree[b])
        for u_ in range(t_):
            mm(PB[b][:, t_ * 32:(t_ + 1) * 32], ones, SEL[:, u_, :], False, u_ == t_ - 1)
    for u_ in range(4):
        t = mm(PB[b][:, 128:160], ones, SEL[:, u_, :], False, u_ == 3, inc=u_ == 3)
    RKf, RBf, OFf, BKf, T1f = (a(o + 368, 128), a(o + 496, 128), a(o + 624, 128), a(o + 752, 128), a(o + 976, 128))
    copy(V, RKf, PB[b][:, 0:128], t)
    bfree[b] = [copy(V, CNT, PB[b][:, 128:160])]
    vts(NX, CNT, 128.5, None, ALU.is_gt, None)
    for lim in (256.5, 384.5):
        stt(NX, CNT, lim, NX, ALU.is_gt, ALU.add)
    V.do(lambda e: e.tensor_tensor_scan(XI, ones[:, 0:32], NX, 0.0, ALU.mult, ALU.add))
    vts(RBf, RKf, 127.5, None, ALU.is_gt, None)
    for lim in (255.5, 383.5):
        stt(RBf, RKf, lim, RBf, ALU.is_gt, ALU.add)
    stt(OFf, RBf, -128.0, RKf, ALU.mult, ALU.add)
    vtt(NX, XI, NX, ALU.subtract)
    vtt(NX, NX, iota[:, 0:32], ALU.subtract)
    vts(NX, NX, 31.0, None, ALU.add, None)
    vts(T1f, RBf, 0.5, None, ALU.is_gt, None)
    vtt(T1, T1, NX.unsqueeze(1).to_broadcast([128, 4, 32]), ALU.mult)
    vtt(T1f, T1f, RBf, ALU.add)
    vtt(BLK, T1, iota[:, 0:32].unsqueeze(1).to_broadcast([128, 4, 32]), ALU.add)
    OH4 = OH.rearrange("p (t k e) -> p t k e", k=4, e=32)
    for src, tmp, res in ((BLK, T2, BK4), (OFF, T3, OF4)):
        vtt(tmp.rearrange("p (t k e) -> p t k e", k=4, e=32), OH4,
            src.unsqueeze(2).to_broadcast([128, 4, 4, 32]), ALU.mult)
        V.do(lambda e, tmp=tmp, res=res: e.tensor_reduce(res, tmp.rearrange("p (i e) -> p i e", e=32), AX.X, ALU.add))
    stt(DF, BK4, 128.0, OF4, ALU.mult, ALU.add)
    copy(V, DEST, DF)
    t = vtt(T2.rearrange("p (j e) -> p j e", e=32), iota[:, 0:16].unsqueeze(2).to_broadcast([128, 16, 32]),
            XI.unsqueeze(1).to_broadcast([128, 16, 32]), ALU.is_ge)
    V.do(lambda e: e.tensor_reduce(XE, T2.rearrange("p (j e) -> p j e", e=32), AX.X, ALU.add))
    vts(XE, XE, 31.0, None, ALU.min, None)
    copy(V, SI[:, 0:16], XE)
    t_si = copy(V, SI[:, 16:17], XI[:, 31:32])
    t_selb = copy(V, SELB, selc)
    vts(SELX, XE, pmod[:, 0:1], None, ALU.is_equal, None)
    b = bank()
    tp_ = [None, None]
    for i in range(16):
        w_ = [tp_[i % 2]] if tp_[i % 2] else []
        vts(LH[i % 2], iota, OF4[:, i:i + 1], None, ALU.is_equal, None, *w_)
        t = vts(RH[i % 2], iota[:, 0:NBLK], BK4[:, i:i + 1], tokc[:, i // 4:i // 4 + 1], ALU.is_equal, ALU.mult)
        tp_[i % 2] = mm(PB[b][:, 0:NBLK], LH[i % 2], RH[i % 2], i == 0, i == 15, t, *bfree[b], inc=True)
    t_idx = copy(V, IDXI, PB[b][:, 0:NBLK], tp_[1])
    bfree[b] = [t_idx]
    raw = ar[0:96, 12000:15072]
    part = ar[0:96, 15072:16608].bitcast(BF16)
    for j in range(3):
        load(A, "bias", raw[32 * j:32 * j + 32, 0:2048], I["b_gu"][0])
        tb = load(A, "bias", raw[32 * j:32 * j + 32, 2048:3072], I["b_down"][0])
    for j in range(3):
        t = copy(A, part, raw, tb, V.now)
        copy(A, BP[32 * j:32 * j + 32, :], part[32 * j:32 * j + 32, :])
        if j < 2:
            vtt(raw, raw, part, ALU.subtract, t)
    barrier()

    XG = [a(0, 1024), a(1024, 1024)]
    XTh = [r(2048, 1024, 128), r(3072, 1024, 128)]
    XTl = [r(4096, 1024, 128), r(5120, 1024, 128)]
    GT = [a(6144, 512), a(6656, 512)]
    UT = [a(7168, 512), a(7680, 512)]
    ZT = [a(8192, 512), a(8704, 512)]
    AC = [a(9216, 512), a(9728, 512)]
    ATh = [r(10240, 512, 128), r(10752, 512, 128)]
    ATl = [r(11264, 512, 128), r(11776, 512, 128)]
    YB = [a(12288, 1024), a(13312, 1024)]
    s_g = [sem("s_g0"), sem("s_g1")]
    s_y = [sem("s_y0"), sem("s_y1")]

    class Block:

        def __init__(self, v, ac, p, w):
            self.V, self.A, self.P, self.W = v, ac, p, w
            self.bf = [[] for _ in range(8)]

        def halves(self, b, hi, lo, t, *toks):
            hf = hi.rearrange("p k c -> p (k c)")
            lf = lo.rearrange("p k c -> p (k c)")
            t1 = self.A.do(lambda e: e.activation(hf, PB[b][:, :], ACT.Copy), t, *toks)
            t2 = self.V.do(lambda e: e.tensor_tensor(lf, PB[b][:, :], hf.bitcast(F32), ALU.subtract), t1)
            self.bf[b] = [t2]
            return t2

        def xturn(self, i, tg_):
            out_ = []
            for h in range(2):
                for k in range(4):
                    kk = 4 * h + k
                    t = self.P.do(lambda e, h=h, k=k, kk=kk: e.transpose(
                        PB[h][:, k * 128:(k + 1) * 128], XG[i][:, kk * 128:(kk + 1) * 128], ident),
                        tg_, *self.bf[h], inc=k == 3)
                out_.append(self.halves(h, XTh[i][:, 4 * h:4 * h + 4, :], XTl[i][:, 4 * h:4 * h + 4, :], t))
            return out_

        def bias(self, b, lhs, c0, *toks):
            self.P.do(lambda e: e.matmul(PB[b][:, :], lhs, BP[0:96, c0:c0 + 512], start=True, stop=False,
                                         skip_group_check=True), *toks, *self.bf[b], inc=False)

        def run(self, i, txt, bias_lhs, tbias, mid, before, prev_store):
            V_, A_, P_ = self.V, self.A, self.P
            done, ta = [None, None], [None, None]

            def aturn(h):
                for k in range(4):
                    t = P_.do(lambda e, k=k: e.transpose(
                        PB[h][:, k * 128:(k + 1) * 128], AC[h][:, k * 128:(k + 1) * 128], ident),
                        done[h], *self.bf[h], inc=k == 3)
                ta[h] = self.halves(h, ATh[h], ATl[h], t)

            def down(h):
                for k in range(4):
                    u = self.W.unit()
                    for n in range(2):
                        ns = slice(n * 512, (n + 1) * 512)
                        t = mm3(PB[6 + n][:, :], (ATh[h][:, k, :], ATl[h][:, k, :]), (u.h[:, 0, ns], u.l[:, 0, ns]),
                                False, h == 1 and k == 3, ta[h], u.tok, inc=n == 1, q=P_)
                    self.W.done(u, t)
                return t

            def finish():
                t = down(1)
                for n in range(2):
                    t2 = A_.do(lambda e, n=n: e.activation(YB[i][:, n * 512:(n + 1) * 512], PB[6 + n][:, :], ACT.Copy),
                               t, *prev_store)
                    self.bf[6 + n] = [t2]
                return [t2]

            for h in range(2):
                for g in range(2):
                    b = 2 + 2 * h + g
                    self.bias(b, bias_lhs, g * 1024 + h * 512, tbias)
                    for u_ in range(4):
                        u = self.W.unit()
                        for k in range(2):
                            kk = 2 * u_ + k
                            t = mm3(PB[b][:, :], (XTh[i][:, kk, :], XTl[i][:, kk, :]), (u.h[:, k, :], u.l[:, k, :]),
                                    False, kk == 7, u.tok, *txt, inc=k == 1, q=P_)
                        if u_ < 3:
                            self.W.done(u, t)
                        if (h, g, u_) == (1,0,1):
                            aturn(0)
                        if (h, g, u_) == (1,1,1):
                            mid()
                        if (h, g, u_) == (0,0,1) and before:
                            before[0](1)
                    t_last = t
                    if g == 0:
                        tg = V_.do(lambda e, h=h, b=b: e.tensor_scalar(GT[h], PB[b][:, :], 7.0, None, ALU.min), t)
                        self.bf[b] = [tg]
                        tz = A_.do(lambda e, h=h: e.activation(ZT[h], GT[h], ACT.Sigmoid, scale=1.702), tg)
                    else:
                        tu = V_.do(lambda e, h=h, b=b: e.tensor_scalar(UT[h], PB[b][:, :], 7.0, -7.0, ALU.min, ALU.max), t)
                        self.bf[b] = [tu]
                        V_.do(lambda e, h=h: e.scalar_tensor_tensor(
                            out=UT[h], in0=UT[h], scalar=1.0, in1=GT[h], op0=ALU.add, op1=ALU.mult))
                        done[h] = V_.do(lambda e, h=h: e.tensor_tensor(AC[h], UT[h], ZT[h], ALU.mult), tz, P_.now)
                    self.W.done(u, t_last)
                    if (h, g) == (0, 0) and before:
                        before[1]()
            for n in range(2):
                self.bias(6 + n, bias_lhs, 2048 + n * 512)
            down(0)
            return [aturn, finish]

    def gather(q, cnt, i, idx, *toks):
        return q.dma(s_g[i], cnt, lambda e: e.indirect_dma_start(
            out=XG[i], out_offset=None, in_=hm_d, in_offset=bass.IndirectOffsetOnAxis(ap=idx, axis=0)), *toks)

    W.add(s_more, [14336 + 1024 * n for n in range(5)] + [20480 + 1024 * n for n in range(3)],
          *[q.now for q in QS], t_zero)
    stream = Block(V, A, P, W)
    tgs = [gather(G, counts, 0, IDXI[:, 0:1], *th[2:]), gather(G, counts, 1, IDXI[:, 1:2])]
    txt = stream.xturn(0, tgs[0])
    tstore = [[], []]

    def stored(e_, fin):
        i = e_ % 2
        ty = fin()
        tstore[i] = [A.dma(s_y[i], counts, lambda e: e.dma_start(y_d[e_ * 128:(e_ + 1) * 128, :], YB[i]), *ty)]

    rest = None
    for e_ in range(32):
        i = e_ % 2
        nxt = [None]

        def mid():
            if e_ + 1 < 32:
                nxt[0] = stream.xturn(1 - i, tgs[1 - i])
                if e_ + 2 < 32:
                    tgs[i] = gather(G, counts, i, IDXI[:, e_ + 2:e_ + 3], P.now)

        before = None
        if rest:
            before = [rest[0], lambda e_=e_, fin=rest[1]: stored(e_ - 1, fin)]
        rest = stream.run(i, txt, SELB[0:96, e_:e_ + 1].to_broadcast([96, 128]), t_selb, mid, before, tstore[i])
        txt = nxt[0]
    rest[0](1)
    stored(31, rest[1])
    W.drop(s_more)
    for b in range(8):
        bfree[b] = stream.bf[b]
    A.wait(*tstore[0], *tstore[1])
    for q in (S, V, G, P):
        q.wait(*tstore[0], *tstore[1])
    barrier()
    S.wait(*[q.now for q in QS])

    for q in (S, G):
        q.wait(t_zero)
    L = {n: Queue(sem("s_l" + n), n in "vag") for n in "vagps"}
    lc = {}
    s_lw = [sem(f"s_lw{n}") for n in range(min(12, NRING))]
    s_lg, s_lst = sem("s_lgather"), sem("s_lst")
    regs = {}
    wgu, wdn = I["w_gu"][0], I["w_down"][0]
    LW = Stream(L["s"], L["a"], L["v"], lc, s_lw)
    for n in range(4):
        c0 = (n % 2) * 1024 + (n // 2) * 512
        for k in range(0, 8, 2):
            LW.plan(lambda c0=c0, k=k: wgu[bass.ds(regs["e"], 1), k * 128:(k + 2) * 128, c0:c0 + 512].rearrange(
                "o (j p) n -> p (o j) n", p=128), 2, 512)
    for k in range(0, 8):
        LW.plan(lambda k=k: wdn[bass.ds(regs["e"], 1), k * 128:(k + 1) * 128, :].rearrange(
            "o (j p) n -> p (o j) n", p=128), 1, 1024)
    LW.fetch()
    tic = L["g"].do(lambda e: e.tensor_copy(IDC, IDXI[:, bass.ds(regs["g"] + 32, 1)]))
    tlg = L["g"].dma(s_lg, lc, lambda e: e.indirect_dma_start(
        out=XG[0], out_offset=None, in_=hm_d, in_offset=bass.IndirectOffsetOnAxis(ap=IDC, axis=0)), tic)
    tsel = L["v"].do(lambda e: e.tensor_copy(SELJ[0:96, :], SELX[0:96, bass.ds(regs["v"], 1)].to_broadcast([96, 128])))
    extra = Block(L["v"], L["a"], L["p"], LW)
    tx_ = extra.xturn(0, tlg)
    rest = extra.run(0, tx_, SELJ[0:96, :], tsel, lambda: None, None, [])
    rest[0](1)
    ty = rest[1]()
    y3 = y_d.rearrange("(b p) d -> b p d", p=128)
    L["s"].dma(s_lst, lc, lambda e: e.dma_start(
        y3[bass.ds(regs["s"] + 32, 1), :, :].rearrange("o p d -> p (o d)"), YB[0]), *ty)
    per = dict(lc)
    for q in L.values():
        if q.n:
            per[q.sem] = q.n
    for q in L.values():
        for s_, n in per.items():
            q.ops.append((0, s_, n))

    s_dum = {key: sem("s_after_" + key) for key in "vagps"}

    def looped(key):
        def f(e):
            n_ = e.value_load(SI[0:1, 16:17], min_val=0, max_val=15)
            with e.If(n_ > 0):
                with e.Fori(0, n_) as j:
                    regs[key] = j
                    if key == "s":
                        regs["e"] = e.value_load(SI[0:1, bass.ds(j, 1)], min_val=0, max_val=31)
                    L[key].emit(e, lambda s_, v_: j * per[s_] + v_, s_dum[key])
        return f

    for q, key in ((S, "s"), (V, "v"), (A, "a"), (G, "g"), (P, "p")):
        q.ops.append((3, looped(key), None))

    l_in, l_out = I["ret_s5_w_in_2"][0], I["ret_s5_w_out_2"][0]
    for c in range(5):
        plan_cols(l_in, 8, c * 512, 512)
    plan_cols(I["s5_w_glu_2"][0], 4, 0, 512)
    HCH = [512, 512, 256, 128]

    def plan_ffn(l):
        for f in range(2):
            at_ = f * 1408
            for n in HCH:
                plan_cols(I["ffn_w_gate_2"][l], 8, at_, n)
                plan_cols(I["ffn_w_up_2"][l], 8, at_, n)
                at_ += n
            for c in range(2):
                plan_cols(I["ffn_w_down_2"][l][f * 1408:(f + 1) * 1408, :], 11, c * 512, 512)

    def plan_ple(l):
        for c in range(2):
            plan_cols(I["ple_w_gate_2"][l], 8, c * 512, 512)
        for c in range(2):
            plan_cols(I["ple_w_proj_2"][l], 2, c * 512, 512)

    for c in range(2):
        plan_cols(l_out, 8, c * 512, 512)
    plan_ffn(0)
    plan_ple(0)
    for c in range(6):
        plan_cols(I["diff_w_qkv_2"][0], 8, c * 512, 512)
    for c in range(2):
        plan_cols(I["diff_w_o_2"][0], 8, c * 512, 512)
    plan_ffn(1)
    plan_ple(1)

    lent = s_ring[10:]
    W.drop(lent)
    W.fetch()

    def xw(lo, n, shape=None):
        v = place(ARENA + 10240 + lo, n)
        return v if shape is None else v.rearrange("p (a b) -> p a b", b=shape)

    RW = [a(0, 1024), a(1024, 1024), a(2048, 1024), a(3072, 1024)]
    YA = [a(4096, 1024), a(5120, 1024)]
    s_rw = [sem(f"s_rw{k}") for k in range(4)]
    rfree = [[], [], [], []]
    yfree = [[], []]
    for t_ in range(4):
        ya = YA[t_ % 2]
        for k in range(4):
            i = t_ * 4 + k
            tg = G.dma(s_rw[k], counts, lambda e, i=i, k=k: e.indirect_dma_start(
                out=RW[k], out_offset=None, in_=y_d,
                in_offset=bass.IndirectOffsetOnAxis(ap=DEST[:, i:i + 1], axis=0)), *rfree[k])
            if k == 0:
                t = vts(ya, RW[k], WTS[:, i:i + 1], None, ALU.mult, None, tg, *yfree[t_ % 2])
            else:
                t = stt(ya, RW[k], WTS[:, i:i + 1], ya, ALU.mult, ALU.add, tg)
            rfree[k] = [t]
        for h in range(2):
            b = bank()
            for k in range(4):
                kk = 4 * h + k
                tt_ = tp(PB[b][:, k * 128:(k + 1) * 128], ya[:, kk * 128:(kk + 1) * 128], t, *bfree[b], inc=k == 3)
            for k in range(4):
                kk = 4 * h + k
                hs = hk(kk)[:, t_ * 128:(t_ + 1) * 128]
                t3 = stt(hs, PB[b][:, k * 128:(k + 1) * 128], M(5, kk), hs, ALU.mult, ALU.add, tt_)
            bfree[b] = [t3]
        yfree[t_ % 2] = [P.now]
    barrier()


    HNh, HNl = r(0, 4096, 512), r(4096, 4096, 512)
    hn_tok = [None] * 8

    def norm(gain, to_h=False):
        t = norm_stat(hk, 8, 512, [a(21504, 512), a(22016, 512)], a(22528, 512), 1.0 / 1024, V.now)
        if to_h:
            norm_apply(hk, hk, 8, a(22528, 512), gain, None, t)
        else:
            hn_tok[:] = norm_split(hk, lambda k: HNh[:, k, :], lambda k: HNl[:, k, :], 8, a(22528, 512), gain, None,
                                   [a(23040, 512), a(23552, 512)], t)

    def hn(k):
        return HNh[:, k, :], HNl[:, k, :], hn_tok[k]

    def hn_tm(k, m):
        return HNh[:, k, m * 128:(m + 1) * 128], HNl[:, k, m * 128:(m + 1) * 128], hn_tok[k]

    norm(lambda k: C("nfin", k), True)

    def ev(dst, f=None, dve=None):
        def g(c, m, b, t):
            if f is not None:
                bfree[b] = [act(dst(c, m), PB[b][:, 0:dst(c, m).shape[-1]], f, t)]
            else:
                bfree[b] = [copy(V if m % 2 else A, dst(c, m), PB[b][:, 0:dst(c, m).shape[-1]], t)]
        return g

    barrier()
    trot = []
    rotc = {}
    for nm, at in (("cos", 0), ("sin", 512), ("rot", 1024)):
        o_, n_ = TOFF[nm]
        rotc[nm] = BPT[:, at:at + n_]
        trot.append(load(A, "t_" + nm, rotc[nm], I["tabs"][:, o_:o_ + n_]))
    rtmp = a(20480, 512)

    def rotated(dst):
        def job(x, t):
            b = bank()
            tm = mm(PB[b][:, :], rotc["rot"], x, True, True, t, *trot, *bfree[b], inc=True)
            t = vtt(rtmp, PB[b][:, :], rotc["sin"], ALU.mult, tm, *trot)
            bfree[b] = [t]
            vtt(x, x, rotc["cos"], ALU.mult)
            vtt(x, x, rtmp, ALU.add)
            yield

        def g(c, m, b, t):
            t = copy(A, dst(c, m), PB[b][:, :], t)
            bfree[b] = [t]
            jobs.append(job(dst(c, m), t))
        return g

    norm(lambda k: C("mix0", k))
    Q3 = a(8192, 2048, 512)
    K3 = a(10240, 2048, 512)
    V3 = a(12288, 2048, 512)
    G3 = a(14336, 2048, 512)
    MX = a(14336, 4096, 512)
    U3 = a(18432, 2048, 512)
    f0 = 20992
    t_n = [V.now, A.now, P.now]
    lraw = ar[0:32, f0:f0 + 260]
    load(A, "s5p", lraw[:, 0:64], I["s5_lambda_re_2"][0], *t_n)
    load(A, "s5p", lraw[:, 64:128], I["s5_lambda_re_2"][0])
    load(A, "s5p", lraw[:, 128:192], I["s5_lambda_im_2"][0])
    load(A, "s5p", lraw[:, 192:256], I["s5_lambda_im_2"][0])
    dl = a(f0 + 260, 32)
    t_sp = load(A, "s5p", dl, I["s5_log_step_2"][0:1, :].to_broadcast([128, 32]))
    B0 = a(16384, 512, 16)
    BI = a(16896, 512, 16)
    for lo, dst, nm in ((0, B0, "s5_b_re_2"), (64, B0, "s5_b_im_2"), (64, BI, "s5_b_re_2"), (0, BI, "s5_b_im_2")):
        t_b = load(A, "s5b", dst[lo:lo + 64, :, :], I[nm][0].rearrange("g p c -> p g c"))
    cr = a(23244, 512, 128)
    for lo, nm in ((0, "s5_c_re_2"), (64, "s5_c_im_2")):
        t_c = load(A, "s5c", cr[:, :, lo:lo + 64], I[nm][0].rearrange("(j g) c p -> (g c) j p", g=8))
    jmT, t_jm = tab("jm", f0 + 300)
    b16, t_b16 = tab("b16", f0 + 428)
    o = f0 + 556

    def sm(n=1):
        nonlocal o
        r = a(o, 32 * n)
        o += 32 * n
        return r

    LR, LI, DL, RE, TH, XX, KI, S_, Cc, RHO, R8, DD, FR, FI, TA, TB = (sm() for _ in range(16))
    AR, AI = sm(9), sm(9)
    TH8, WC, WS = sm(), sm(), sm()
    C1 = float(np.float32(6.28125))
    C2 = float(np.float32(TWO_PI - C1))
    C3 = float(TWO_PI - C1 - C2)
    tmp = a(22732, 512, 16)
    PA, PI_ = a(17408, 512, 16), a(17920, 512, 16)
    QA, QI = B0, BI
    KK = xw(0, 4096, 128)
    MG = xw(4096, 4096)
    t_par = {}

    def sincos(x, s, c):
        ki = KI.bitcast(I32)
        vts(XX, x, 1.0 / TWO_PI, None, ALU.mult, None)
        copy(V, ki, XX)
        copy(V, XX, ki)
        vts(TA, x, 1.0, None, ALU.mult, None)
        for cst in (C1, C2, C3):
            stt(TA, XX, -cst, TA, ALU.mult, ALU.add)
        t = vts(TA, TA, 3.1415925, -3.1415925, ALU.min, ALU.max)
        act(s, TA, ACT.Sin, t)
        t = act(TB, TA, ACT.Sin, scale=0.5)
        yield
        vtt(TB, TB, TB, ALU.mult, t)
        vts(c, TB, -2.0, 1.0, ALU.mult, ALU.add)

    def sl(x, i):
        return x[:, i * 32:(i + 1) * 32]

    def bc(x):
        return x.unsqueeze(2).to_broadcast([128, 32, 16])

    def power(dst, X, XI_, i, sign):
        vtt(tmp, XI_, bc(sl(AI, i)), ALU.mult)
        vtt(dst, X, bc(sl(AR, i)), ALU.mult)
        vtt(dst, dst, tmp, ALU.add if sign > 0 else ALU.subtract)

    def s5_prep():
        yield
        b = bank()
        tp(PB[b][:, 0:32], lraw[:, 0:128], t_sp, *bfree[b])
        t = tp(PB[b][:, 32:64], lraw[:, 128:256], inc=True)
        copy(V, LR, PB[b][:, 0:32], t)
        bfree[b] = [copy(V, LI, PB[b][:, 32:64])]
        t = act(DL, dl, ACT.Exp, t_sp)
        vtt(RE, LR, DL, ALU.mult, t)
        t = vtt(TH, LI, DL, ALU.mult)
        act(RHO, RE, ACT.Exp, t)
        t_par["r8"] = t_r = act(R8, RE, ACT.Exp, scale=8.0)
        vts(TH8, TH, 8.0, None, ALU.mult, None)
        yield
        yield from sincos(TH, S_, Cc)
        yield from sincos(TH8, WS, WC)
        yield
        V.do(lambda e: e.memset(sl(AR, 0), 1.0))
        V.do(lambda e: e.memset(sl(AI, 0), 0.0))
        vtt(sl(AR, 1), RHO, Cc, ALU.mult, t_r)
        vtt(sl(AI, 1), RHO, S_, ALU.mult)
        for i in range(2, 9):
            h1, h2 = i // 2, i - i // 2
            vtt(TA, sl(AR, h1), sl(AR, h2), ALU.mult)
            vtt(TB, sl(AI, h1), sl(AI, h2), ALU.mult)
            vtt(sl(AR, i), TA, TB, ALU.subtract)
            vtt(TA, sl(AR, h1), sl(AI, h2), ALU.mult)
            vtt(TB, sl(AI, h1), sl(AR, h2), ALU.mult)
            vtt(sl(AI, i), TA, TB, ALU.add)
            if i % 2:
                yield
        vtt(TA, LR, LR, ALU.mult)
        vtt(TB, LI, LI, ALU.mult)
        vtt(DD, TA, TB, ALU.add)
        V.do(lambda e: e.reciprocal(DD, DD))
        vts(XX, sl(AR, 1), -1.0, None, ALU.add, None)
        vtt(TA, XX, LR, ALU.mult)
        vtt(TB, sl(AI, 1), LI, ALU.mult)
        vtt(FR, TA, TB, ALU.add)
        yield
        vtt(TA, sl(AI, 1), LR, ALU.mult)
        vtt(TB, XX, LI, ALU.mult)
        vtt(FI, TA, TB, ALU.subtract)
        vtt(FR, FR, DD, ALU.mult)
        vtt(FI, FI, DD, ALU.mult)
        vts(BI[0:64, :, :], BI[0:64, :, :], -1.0, None, ALU.mult, None, t_b)
        yield
        vtt(tmp, BI, bc(FI), ALU.mult)
        vtt(PA, B0, bc(FR), ALU.mult)
        vtt(PA, PA, tmp, ALU.add)
        yield
        vtt(tmp, B0, bc(FI), ALU.mult)
        vtt(PI_, BI, bc(FR), ALU.mult)
        vtt(PI_, PI_, tmp, ALU.subtract)
        yield
        b = bank()
        for j in range(4):
            t = tp(PB[b][:, j * 128:(j + 1) * 128], cr[:, j, :], t_c, *bfree[b], inc=j == 3)
        t = copy(V, QA.rearrange("p g c -> p (g c)"), PB[b][:, :], t)
        bfree[b] = [t]
        t = V.do(lambda e: e.tensor_scalar(QA[64:128, :, :], QA[64:128, :, :], -1.0, None, ALU.mult))
        yield
        b = bank()
        t = mm(PB[b][:, :], jmT, QA.rearrange("p g c -> p (g c)"), True, True, t, t_jm, *bfree[b], inc=True)
        bfree[b] = [copy(V, QI.rearrange("p g c -> p (g c)"), PB[b][:, :], t)]
        PAf = PA.rearrange("p g c -> p (g c)")
        QT = xw(4096, 1024).rearrange("p (i g c) -> p i g c", g=32, c=16)
        power(QT[:, 0], QA, QI, 0, -1)
        yield
        for tau in range(8):
            q_ = QT[:, tau % 2].rearrange("p g c -> p (g c)")
            b = bank()
            for j in range(4):
                t = mm(PB[b][:, j * 128:(j + 1) * 128], PAf[:, j * 128:(j + 1) * 128], q_[:, j * 128:(j + 1) * 128],
                       j == 0, j == 3, V.now, *bfree[b], inc=j == 3)
            if tau < 7:
                power(QT[:, (tau + 1) % 2], QA, QI, tau + 1, -1)
            bfree[b] = [vtt(KK[:, tau * 4:tau * 4 + 4, :], PB[b][:, :].rearrange("p (j c) -> p j c", c=128),
                            b16.unsqueeze(1).to_broadcast([128, 4, 128]), ALU.mult, t, t_b16)]
            if tau == 0:
                for j in range(4):
                    stt(KK[:, j, :], ident, C("s5d", j), KK[:, j, :], ALU.mult, ALU.add)
            yield
        PM4 = MG.rearrange("p (g s c) -> p g s c", s=8, c=16)
        for s_ in range(8):
            power(PM4[:, :, s_, :], PA, PI_, 7 - s_, 1)
            yield
        t_pm = V.now
        for g0 in range(0, 32, 4):
            b = bank()
            for g in range(4):
                t = tp(PB[b][:, g * 128:(g + 1) * 128], MG[:, (g0 + g) * 128:(g0 + g + 1) * 128], t_pm, *bfree[b],
                       inc=g == 3)
            bfree[b] = [copy(A, MG[:, g0 * 128:(g0 + 4) * 128], PB[b][:, :], t)]
            if g0 % 8:
                yield

    slow.append(s5_prep())
    dense([512], hn, 8, rotated(lambda c, m: Q3[:, m, :]))
    dense([512], hn, 8, rotated(lambda c, m: K3[:, m, :]))
    dense([512], hn_tm, 8, ev(lambda c, m: V3[:, m, :]), mode="tm")
    dense([512], hn, 8, ev(lambda c, m: G3[:, m, :], ACT.Silu))
    dense([512], hn, 8, ev(lambda c, m: U3[:, m, :]))
    finish_jobs()
    barrier()

    DT, t4 = tab("dt", 6272)
    KD, t5 = tab("kdec", 7296)
    QD_, t6 = tab("qdec", 3200)
    CD, t7 = tab("cdec", 7936)
    B64, t8 = tab("b64", 7808)
    QD = a(4224, 2048, 512)
    t = vtt(QD.rearrange("p a (c t) -> p a c t", t=128), Q3.rearrange("p a (c t) -> p a c t", t=128),
            QD_.rearrange("p (a t) -> p a t", t=128).unsqueeze(2).to_broadcast([128, 4, 4, 128]), ALU.mult, t6)
    KT = a(1664, 1536, 512)
    barrier()
    for ch in range(3):
        b = bank()
        for pr in range(4):
            t = tp(PB[b][:, pr * 128:(pr + 1) * 128], K3[:, pr, ch * 128:(ch + 1) * 128], *bfree[b], inc=pr == 3)
        bfree[b] = [vtt(KT[:, ch, :], PB[b][:, :], KD, ALU.mult, t, t5)]
    RS = a(0, 1536).rearrange("p (c a e) -> p c a e", a=4, e=128)
    for ch in range(3):
        b = bank()
        for pr in range(4):
            t = mm(PB[b][:, pr * 128:(pr + 1) * 128], KT[:, ch, pr * 128:(pr + 1) * 128],
                   V3[:, ch, pr * 128:(pr + 1) * 128], pr == 0, pr == 3, V.now, *bfree[b], inc=pr == 3)
        for pr in range(4):
            pu = PB[b][:, pr * 128:(pr + 1) * 128]
            if ch == 0:
                t = copy(V, RS[:, 0, pr, :], pu, t)
            else:
                t = stt(RS[:, ch, pr, :], RS[:, ch - 1, pr, :], CD[:, pr:pr + 1], pu, ALU.mult, ALU.add, t, t7)
        bfree[b] = [t]
    t_rs = V.now
    SMs = [a(3200, 512), a(3712, 512)]
    OTs = [a(1664, 512), a(2176, 512)]
    XC, SQ_ = a(2688, 512), a(7296, 512)
    pfree = [[], []]

    def group_norm(pr, OT, t):
        b = bank()
        t = mm(PB[b][:, :], B64, OT, True, True, t, t8, *bfree[b], inc=True)
        yield
        t = stt(XC, PB[b][:, :], -1.0 / 64, OT, ALU.mult, ALU.add, t)
        bfree[b] = [t]
        t = act(SQ_, XC, ACT.Square, t)
        yield
        b = bank()
        t = mm(PB[b][:, :], B64, SQ_, True, True, t, *bfree[b], inc=True)
        yield
        t = vts(OT, PB[b][:, :], 1.0 / 64, EPS, ALU.mult, ALU.add, t)
        bfree[b] = [t]
        t = act(OT, OT, ACT.Sqrt, t)
        yield
        V.do(lambda e: e.reciprocal(OT, OT), t)
        vtt(XC, XC, OT, ALU.mult)
        vtt(G3[:, pr, :], XC, G3[:, pr, :], ALU.mult)
        yield

    for pr in range(4):
        ob = bank()
        inuse.append(ob)
        for hl in range(2):
            h = 2 * pr + hl
            ps = slice(hl * 64, hl * 64 + 64)
            b = bank()
            for ch in range(4):
                cs = slice(ch * 128, (ch + 1) * 128)
                t = mm(PB[b][:, cs], K3[ps, pr, cs], Q3[ps, pr, cs], ch == 0, ch == 3, *bfree[b], inc=ch == 3)
            t = vtt(SMs[hl].rearrange("p (c t) -> p c t", t=128), PB[b][:, :].rearrange("p (c t) -> p c t", t=128),
                    DT[:, h * 128:(h + 1) * 128].unsqueeze(1).to_broadcast([128, 4, 128]), ALU.mult, t, t4,
                    *pfree[hl])
            bfree[b] = [t]
            step()
            for ch in range(4):
                cs = slice(ch * 128, (ch + 1) * 128)
                mm(PB[ob][ps, cs], V3[:, ch, h * 64:(h + 1) * 64], SMs[hl][:, cs], ch == 0, False, t, *bfree[ob])
            for ch in range(1, 4):
                cs = slice(ch * 128, (ch + 1) * 128)
                t = mm(PB[ob][ps, cs], RS[ps, ch - 1, pr, hl * 64:hl * 64 + 64], QD[ps, pr, cs], False, ch == 3,
                       t_rs, inc=ch == 3)
            pfree[hl] = [t]
            step()
            step()
        t = copy(V, OTs[pr % 2], PB[ob][:, :], t)
        bfree[ob] = [t]
        inuse.remove(ob)
        jobs.append(group_norm(pr, OTs[pr % 2], t))
    while jobs or slow:
        step()
    barrier()
    inuse.extend(range(4))
    for b_ in range(4):
        P.wait(*bfree[b_])
    for j in range(4):
        yv = PB[j][:, :].rearrange("p (n t) -> p n t", t=8)
        uv = U3[:, j, :].rearrange("p (n t) -> p n t", t=8)
        for tau in range(8):
            mm(yv[:, :, tau:8], KK[:, tau * 4 + j, :], uv[:, :, 0:8 - tau], tau == 0, False, inc=tau == 7)
    UN = ar[0:64, 0:4096].rearrange("p (g s c) -> p g s c", s=8, c=16)
    for s_ in range(8):
        b = bank()
        for j in range(4):
            t = tp(PB[b][0:64, j * 128:(j + 1) * 128], U3[:, j, s_::8], *bfree[b], inc=j == 3)
        bfree[b] = [copy(A, UN[:, :, s_, :], PB[b][0:64, :].rearrange("p (g c) -> p g c", c=16), t)]
    t_un = A.now
    UG = a(18432, 2048, 64)
    for g0 in range(0, 32, 8):
        b = bank()
        for g in range(8):
            t = tp(PB[b][:, g * 64:(g + 1) * 64], ar[0:64, (g0 + g) * 128:(g0 + g + 1) * 128], t_un, *bfree[b],
                   inc=g == 7)
        bfree[b] = [copy(A, UG[:, g0:g0 + 8, :], PB[b][:, :].rearrange("p (g n) -> p g n", n=64), t)]
    t_ug = A.now
    VV = a(0, 2048)
    VI = a(2048, 2048)
    for g0 in range(0, 32, 8):
        b = bank()
        for g in range(8):
            t = mm(PB[b][:, g * 64:(g + 1) * 64], MG[:, (g0 + g) * 128:(g0 + g + 1) * 128], UG[:, g0 + g, :],
                   g == 0, g == 7, t_ug, *bfree[b], inc=g == 7)
        t = copy(A, VV[:, g0 * 64:(g0 + 8) * 64], PB[b][:, :], t)
        bfree[b] = [t]
        b = bank()
        t = mm(PB[b][:, :], jmT, VV[:, g0 * 64:(g0 + 8) * 64], True, True, t, *bfree[b], inc=True)
        bfree[b] = [copy(A, VI[:, g0 * 64:(g0 + 8) * 64], PB[b][:, :], t)]
    t_vi = A.now
    W.add(lent, [ARENA + 10240 + n * SLOT for n in range(8)], V.now, A.now, P.now)
    WR_, WI_ = a(6144, 2048, 64), a(8192, 2048, 64)
    TT1, TT2 = a(4096, 1024), a(5120, 1024)
    copy(V, WR_[:, :, 0:1], WC.unsqueeze(2))
    copy(V, WI_[:, :, 0:1], WS.unsqueeze(2))
    m_ = 1
    while m_ < 64:
        br_ = WR_[:, :, m_ - 1:m_].to_broadcast([128, 32, m_])
        bi_ = WI_[:, :, m_ - 1:m_].to_broadcast([128, 32, m_])
        x1 = TT1[:, 0:32 * m_].rearrange("p (g n) -> p g n", n=m_)
        x2 = TT2[:, 0:32 * m_].rearrange("p (g n) -> p g n", n=m_)
        vtt(x1, WR_[:, :, 0:m_], br_, ALU.mult)
        vtt(x2, WI_[:, :, 0:m_], bi_, ALU.mult)
        vtt(WR_[:, :, m_:2 * m_], x1, x2, ALU.subtract)
        vtt(x1, WR_[:, :, 0:m_], bi_, ALU.mult)
        vtt(x2, WI_[:, :, 0:m_], br_, ALU.mult)
        vtt(WI_[:, :, m_:2 * m_], x1, x2, ALU.add)
        m_ *= 2
    GS = a(10240, 4096)
    GS4 = GS.rearrange("p (g s c) -> p g s c", s=8, c=16)
    for s_ in range(8):
        power(GS4[:, :, s_, :], QA, QI, s_ + 1, -1)
    D0 = a(4096, 2048, 64)
    copy(V, D0, R8.unsqueeze(2).to_broadcast([128, 32, 64]), t_par["r8"])
    V.do(lambda e: e.memset(D0[:, :, 0:1], 0.0))
    WRf, WIf = a(6144, 2048), a(8192, 2048)
    vtt(VV, VV, WRf, ALU.mult, t_vi)
    vtt(VI, VI, WIf, ALU.mult)
    vtt(VV, VV, VI, ALU.subtract)
    ZZ = VI
    t_z = V.do(lambda e: e.tensor_tensor_scan(ZZ, a(4096, 2048), VV, 0.0, ALU.mult, ALU.add))
    ZI = a(18432, 2048)
    for g0 in range(0, 4):
        b = bank()
        t = mm(PB[b][:, :], jmT, ZZ[:, g0 * 512:(g0 + 1) * 512], True, True, t_z, *bfree[b], inc=True)
        bfree[b] = [copy(A, ZI[:, g0 * 512:(g0 + 1) * 512], PB[b][:, :], t)]
    XS = a(4096, 2048, 64)
    V.do(lambda e: e.memset(XS[:, :, 0:1], 0.0), A.now)
    Z3, I3 = ZZ.rearrange("p (g n) -> p g n", n=64), ZI.rearrange("p (g n) -> p g n", n=64)
    vtt(ZZ, ZZ, WRf, ALU.mult)
    vtt(ZI, ZI, WIf, ALU.mult)
    t_xs = vtt(XS[:, :, 1:64], Z3[:, :, 0:63], I3[:, :, 0:63], ALU.add)
    YN = ar[0:64, 0:4096].rearrange("p (t c) -> p t c", c=512)
    for g0 in range(0, 32, 4):
        b = bank()
        for g in range(4):
            t = mm(PB[b][0:64, g * 128:(g + 1) * 128], XS[:, g0 + g, :], GS[:, (g0 + g) * 128:(g0 + g + 1) * 128],
                   g == 0, g == 3, t_xs, *bfree[b], inc=g == 3)
        src = PB[b][0:64, :].rearrange("p (g t c) -> p t g c", t=8, c=16)
        dst = YN[:, :, g0 * 16:(g0 + 4) * 16].rearrange("p t (g c) -> p t g c", c=16)
        bfree[b] = [copy(A if g0 % 8 else V, dst, src, t)]
    t_yn = [V.now, A.now]
    SS3 = a(8192, 2048, 512)
    for j in range(4):
        yv = PB[j][:, :].rearrange("p (n t) -> p t n", t=8)
        for s_ in range(8):
            t = mm(yv[:, s_, :], YN[:, s_, j * 128:(j + 1) * 128], ident[0:64, 0:64], False, s_ == 7, *t_yn,
                   inc=s_ == 7)
        t = act(SS3[:, j, :], PB[j][:, :], ACT.Gelu_apprx_tanh, t)
        bfree[j] = [t]
    del inuse[:]
    barrier()
    ss = split_tiles(lambda k: SS3[:, k, :], 10240, 4)

    def glu_ev(c, m, b, t):
        z = a(2048 + m * 512, 512)
        t = act(z, PB[b][:, :], ACT.Sigmoid, t)
        bfree[b] = [t]
        vtt(MX[:, 4 + m, :], SS3[:, m, :], z, ALU.mult, t)

    dense([512], ss, 4, glu_ev)
    barrier()
    mx = split_tiles(lambda k: MX[:, k, :], 0)
    dense([512, 512], mx, 8, resid(None))

    def ffn(l):
        barrier()
        norm(lambda k: C(f"ffn{l}", k))
        AH, AL = r(8192, 5632, 512), r(13824, 5632, 512)
        sg = [a(19456 + i * 512, 512) for i in range(4)]
        sgf = [[], [], [], []]
        pd = []
        for f in range(2):
            at_ = [None] * 11
            kk = 0
            for n in HCH:
                ts_ = {}

                def ev_g(c, m, b, t):
                    ts_[m] = act(sg[m], PB[b][:, :], ACT.Silu, t, *sgf[m])
                    bfree[b] = [ts_[m]]

                def ev_u(c, m, b, t):
                    t = vtt(sg[m], sg[m], PB[b][:, :], ALU.mult, t, ts_[m])
                    bfree[b] = [t]
                    at_[kk + m] = split(AH[:, kk + m, :], AL[:, kk + m, :], sg[m], t, *pd)
                    sgf[m] = [at_[kk + m]]

                dense([n], hn, 8, ev_g)
                dense([n], hn, 8, ev_u)
                kk += n // 128
            dense([512, 512], lambda k: (AH[:, k, :], AL[:, k, :], at_[k]), 11, resid(None))
            pd = [P.now]

    def ple(l):
        barrier()
        norm(lambda k: C(f"ple{l}", k))
        pt = a(8192, 1024, 256)
        t0 = load(A, f"p{l}", pt, I["p_2"][l, 0].rearrange("(t p) d -> p t d", p=128))
        PH, PL = r(9216, 1024, 512), r(10240, 1024, 512)
        tpt = []
        for k in range(2):
            b = bank()
            for t_ in range(4):
                t = tp(PB[b][:, t_ * 128:(t_ + 1) * 128], pt[:, t_, k * 128:(k + 1) * 128], t0, *bfree[b], inc=t_ == 3)
            t = split(PH[:, k, :], PL[:, k, :], PB[b][:, :], t)
            bfree[b] = [t]
            tpt.append(t)
        SG = a(11264, 4096, 512)
        dense([512, 512], hn, 8, lambda c, m, b, t: bfree.__setitem__(
            b, [act(SG[:, c * 4 + m, :], PB[b][:, :], ACT.Sigmoid, t)]))
        tp1 = [a(15360, 512), a(15872, 512)]
        tsg = A.now

        def ev_p(c, m, b, t):
            m = c * 4 + m
            t = vtt(tp1[m % 2], PB[b][:, :], SG[:, m, :], ALU.mult, t, tsg)
            bfree[b] = [t]
            vtt(hk(m), hk(m), tp1[m % 2], ALU.add)

        dense([512, 512], lambda k: (PH[:, k, :], PL[:, k, :], tpt[k]), 2, ev_p)

    ffn(0)
    ple(0)

    barrier()
    norm(lambda k: C("mix1", k))
    Q8 = a(8192, 4096, 512)
    K8 = a(12288, 4096, 512)
    V8 = a(16384, 4096, 1024)
    nlam, slc = a(21256, 1), a(21258, 1)

    def lam_job():
        lv_ = ar[0:1, 20992:21248].rearrange("p (i d) -> p i d", d=64)
        for i, nm in enumerate(("diff_lambda_q1_2", "diff_lambda_k1_2", "diff_lambda_q2_2", "diff_lambda_k2_2")):
            t = load(A, "lam", lv_[:, i, :], I[nm], V.now)
        yield
        ls = ar[0:1, 21250:21252]
        for i in range(2):
            vtt(lv_[:, 2 * i, :], lv_[:, 2 * i, :], lv_[:, 2 * i + 1, :], ALU.mult, t)
            V.do(lambda e, i=i: e.tensor_reduce(ls[:, i:i + 1], lv_[:, 2 * i, :], AX.X, ALU.add))
        t = act(ls, ls, ACT.Exp, V.now)
        yield
        b = bank()
        t = mm(PB[b][:, 0:2], ones[0:1, :], ls, True, True, t, *bfree[b], inc=True)
        le = a(21252, 2)
        t = copy(V, le, PB[b][:, 0:2], t)
        bfree[b] = [t]
        vtt(nlam, le[:, 1:2], le[:, 0:1], ALU.subtract)
        vts(nlam, nlam, -LAMBDA_INIT, None, ALU.add, None)
        vts(slc, C("subln"), 1.0 - LAMBDA_INIT, None, ALU.mult, None)
        yield

    jobs.append(lam_job())
    dense([512, 512], hn, 8, rotated(lambda c, m: Q8[:, c * 4 + m, :]))
    dense([512, 512], hn, 8, rotated(lambda c, m: K8[:, c * 4 + m, :]))
    dense([512, 512], hn_tm, 8,
          ev(lambda c, m: V8[:, m, c * 512:(c + 1) * 512]), mode="tm")
    finish_jobs()
    barrier()
    OO = a(0, 4096, 512)
    EE = [[a(4096 + (2 * p + s_) * 512, 512) for s_ in range(2)] for p in range(2)]
    WT = [a(6144 + p * 512, 512) for p in range(2)]
    DG = [[a(7168 + (2 * p + s_) * 128, 128) for s_ in range(2)] for p in range(2)]
    caus, t_ca = tab("caus", 7680)
    mxc = [a(7808 + 2 * p, 2) for p in range(2)]
    dnc = [a(7812 + 2 * p, 2) for p in range(2)]
    sqh, rrh = a(21504, 512), a(22016, 512)
    OH_, OL_ = r(8192, 4096, 512), r(12288, 4096, 512)
    t_oo = [None] * 8
    t_sc, t_exp, t_tr, t_wt, t_pv, t_dg = {}, {}, {}, {}, {}, {}
    units_ = [(h, i) for h in range(8) for i in range(4)]

    def scores(u):
        h, i = units_[u]
        p, nk = u % 2, (i + 1) * 128
        qs = slice(i * 128, nk)
        for s_ in range(2):
            ps = slice(s_ * 64, s_ * 64 + 64)
            b = 2 * p + s_
            t = mm(PB[b][:, 0:nk], Q8[ps, h, qs], K8[ps, h, 0:nk], True, False, *bfree[b], inc=True)
            t_sc[u, s_] = t

    def exps(u):
        h, i = units_[u]
        p, nk = u % 2, (i + 1) * 128
        qs = slice(i * 128, nk)
        for s_ in range(2):
            b = 2 * p + s_
            t = mm(PB[b][:, qs], ident, caus, False, True, t_sc[u, s_], t_ca, inc=True)
            V.do(lambda e, s_=s_, b=b: e.tensor_reduce(mxc[p][:, s_:s_ + 1], PB[b][:, 0:nk], AX.X, ALU.max), t,
                 *([t_exp[u - 2]] if u >= 2 else []))
        tm = vts(mxc[p], mxc[p], -0.125, None, ALU.mult, None)
        for s_ in range(2):
            b = 2 * p + s_
            t_exp[u] = act(EE[p][s_][:, 0:nk], PB[b][:, 0:nk], ACT.Exp, tm, *([t_tr[u - 2]] if u >= 2 else []),
                           bias=mxc[p][:, s_:s_ + 1], scale=0.125, accum=dnc[p][:, s_:s_ + 1])
            bfree[b] = [t_exp[u]]

    def weights(u):
        h, i = units_[u]
        p, nk = u % 2, (i + 1) * 128
        V.do(lambda e: e.reciprocal(dnc[p], dnc[p]), t_exp[u])
        vtt(dnc[p][:, 1:2], dnc[p][:, 1:2], nlam, ALU.mult)
        w_ = [t_tr[u - 2]] if u >= 2 else []
        for s_ in range(2):
            t_dg[u] = vts(DG[p][s_], ident, dnc[p][:, s_:s_ + 1], None, ALU.mult, None, *w_)

    def turned(u):
        h, i = units_[u]
        p, nk = u % 2, (i + 1) * 128
        t = t_dg[u]
        b = 4 + p
        for j in range(i + 1):
            js = slice(j * 128, (j + 1) * 128)
            mm(PB[b][:, js], EE[p][0][:, js], DG[p][0], j == 0, False, t, *bfree[b])
            t_tr[u] = mm(PB[b][:, js], EE[p][1][:, js], DG[p][1], False, j == i, inc=j == i)
        t_wt[u] = copy(A, WT[p][:, 0:nk], PB[b][:, 0:nk], t_tr[u], *([t_pv[u - 2]] if u >= 2 else []))
        bfree[b] = [t_wt[u]]

    def values(u):
        h, i = units_[u]
        p, ob = u % 2, 6 + h % 2
        for j in range(i + 1):
            js = slice(j * 128, (j + 1) * 128)
            t = mm(PB[ob][:, i * 128:(i + 1) * 128], V8[:, j, h * 128:(h + 1) * 128], WT[p][:, js],
                   i == 0 and j == 0, j == i, t_wt[u], *bfree[ob], inc=j == i)
        t_pv[u] = t
        if i == 3:
            jobs.append(head(h, ob, t))

    def head(h, ob, t):
        act(OO[:, h, :], PB[ob][:, :], ACT.Copy, t)
        t = act(sqh, PB[ob][:, :], ACT.Square)
        bfree[ob] = [t]
        t = mm(PB[ob][:, :], ones, sqh, True, True, t, inc=True)
        yield
        t = vts(rrh, PB[ob][:, :], 1.0 / 128, EPS, ALU.mult, ALU.add, t)
        bfree[ob] = [t]
        t = act(rrh, rrh, ACT.Sqrt, t)
        yield
        V.do(lambda e: e.reciprocal(rrh, rrh), t)
        yield
        t = stt(OO[:, h, :], OO[:, h, :], slc, rrh, ALU.mult, ALU.mult)
        t_oo[h] = split(OH_[:, h, :], OL_[:, h, :], OO[:, h, :], t)
        yield

    for n in range(34):
        if n < 32:
            scores(n)
        if 1 <= n < 33:
            weights(n - 1)
        if n < 32:
            exps(n)
        if 1 <= n < 33:
            turned(n - 1)
        if n >= 2:
            values(n - 2)
        step()
    finish_jobs()
    turn[0] = 0
    dense([512, 512], lambda k: (OH_[:, k, :], OL_[:, k, :], t_oo[k]), 8, resid(None))
    ffn(1)
    ple(1)
    barrier()
    norm(lambda k: C("fin2", k), True)
    barrier()
    store_out(hk)
    emit_all()


_INS = ["x", "c", "ctx", "c_ctx", "w_ada", "b_ada", "norm_mix_w", "norm_mlp_w", "w_in", "w_gk_f", "b_gk_f", "w_gk_b",
        "b_gk_b", "gla_norm_w", "w_pool", "pool_scale", "w_out", "w_router", "b_router", "w_gu", "b_gu", "w_down",
        "b_down", "final_norm_w", "p_2", "norm_mix_2", "norm_ffn_2", "norm_ple_2", "ret_s5_w_in_2", "ret_s5_w_out_2",
        "s5_lambda_re_2", "s5_lambda_im_2", "s5_b_re_2", "s5_b_im_2", "s5_c_re_2", "s5_c_im_2", "s5_d_2",
        "s5_log_step_2", "s5_w_glu_2", "diff_w_qkv_2", "diff_w_o_2", "diff_lambda_q1_2", "diff_lambda_k1_2",
        "diff_lambda_q2_2", "diff_lambda_k2_2", "diff_subln_2", "ffn_w_gate_2", "ffn_w_up_2", "ffn_w_down_2",
        "ple_w_proj_2", "ple_w_gate_2", "final_norm_2"]


def kernel(**inputs):
    import concourse.bacc as bacc
    from concourse.bass_utils import run_bass_kernel_spmd

    nc = bacc.Bacc("TRN2", target_bir_lowering=False, num_devices=1)
    arrays, ins = {}, {}
    consts = const_tables()
    held = {name: np.ascontiguousarray(inputs[name]) for name in _INS}
    held["tabs"] = np.concatenate([consts[n] for n in TABLE_ORDER], axis=1)
    held["ptab"] = pool_tables()
    for name, v in held.items():
        arrays[f"in_{name}"] = v
        ins[name] = nc.dram_tensor(f"in_{name}", v.shape, F32, kind="ExternalInput").ap()
    out = nc.dram_tensor("out_0", (1, 512, 1024), F32, kind="ExternalOutput").ap()
    build(nc, ins, out)
    r = run_bass_kernel_spmd(nc, [arrays], core_ids=[0])
    return r.results[0]["out_0"]
```
